# Optimizing a Trainium2 kernel written in Bass

```python
import math
import jax, jax.numpy as jnp
from jax import lax
import numpy as np

D_MODEL = 2048
BATCH = 1
SEQ = 256
DEPTH = 1

HEAD_DIM = 128
N_HEADS_A = 4
N_HEADS_B = 4
N_HEADS_D = 4
DIFF_DIM = HEAD_DIM // 2
CONV_CH = 512
CONV_K = 3
IDX_HEADS = 4
IDX_DIM = 64
TOPK_MAX = 256
MIX_W = 512
N_BRANCH = 4
D_FF = 4 * D_MODEL
N_BUCKETS = 32
MAX_DIST = 128
Q_BLOCK = 128
EPS = 1e-6
NEG = -1e30
IDX_SCALE = (IDX_DIM ** -0.5) * (IDX_HEADS ** -0.5)

IN_SIZES = (
    N_HEADS_A * HEAD_DIM, N_HEADS_A * HEAD_DIM, N_HEADS_A * HEAD_DIM,
    IDX_HEADS * IDX_DIM, IDX_DIM, IDX_HEADS,
    N_HEADS_B * HEAD_DIM, N_HEADS_B * HEAD_DIM, N_HEADS_B * HEAD_DIM,
    CONV_CH, CONV_CH, CONV_CH,
    N_HEADS_D * HEAD_DIM, N_HEADS_D * HEAD_DIM, N_HEADS_D * HEAD_DIM,
    N_HEADS_D,
)
D_IN = sum(IN_SIZES)

kernel_name = "hybrid_gated_dsa_diff_conv_fox"

def _split_points():
    pts, acc = [], 0
    for s in IN_SIZES[:-1]:
        acc += s
        pts.append(acc)
    return pts

def rmsnorm(x, g):
    xf = x.astype(jnp.float32)
    y = xf * lax.rsqrt(jnp.mean(xf * xf, axis=-1, keepdims=True) + EPS)
    return (y * g.astype(jnp.float32)).astype(x.dtype)

def t5_bucket(rel):
    n = jnp.maximum(rel, 0)
    max_exact = N_BUCKETS // 2
    nf = jnp.maximum(n, 1).astype(jnp.float32)
    large = max_exact + (jnp.log(nf / max_exact) / math.log(MAX_DIST / max_exact)
                         * (N_BUCKETS - max_exact)).astype(jnp.int32)
    large = jnp.minimum(large, N_BUCKETS - 1)
    return jnp.where(n < max_exact, n, large)

def merge_blocks(o):
    nb, b, q, h, d = o.shape
    return jnp.moveaxis(o, 0, 1).reshape(b, nb * q, h, d)

def dsa_attention(q, k, v, iq, ik, iw, bias_tab, k_top):
    S = q.shape[1]
    hd = q.shape[-1]
    scale = hd ** -0.5
    kpos = jnp.arange(S)

    def block(i):
        t0 = i * Q_BLOCK
        qb = lax.dynamic_slice_in_dim(q, t0, Q_BLOCK, 1)
        iqb = lax.dynamic_slice_in_dim(iq, t0, Q_BLOCK, 1)
        iwb = lax.dynamic_slice_in_dim(iw, t0, Q_BLOCK, 1)
        qpos = t0 + jnp.arange(Q_BLOCK)
        causal = kpos[None, :] <= qpos[:, None]
        dots = jnp.einsum('bqhd,bsd->bqhs', iqb, ik).astype(jnp.float32)
        score = jnp.einsum('bqh,bqhs->bqs', iwb.astype(jnp.float32) * IDX_SCALE, jax.nn.relu(dots))
        score = jnp.where(causal[None], score, NEG)
        _, idx = lax.top_k(score, k_top)
        k_sel = jax.vmap(lambda kk, ii: kk[ii])(k, idx)
        v_sel = jax.vmap(lambda vv, ii: vv[ii])(v, idx)
        logits = jnp.einsum('bqhd,bqkhd->bhqk', qb, k_sel).astype(jnp.float32) * scale
        rel = qpos[None, :, None] - idx
        bias = bias_tab[t5_bucket(rel)].astype(jnp.float32)
        logits = logits + jnp.transpose(bias, (0, 3, 1, 2))
        logits = jnp.where((rel >= 0)[:, None], logits, NEG)
        p = jax.nn.softmax(logits, axis=-1).astype(v.dtype)
        return jnp.einsum('bhqk,bqkhd->bqhd', p, v_sel)

    return merge_blocks(lax.map(block, jnp.arange(S // Q_BLOCK)))

def diff_attention(q, k, v, lam_val, lam_init, g_subln, bias_tab):
    S = q.shape[1]
    scale = DIFF_DIM ** -0.5
    kpos = jnp.arange(S)

    def block(i):
        t0 = i * Q_BLOCK
        qb = lax.dynamic_slice_in_dim(q, t0, Q_BLOCK, 1)
        qpos = t0 + jnp.arange(Q_BLOCK)
        rel = qpos[:, None] - kpos[None, :]
        bias = jnp.transpose(bias_tab[t5_bucket(rel)], (2, 0, 1)).astype(jnp.float32)
        logits = jnp.einsum('bqhcd,bshcd->bchqs', qb, k).astype(jnp.float32) * scale + bias
        logits = jnp.where((rel >= 0)[None, None, None], logits, NEG)
        p = jax.nn.softmax(logits, axis=-1)
        attn = (p[:, 0] - lam_val * p[:, 1]).astype(v.dtype)
        return jnp.einsum('bhqs,bshd->bqhd', attn, v)

    o = merge_blocks(lax.map(block, jnp.arange(S // Q_BLOCK)))
    return rmsnorm(o, g_subln) * (1.0 - lam_init)

def short_conv(bg, cg, xin, conv_w):
    u = cg * xin
    y = lax.conv_general_dilated(
        u, conv_w[:, None, :], window_strides=(1,), padding=[(CONV_K - 1, 0)],
        dimension_numbers=('NWC', 'WIO', 'NWC'), feature_group_count=CONV_CH)
    return bg * y

def forgetting_attention(q, k, v, f_logit):
    S = q.shape[1]
    scale = q.shape[-1] ** -0.5
    kpos = jnp.arange(S)
    F = jnp.cumsum(jax.nn.log_sigmoid(f_logit.astype(jnp.float32)), axis=1)
    Fk = jnp.transpose(F, (0, 2, 1))

    def block(i):
        t0 = i * Q_BLOCK
        qb = lax.dynamic_slice_in_dim(q, t0, Q_BLOCK, 1)
        Fq = lax.dynamic_slice_in_dim(Fk, t0, Q_BLOCK, 2)
        qpos = t0 + jnp.arange(Q_BLOCK)
        causal = kpos[None, :] <= qpos[:, None]
        logits = (jnp.einsum('bqhd,bshd->bhqs', qb, k).astype(jnp.float32) * scale
                  + Fq[..., None] - Fk[:, :, None, :])
        logits = jnp.where(causal[None, None], logits, NEG)
        p = jax.nn.softmax(logits, axis=-1).astype(v.dtype)
        return jnp.einsum('bhqs,bshd->bqhd', p, v)

    return merge_blocks(lax.map(block, jnp.arange(S // Q_BLOCK)))

def setup_inputs(seed: int = 0) -> dict:
    key = jax.random.key(seed)
    ks = jax.random.split(key, 24)
    n = lambda k, shape, s: jax.random.normal(k, shape, jnp.float32) * s
    D = D_MODEL
    return {
        "x": n(ks[0], (BATCH, SEQ, D), 1.0),
        "c": n(ks[1], (BATCH, D), 1.0),
        "w_ada": n(ks[2], (DEPTH, D, 6 * D), 0.5 * D ** -0.5),
        "b_ada": n(ks[3], (DEPTH, 6 * D), 0.02),
        "g_norm1": 1.0 + n(ks[4], (DEPTH, D), 0.05),
        "w_in": n(ks[5], (DEPTH, D, D_IN), D ** -0.5),
        "b_f": 2.0 + n(ks[6], (DEPTH, N_HEADS_D), 0.1),
        "conv_w": n(ks[7], (DEPTH, CONV_K, CONV_CH), CONV_K ** -0.5),
        "lam": n(ks[8], (DEPTH, 4, DIFF_DIM), 0.1),
        "g_subln": 1.0 + n(ks[9], (DEPTH, HEAD_DIM), 0.05),
        "rel_bias": n(ks[10], (N_BUCKETS, N_HEADS_A + N_HEADS_B), 0.5),
        "w_gate": n(ks[11], (DEPTH, D, N_BRANCH * D), D ** -0.5),
        "b_gate": n(ks[12], (DEPTH, N_BRANCH * D), 0.02),
        "w_branch": n(ks[13], (DEPTH, N_BRANCH, MIX_W, D), MIX_W ** -0.5),
        "w_o": n(ks[14], (DEPTH, D, D), D ** -0.5),
        "g_norm2": 1.0 + n(ks[15], (DEPTH, D), 0.05),
        "w_ff1": n(ks[16], (DEPTH, D, D_FF), D ** -0.5),
        "w_ff2": n(ks[17], (DEPTH, D_FF, D), D_FF ** -0.5),
        "g_final": 1.0 + n(ks[18], (D,), 0.05),
    }

def reference(x, c, w_ada, b_ada, g_norm1, w_in, b_f, conv_w, lam, g_subln, rel_bias,
              w_gate, b_gate, w_branch, w_o, g_norm2, w_ff1, w_ff2, g_final):
    Bn, S, D = x.shape
    k_top = min(TOPK_MAX, S // 4)
    c_act = jax.nn.silu(c)
    bias_a = rel_bias[:, :N_HEADS_A]
    bias_b = rel_bias[:, N_HEADS_A:]
    heads = lambda t, nh: t.reshape(Bn, S, nh, -1)
    for l in range(DEPTH):
        mod = (c_act @ w_ada[l] + b_ada[l])[:, None, :]
        sh1, sc1, gt1, sh2, sc2, gt2 = jnp.split(mod, 6, axis=-1)
        h = rmsnorm(x, g_norm1[l]) * (1.0 + sc1) + sh1
        (qa, ka, va, iq, ik, iw, qb, kb, vb, bg, cg, xin, qd, kd, vd, fd) = jnp.split(
            h @ w_in[l], _split_points(), axis=-1)
        y_a = dsa_attention(heads(qa, N_HEADS_A), heads(ka, N_HEADS_A), heads(va, N_HEADS_A),
                            heads(iq, IDX_HEADS), ik, iw, bias_a, k_top)
        lam_init = 0.8 - 0.6 * math.exp(-0.3 * l)
        lq = lam[l].astype(jnp.float32)
        lam_val = jnp.exp(jnp.sum(lq[0] * lq[1])) - jnp.exp(jnp.sum(lq[2] * lq[3])) + lam_init
        y_b = diff_attention(qb.reshape(Bn, S, N_HEADS_B, 2, DIFF_DIM),
                             kb.reshape(Bn, S, N_HEADS_B, 2, DIFF_DIM),
                             heads(vb, N_HEADS_B), lam_val, lam_init, g_subln[l], bias_b)
        y_c = short_conv(bg, cg, xin, conv_w[l])
        y_d = forgetting_attention(heads(qd, N_HEADS_D), heads(kd, N_HEADS_D), heads(vd, N_HEADS_D),
                                   fd + b_f[l])
        branches = jnp.stack([y_a.reshape(Bn, S, MIX_W), y_b.reshape(Bn, S, MIX_W),
                              y_c, y_d.reshape(Bn, S, MIX_W)], axis=2)
        gates = jax.nn.sigmoid(h @ w_gate[l] + b_gate[l]).reshape(Bn, S, N_BRANCH, D)
        merged = jnp.einsum('bsgd,bsgd->bsd', gates,
                            jnp.einsum('bsgk,gkd->bsgd', branches, w_branch[l]))
        x = x + gt1 * (merged @ w_o[l])
        h2 = rmsnorm(x, g_norm2[l]) * (1.0 + sc2) + sh2
        x = x + gt2 * (jnp.square(jax.nn.relu(h2 @ w_ff1[l])) @ w_ff2[l])
    return rmsnorm(x, g_final)


_drawn_inputs = setup_inputs


def setup_inputs(seed=0):
    import zlib

    import numpy as np

    out = dict(_drawn_inputs(seed))
    spreads = {}
    factors = {'b_f': 64.0, 'lam': 4.81, 'g_subln': 7.835, 'b_gate': 8.0, 'g_norm2': 3.254}
    for name, (base, spread) in spreads.items():
        noise = np.random.default_rng([zlib.crc32(name.encode()), seed]).standard_normal(out[name].shape)
        drawn = base * np.exp(spread * noise) if base else spread * noise
        out[name] = __import__('jax').numpy.asarray(drawn.astype(out[name].dtype))
    for name, factor in factors.items():
        out[name] = (out[name] * factor).astype(out[name].dtype)
    return out
```

```python
import math
from contextlib import ExitStack

import concourse.bass as bass
from concourse import mybir

F32 = mybir.dt.float32
F32R = mybir.dt.float32r
ALU = mybir.AluOpType
ACT = mybir.ActivationFunctionType
AX_X = mybir.AxisListType.X

P = 128
D = 2048
SEQ = 256
NT = SEQ // P
KT = D // P
NB = 512
DB = D // NB
HD = 128
NH = 4
DD = HD // 2
IDX_DIM = 64
K_TOP = 64
N_BUCKETS = 32
MAX_DIST = 128
EPS = 1e-6
NEG = -1e30
TAKEN = -3e38
IDX_SCALE = (IDX_DIM ** -0.5) * (NH ** -0.5)
LAM_INIT = 0.8 - 0.6 * math.exp(0.0)
LOG_COLS = P + SEQ

RING = 4
CK = 2
UC = KT // CK
BC = NH // CK
ADA_UNITS = 6 * DB
WIN_UNITS = 13
GATE_UNITS = 2 * 4 * DB
MIXERS = (2, 0, 1, 3)
G_WIN = ADA_UNITS * UC
G_GATE = G_WIN + WIN_UNITS * UC
G_WO = G_GATE + 4 * DB * (UC + BC)
G_FF = G_WO + DB * UC
CHUNKS = G_FF + 32 * UC
V_WIN = ADA_UNITS
V_GATE = V_WIN + WIN_UNITS
V_WO = V_GATE + GATE_UNITS
V_FF = V_WO + DB
FF_GROUPS = 4

MISC, QA, KA, VA, QB, KB, VB, BG, CG, XIN = range(10)
QD, KD, VD = QA, KA, VA
IK0 = 4 * IDX_DIM
IW0 = IK0 + IDX_DIM
FD0 = IW0 + NH


class Links:

    def __init__(self, eng, sem):
        self.eng, self.sem, self.base, self.n = eng, sem, 0, 0

    def enter(self, i, per):
        self.base0, self.per = self.base + self.n, per
        self.base, self.n = self.base0 + i * per, 0

    def leave(self, times):
        assert self.n == self.per, (self.n, self.per)
        self.base, self.n = self.base0 + times * self.per, 0

    def step(self, ins):
        ins.then_inc(self.sem, 1)
        self.n += 1

    def wait(self):
        self.eng.wait_ge(self.sem, self.base + self.n)

    def __call__(self, ins):
        self.step(ins)
        self.wait()


def t5_runs():
    exact = N_BUCKETS // 2
    of = [n if n < exact else min(N_BUCKETS - 1, exact + int(math.log(n / exact) / math.log(MAX_DIST / exact)
                                                            * (N_BUCKETS - exact))) for n in range(SEQ)]
    return [(b, of.index(b), SEQ - of[::-1].index(b)) for b in sorted(set(of))]


def build(nc, stream, bias_rows, x_in, c_cols, conv_cols, lam, g_subln, tab, b_f, g_norm1, g_norm2, g_final, out):
    base = (nc.sbuf_base + 31) // 32 * 32
    K = 1024

    def at(name, off, shape, dt=F32):
        return nc.alloc_sbuf_tensor_at(name, shape, dt, offset=base + int(off))

    raw = at("raw", 0, [P, RING, CK * NB])
    w_hi = at("w_hi", 16 * K, [P, RING, CK * NB], F32R)
    w_lo = at("w_lo", 32 * K, [P, RING, CK * NB], F32R)
    act_hi = at("act_hi", 48 * K, [P, KT, SEQ], F32R)
    act_lo = at("act_lo", 64 * K, [P, KT, SEQ], F32R)
    sq_junk = at("sq_junk", 48 * K, [P, D])
    Z = 80 * K
    ident = at("ident", Z, [P, P])
    triones = at("triones", Z + 512, [P, SEQ])
    so = [Z + 1536]

    def small(name, shape):
        n = 1
        for s in shape[1:]:
            n *= s
        t = at(name, (so[0] + 31) // 32 * 32, shape)
        so[0] = (so[0] + 31) // 32 * 32 + 4 * n
        return t

    gsub = small("gsub", [P, HD])
    convw = small("convw", [P, NH, 3])
    bf = small("bf", [P, NH])
    nlam = small("nlam", [P, 1])
    ss = small("ss", [P, 2])
    rstd = small("rstd", [P, 2])
    iws = small("iws", [P, NT, NH])
    lsig = small("lsig", [P, NT, NH])
    lsig2 = small("lsig2", [P, NT, NH])
    Ftok = small("Ftok", [P, NT, NH])
    nmax = small("nmax", [P, 2, NT, NH])
    esum = small("esum", [P, 2, NT, NH])
    rec = small("rec", [P, 2, NT, NH])
    m8 = small("m8", [P, NT, 8])
    assert so[0] <= Z + 3 * K
    brow = at("brow", Z + 3 * K, [P, 2, NB])
    zt = at("zt", Z + 7 * K, [P, 2, NT, NB])
    x1 = at("x1", Z + 15 * K, [P, NT, D])
    sh1 = at("sh1", Z + 31 * K, [P, D])
    gs1 = at("gs1", Z + 39 * K, [P, D])
    cb_hi = at("cb_hi", Z + 47 * K, [P, KT, P], F32R)
    cb_lo = at("cb_lo", Z + 55 * K, [P, KT, P], F32R)
    rows_a = at("rows_a", Z + 63 * K, [1, 8 * NB])
    steps = at("steps", Z + 79 * K, [P, 2 * NH, SEQ])
    lamb = at("lamb", Z + 87 * K, [P, 4, DD])
    lprod = at("lprod", Z + 88 * K, [P, 2, DD])
    lsum = at("lsum", Z + 88.5 * K, [P, 4])
    tabT = at("tabT", Z + 88.75 * K, [8, N_BUCKETS])
    dist = at("dist", Z + 89 * K, [8, LOG_COLS])
    cc = at("cc", Z + 90.5 * K, [P, 3, KT])
    mirror = at("mirror", Z + 115 * K, [P, P])
    rows_b = at("rows_b", Z + 99 * K, [1, 8 * NB])
    proj = at("proj", Z + 15 * K, [P, 10, NT, NB])
    merged = at("merged", Z + 43 * K, [P, NT, D])
    y_hi = at("y_hi", Z + 59 * K, [P, 4, NH, SEQ], F32R)
    y_lo = at("y_lo", Z + 75 * K, [P, 4, NH, SEQ], F32R)
    Bm = at("Bm", Z + 91 * K, [P, 2 * NH, SEQ])
    qkT = at("qkT", Z + 99 * K, [P, 2, NH, SEQ])
    pr = at("pr", Z + 107 * K, [P, NH, LOG_COLS])
    pr2 = at("pr2", Z + 113 * K, [P, NH, LOG_COLS])
    iqT = at("iqT", Z + 113 * K, [IDX_DIM, NH + 1, SEQ])
    ob = at("ob", Z + 113 * K, [P, NT, NH, HD])
    pT = at("pT", Z + 119 * K, [P, NH, LOG_COLS])
    score = at("score", Z + 125 * K, [P, LOG_COLS])
    work = at("work", Z + 119 * K, [P, LOG_COLS])
    selm = at("selm", Z + 121 * K, [P, LOG_COLS])
    x3 = at("x3", Z + 15 * K, [P, NT, D])
    gt1b = at("gt1b", Z + 31 * K, [P, D])
    a_hi = at("a_hi", Z + 59 * K, [P, KT, SEQ], F32R)
    a_lo = at("a_lo", Z + 75 * K, [P, KT, SEQ], F32R)
    gs2 = at("gs2", Z + 91 * K, [P, D])
    sh2b = at("sh2b", Z + 99 * K, [P, D])
    gt2b = at("gt2b", Z + 107 * K, [P, D])
    gnb = at("gnb", Z + 115 * K, [P, D])
    h2 = at("h2", Z + 43 * K, [P, NT, D])

    dist_d = nc.dram_tensor("dist_d", (8, LOG_COLS), F32, kind="Internal")
    mods_d = nc.dram_tensor("mods_d", (1, 16 * NB), F32, kind="Internal")
    x_v = x_in.rearrange("(t p) d -> p t d", p=P)
    out_v = out.rearrange("(t p) d -> p t d", p=P)

    def bcast_rows(ap, n=P):
        return ap.partition_broadcast(n)

    with ExitStack() as ctx:
        def sem(name):
            return ctx.enter_context(nc.semaphore(name))

        ps = ctx.enter_context(nc.psum_tensor("ps", [P, 2, NT, NB], F32))
        aux = ctx.enter_context(nc.psum_tensor("aux", [P, 4, NB], F32))

        loaded = [sem(f"loaded{i}") for i in range(RING)]
        hi_ready = sem("hi_ready")
        lo_ready = sem("lo_ready")
        used = sem("used")
        evacuated = sem("evacuated")
        aux_full = sem("aux_full")
        aux_free = sem("aux_free")
        aux_hi = sem("aux_hi")
        brow_in = [sem("brow_in0"), sem("brow_in1")]
        brow_used = sem("brow_used")
        consts = sem("consts")
        small_in = sem("small_in")
        x_loaded = sem("x_loaded")
        c_ready = sem("c_ready")
        cb_ready = sem("cb_ready")
        sumsq = sem("sumsq")
        root = sem("root")
        var_ready = sem("var_ready")
        h_ready = sem("h_ready")
        rows_out = sem("rows_out")
        dist_ready = sem("dist_ready")
        dist_out = sem("dist_out")
        steps_in = sem("steps_in")
        bias_full = sem("bias_full")
        bias_turned = sem("bias_turned")
        bm_ready = sem("bm_ready")
        lam_sum = sem("lam_sum")
        lam_exp = sem("lam_exp")
        score_ready = sem("score_ready")
        score_masked = sem("score_masked")
        neg_max = sem("neg_max")
        exps = sem("exps")
        p_ready = sem("p_ready")
        u_ready = sem("u_ready")
        yc_raw = sem("yc_raw")
        yc_hi = sem("yc_hi")
        yc_ready = sem("yc_ready")
        yb_var = sem("yb_var")
        yb_root = sem("yb_root")
        yb_ready = sem("yb_ready")
        f_abs = sem("f_abs")
        f_log = sem("f_log")
        ls_ready = sem("ls_ready")
        dm_ready = sem("dm_ready")
        gate_ready = sem("gate_ready")
        merged_ready = sem("merged_ready")
        late_in = sem("late_in")
        gfin_in = sem("gfin_in")
        gs2_ready = sem("gs2_ready")
        x_added = sem("x_added")
        a_ready = sem("a_ready")
        dve_step = sem("dve_step")
        act_step = sem("act_step")
        pool_step = sem("pool_step")
        y_out = sem("y_out")
        fin_ready = sem("fin_ready")

        block = ctx.enter_context(nc.Block())

        @block.sync
        def _(sp):
            def load(g, slot, first=False):
                if not first:
                    sp.wait_ge(lo_ready, g - RING + 1)
                sp.dma_start(raw[:, slot, :], stream[g]).then_inc(loaded[slot], 16)

            for s in range(RING):
                load(s, s, True)
            with sp.Fori(1, CHUNKS // RING) as i:
                for s in range(RING):
                    load(i * RING + s, s)
            for t in range(NT):
                sp.wait_ge(fin_ready, t + 1)
                sp.dma_start(out_v[:, t, :], x3[:, t, :]).then_inc(y_out, 16)
            sp.wait_ge(y_out, 16 * NT)

        @block.tensor
        def _(pe):
            def products(dst, acts, kt, t, slot, j, first, last, one_tile=False):
                a_h, a_l = (a[:, kt, 0:P] if one_tile else a[:, kt, t * P:(t + 1) * P] for a in acts)
                wh, wl = (w[:, slot, j * NB:(j + 1) * NB] for w in (w_hi, w_lo))
                pe.matmul(dst, a_h, wh, start=first, stop=False)
                pe.matmul(dst, a_h, wl, start=False, stop=False)
                return pe.matmul(dst, a_l, wh, start=False, stop=last)

            def chunk(v_pair, acts, g, slot, c, n, tiles=NT, one_tile=False):
                pe.wait_ge(lo_ready, g + 1)
                for j in range(CK):
                    kt = c * CK + j
                    for t in range(tiles):
                        mm = products(ps[:, v_pair, t, :], acts, kt, t, slot, j, kt == 0, kt == n * CK - 1,
                                      one_tile)
                mm.then_inc(used, 1)

            def unit(v, pair, acts, g, slot0=0, n=UC, **kw):
                if not (isinstance(v, int) and v < 2):
                    pe.wait_ge(evacuated, v - 1)
                for c in range(n):
                    chunk(pair, acts, g + c, (slot0 + c) % RING, c, n, **kw)

            def pair_of_units(v, p0, acts, g, **kw):
                unit(v, p0, acts, g, **kw)
                unit(v + 1, 1 - p0, acts, g + UC, **kw)

            rounds = [0]

            def open_aux():
                if rounds[0]:
                    pe.wait_ge(aux_free, rounds[0])
                rounds[0] += 1

            def T(dst, src):
                k, m = src.shape[0], src.shape[1]
                return pe.transpose(dst, src, ident[0:k, 0:k])

            def act_T(src, r):
                open_aux()
                v = aux[:, :, :].rearrange("p b (k s) -> p (b k) s", s=SEQ)
                for k in range(8):
                    for t in range(NT):
                        mm = T(v[:, k, t * P:(t + 1) * P], src[:, t, (8 * r + k) * P:(8 * r + k + 1) * P])
                mm.then_inc(aux_full, 1)

            def heads_T(first, second):
                open_aux()
                v = aux[:, :, :].rearrange("p (q b) (h s) -> p q (b h) s", q=2, s=SEQ)
                for q, slot in enumerate((first, second)):
                    for h in range(NH):
                        for t in range(NT):
                            mm = T(v[:, q, h, t * P:(t + 1) * P], proj[:, slot, t, h * HD:(h + 1) * HD])
                mm.then_inc(aux_full, 1)

            def scores(rows_of, keys_of):
                open_aux()
                for h in range(NH):
                    q, k = rows_of(h), keys_of(h)
                    pe.matmul(aux[:, h, 0:P], q[:, 0:P], k[:, 0:P], start=True, stop=True)
                    mm = pe.matmul(aux[:, h, P:LOG_COLS], q[:, P:SEQ], k, start=True, stop=True)
                mm.then_inc(aux_full, 1)

            def probs_T():
                open_aux()
                for h in range(NH):
                    for b in range(3):
                        mm = T(aux[:, h, b * P:(b + 1) * P], pr[:, h, b * P:(b + 1) * P])
                mm.then_inc(aux_full, 1)

            def values_T(slot):
                open_aux()
                v = aux[:, 0:2, :].rearrange("p b (h s) -> p (b h) s", s=SEQ)
                for h in range(NH):
                    pe.matmul(v[:, h, :], proj[:, slot, 0, h * HD:(h + 1) * HD], pT[:, h, 0:SEQ],
                              start=True, stop=False)
                    mm = pe.matmul(v[:, h, P:SEQ], proj[:, slot, 1, h * HD:(h + 1) * HD], pT[:, h, SEQ:LOG_COLS],
                                   start=False, stop=True)
                mm.then_inc(aux_full, 1)

            cb = (cb_hi, cb_lo)
            hT = (act_hi, act_lo)
            pe.wait_ge(consts, 3)
            pe.wait_ge(cb_ready, 1)
            ada = dict(tiles=1, one_tile=True)
            pair_of_units(0, 0, cb, 0, **ada)
            with pe.Fori(1, 8) as i:
                pair_of_units(2 * i, 0, cb, 2 * UC * i, **ada)
            pe.wait_ge(steps_in, 16)
            for b in range(4):
                mm = pe.matmul(aux[:, b, :], mirror[:, :], steps[:, 2 * b:2 * b + 2, :], start=True, stop=True)
            mm.then_inc(bias_full, 1)
            pe.wait_ge(h_ready, 1)
            pe.wait_ge(bias_turned, 1)
            act_T(x1, 0)
            with pe.Fori(8, 10) as i:
                pair_of_units(2 * i, 0, cb, 2 * UC * i, **ada)
            act_T(x1, 1)
            with pe.Fori(10, 12) as i:
                pair_of_units(2 * i, 0, cb, 2 * UC * i, **ada)

            pe.wait_ge(aux_free, 2)
            unit(V_WIN, 0, hT, G_WIN)
            with pe.Fori(0, 2) as i:
                pair_of_units(V_WIN + 1 + 2 * i, 1, hT, G_WIN + UC + 2 * UC * i)
            open_aux()
            vi = aux[0:IDX_DIM, :, :].rearrange("p b (k s) -> p (b k) s", s=SEQ)
            for h in range(NH + 1):
                for t in range(NT):
                    mm = T(vi[:, h, t * P:(t + 1) * P], proj[:, MISC, t, h * IDX_DIM:(h + 1) * IDX_DIM])
            mm.then_inc(aux_full, 1)
            scores(lambda h: iqT[:, h, :], lambda h: iqT[:, NH, :])
            pair_of_units(V_WIN + 5, 1, hT, G_WIN + 5 * UC)
            heads_T(QA, KA)
            scores(lambda h: qkT[:, 0, h, :], lambda h: qkT[:, 1, h, :])
            pair_of_units(V_WIN + 7, 1, hT, G_WIN + 7 * UC)
            pe.wait_ge(p_ready, 1)
            probs_T()
            heads_T(QB, KB)
            pair_of_units(V_WIN + 9, 1, hT, G_WIN + 9 * UC)
            values_T(VA)
            for half in range(2):
                lo = half * DD
                scores(lambda h: qkT[lo:lo + DD, 0, h, :], lambda h: qkT[lo:lo + DD, 1, h, :])
            pair_of_units(V_WIN + 11, 1, hT, G_WIN + 11 * UC)
            pe.wait_ge(p_ready, 2)
            probs_T()
            pe.wait_ge(u_ready, 1)
            heads_T(CG, BG)

            def gate_stage(m):
                yT = (y_hi[:, MIXERS[m]], y_lo[:, MIXERS[m]])
                g0, v0 = G_GATE + m * DB * (UC + BC), V_GATE + m * 2 * DB
                with pe.Fori(0, DB // 2) as i:
                    for b in range(2):
                        g = g0 + (2 * i + b) * (UC + BC)
                        v = v0 + 2 * (2 * i + b)
                        unit(v, 1, hT, g, slot0=b * (UC + BC))
                        if b == 0:
                            if m == 0:
                                pe.wait_ge(yc_ready, 1)
                            else:
                                pe.wait_ge(aux_free, {1: 9, 2: 18, 3: 20}[m])
                        unit(v + 1, 0, yT, g + UC, slot0=b * (UC + BC) + UC, n=BC)

            gate_stage(0)
            open_aux()
            vo = aux[:, 0:2, :].rearrange("p t (h d) -> p t h d", h=NH)
            for h in range(NH):
                v0, v1 = (proj[:, VB, t, h * HD:(h + 1) * HD] for t in range(NT))
                pe.matmul(vo[:, 0, h, :], pT[:, h, 0:P], v0, start=True, stop=True)
                pe.matmul(vo[:, 1, h, :], pT[:, h, P:SEQ], v0, start=True, stop=False)
                mm = pe.matmul(vo[:, 1, h, :], pT[:, h, SEQ:LOG_COLS], v1, start=False, stop=True)
            mm.then_inc(aux_full, 1)
            heads_T(QD, KD)
            pe.wait_ge(ls_ready, 1)
            open_aux()
            vf = aux[:, 0:2, :].rearrange("p b (h s) -> p (b h) s", s=SEQ)
            for h in range(NH):
                pe.matmul(vf[:, h, :], lsig[:, 0, h:h + 1].to_broadcast([P, P]), triones[:, :], start=True, stop=False)
                pe.matmul(vf[:, h, P:SEQ], lsig[:, 1, h:h + 1].to_broadcast([P, P]), triones[:, 0:P],
                          start=False, stop=True)
            pe.matmul(aux[:, 2, 0:NH], triones[:, 0:P], lsig[:, 0, :], start=True, stop=True)
            pe.matmul(aux[:, 2, NH:2 * NH], triones[:, P:SEQ], lsig[:, 0, :], start=True, stop=False)
            pe.matmul(aux[:, 2, NH:2 * NH], triones[:, 0:P], lsig[:, 1, :], start=False, stop=True)\
                .then_inc(aux_full, 1)
            scores(lambda h: qkT[:, 0, h, :], lambda h: qkT[:, 1, h, :])
            gate_stage(1)
            pe.wait_ge(yb_ready, 1)
            open_aux()
            vb = aux[:, 0:2, :].rearrange("p b (h s) -> p (b h) s", s=SEQ)
            for h in range(NH):
                for t in range(NT):
                    mm = T(vb[:, h, t * P:(t + 1) * P], ob[:, t, h, :])
            mm.then_inc(aux_full, 1)
            pe.wait_ge(p_ready, 3)
            probs_T()
            gate_stage(2)
            values_T(VD)
            gate_stage(3)

            pe.wait_ge(merged_ready, 3 * DB)
            act_T(merged, 0)
            act_T(merged, 1)
            pe.wait_ge(aux_free, 22)
            with pe.Fori(0, 2) as i:
                pair_of_units(V_WO + 2 * i, 1, hT, G_WO + 2 * UC * i)
            pe.wait_ge(h_ready, 2)
            act_T(h2, 0)
            act_T(h2, 1)
            pe.wait_ge(aux_free, 24)

            def hidden_T(q, j):
                pe.wait_ge(aux_free, 24 + 4 * q + j)
                pe.wait_ge(a_ready, 4 * q + j + 1)
                for k in range(4):
                    for t in range(NT):
                        mm = T(vb[:, k, t * P:(t + 1) * P], zt[:, j % 2, t, k * P:(k + 1) * P])
                mm.then_inc(aux_full, 1)

            aT = (a_hi, a_lo)
            with pe.Fori(0, FF_GROUPS) as q:
                v, g = V_FF + 2 * DB * q, G_FF + 2 * DB * UC * q
                for j in range(DB):
                    unit(v + j, (1 + j) % 2, hT, g + j * UC)
                    if j:
                        hidden_T(q, j - 1)
                v, g = v + DB, g + DB * UC
                for j in range(DB):
                    pair = (1 + j) % 2
                    pe.wait_ge(evacuated, v + j - 1)
                    for c in range(UC):
                        if j == 0 and c == 0:
                            pe.wait_ge(aux_free, 24 + 4 * q + 3)
                        if j == 0 and c == 3:
                            hidden_T(q, DB - 1)
                        if j == 0 and c == 6:
                            pe.wait_ge(aux_free, 24 + 4 * q + 4)
                        chunk(pair, aT, g + j * UC + c, c % RING, c, UC)

        @block.scalar
        def _(act):
            link = Links(act, act_step)

            def split(g, slot):
                act.wait_ge(loaded[slot], (g - slot) * 4 + 16)
                if not (isinstance(g, int) and g < RING):
                    act.wait_ge(used, g - RING + 1)
                act.activation(w_hi[:, slot, :], raw[:, slot, :], ACT.Copy).then_inc(hi_ready, 1)

            def ahead(g, slot0=0, n=UC):
                for c in range(RING, RING + n):
                    split(g + c, (slot0 + c) % RING)

            act.dma_start(x1[:, :, :], x_v).then_inc(x_loaded, 16)
            act.dma_start(gs1[:, :], bcast_rows(g_norm1[0:1, :])).then_inc(x_loaded, 16)
            act.wait_ge(small_in, 16 * 6)
            act.activation(cc[:, 1, :], cc[:, 0, :], ACT.Sigmoid).then_inc(c_ready, 1)
            for s in range(RING):
                split(s, s)
            act.wait_ge(lam_sum, 1)
            act.activation(lsum[:, 2:4], lsum[:, 0:2], ACT.Exp).then_inc(lam_exp, 1)
            act.wait_ge(x_loaded, 32)
            for t in range(NT):
                if t:
                    act.wait_ge(sumsq, t)
                act.activation(sq_junk[:, :], x1[:, t, :], ACT.Square, accum_out=ss[:, t:t + 1]).then_inc(sumsq, 1)
            act.wait_ge(var_ready, 1)
            act.activation(rstd[:, :], ss[:, :], ACT.Sqrt).then_inc(root, 1)
            with act.Fori(0, 4) as i:
                for b in range(2):
                    ahead((2 * i + b) * UC)
            with act.Fori(4, 8) as i:
                for b in range(2):
                    ahead((2 * i + b) * UC)

            def hi_from_aux(dst, src, a):
                act.wait_ge(aux_full, a + 1)
                act.activation(dst, src, ACT.Copy).then_inc(aux_hi, 1)

            auxw = aux[:, :, :].rearrange("p b n -> p (b n)")
            aux8 = aux[:, :, :].rearrange("p b (k s) -> p (b k) s", s=SEQ)
            aux4 = aux[:, 0:2, :].rearrange("p b (h s) -> p (b h) s", s=SEQ)

            act.wait_ge(bias_full, 1)
            act.activation(Bm[:, :, :], aux8, ACT.Copy).then_inc(bias_turned, 1)
            hi_from_aux(act_hi[:, 0:8, :], aux8, 0)
            with act.Fori(8, 10) as i:
                for b in range(2):
                    ahead((2 * i + b) * UC)
            hi_from_aux(act_hi[:, 8:16, :], aux8, 1)
            with act.Fori(10, 12) as i:
                for b in range(2):
                    ahead((2 * i + b) * UC)

            def take_aux(dst, src, a, func=ACT.Copy):
                act.wait_ge(aux_full, a + 1)
                act.activation(dst, src, func).then_inc(aux_free, 1)

            def take_qk(a):
                take_aux(qkT[:, :, :, :].rearrange("p q h s -> p (q h s)"), auxw, a)

            def exps_of(buf, c, n):
                act.wait_ge(neg_max, n)
                for h in range(NH):
                    for t, (c0, c1) in enumerate(((0, P), (P, LOG_COLS))):
                        act.activation(buf[:, h, c0:c1], buf[:, h, c0:c1], ACT.Exp, bias=nmax[:, c, t, h:h + 1],
                                       accum_out=esum[:, c, t, h:h + 1]).then_inc(exps, 1)

            G = G_WIN
            ahead(G)
            with act.Fori(0, 2) as i:
                for b in range(2):
                    ahead(G + UC + (2 * i + b) * UC)
            act.wait_ge(rows_out, 32)
            take_aux(iqT[:, :, :], aux8[0:IDX_DIM, 0:NH + 1, :], 2)
            take_aux(pr[:, :, :], aux[:, :, 0:LOG_COLS], 3, ACT.Relu)
            ahead(G + 5 * UC)
            ahead(G + 6 * UC)
            take_qk(4)
            exps_of(pr, 0, 1)
            ahead(G + 7 * UC)
            ahead(G + 8 * UC)
            take_aux(pT[:, :, :], aux[:, :, 0:LOG_COLS], 6)
            take_qk(7)
            act.wait_ge(f_abs, 1)
            link(act.activation(lsig2[:, :, :], lsig2[:, :, :], ACT.Exp, scale=-1.0))
            act.activation(lsig2[:, :, :], lsig2[:, :, :], ACT.Ln, bias=1.0).then_inc(f_log, 1)
            ahead(G + 9 * UC)
            ahead(G + 10 * UC)
            hi_from_aux(y_hi[:, 0, :, :], aux4, 8)
            exps_of(pr, 0, 2)
            exps_of(pr2, 1, 3)
            ahead(G + 11 * UC)
            ahead(G + 12 * UC)
            take_aux(pT[:, :, :], aux[:, :, 0:LOG_COLS], 11)
            take_qk(12)
            act.wait_ge(yc_raw, 1)
            act.activation(y_hi[:, 2, :, :], pr[:, :, 0:SEQ], ACT.Copy).then_inc(yc_hi, 1)

            def gate_stage(m):
                g0 = G_GATE + m * DB * (UC + BC)
                with act.Fori(0, DB // 2) as i:
                    for b in range(2):
                        g, s = g0 + (2 * i + b) * (UC + BC), b * (UC + BC)
                        ahead(g, s)
                        act.wait_ge(evacuated, V_GATE + 2 * (m * DB + 2 * i + b) + 1)
                        act.activation(zt[:, 0], zt[:, 0], ACT.Sigmoid).then_inc(gate_ready, 1)
                        ahead(g + UC, s + UC, BC)

            gate_stage(0)
            take_aux(ob[:, :, :, :].rearrange("p t h d -> p (t h d)"), auxw[:, 0:NT * NB], 13)
            take_qk(14)
            act.wait_ge(yb_var, 1)
            act.activation(rec[:, 1, :, :], rec[:, 0, :, :], ACT.Sqrt).then_inc(yb_root, 1)
            exps_of(pr, 0, 4)
            gate_stage(1)
            hi_from_aux(y_hi[:, 1, :, :], aux4, 17)
            take_aux(pT[:, :, :], aux[:, :, 0:LOG_COLS], 18)
            gate_stage(2)
            hi_from_aux(y_hi[:, 3, :, :], aux4, 19)
            gate_stage(3)
            for r in range(2):
                hi_from_aux(act_hi[:, 8 * r:8 * r + 8, :], aux8, 20 + r)
            with act.Fori(0, 2) as i:
                for b in range(2):
                    ahead(G_WO + (2 * i + b) * UC)

            def sumsq_of(n):
                act.wait_ge(x_added, DB if n == 2 else DB * (1 + FF_GROUPS))
                for t in range(NT):
                    if t:
                        act.wait_ge(sumsq, NT * (n - 1) + t)
                    act.activation(gt1b[:, :], x3[:, t, :], ACT.Square, accum_out=ss[:, t:t + 1]).then_inc(sumsq, 1)
                act.wait_ge(var_ready, n)
                act.activation(rstd[:, :], ss[:, :], ACT.Sqrt).then_inc(root, 1)

            sumsq_of(2)
            for r in range(2):
                hi_from_aux(act_hi[:, 8 * r:8 * r + 8, :], aux8, 22 + r)

            def square(q, j):
                act.wait_ge(evacuated, V_FF + 2 * DB * q + j + 1)
                act.activation(zt[:, j % 2], zt[:, j % 2], ACT.Square).then_inc(a_ready, 1)

            def hidden_hi(q, j):
                act.wait_ge(aux_full, 24 + 4 * q + j + 1)
                act.activation(a_hi[:, 4 * j:4 * j + 4, :], aux4, ACT.Copy).then_inc(aux_hi, 1)

            def ff_group(q, last):
                g = G_FF + 2 * DB * UC * q
                for j in range(DB):
                    ahead(g + j * UC)
                    square(q, j)
                    if j:
                        hidden_hi(q, j - 1)
                g = g + DB * UC
                for j in range(DB):
                    for c in range(RING, RING + UC):
                        if j == 0 and c == RING + 3:
                            hidden_hi(q, DB - 1)
                        if not (last and j == DB - 1 and c >= UC):
                            split(g + j * UC + c, c % RING)

            with act.Fori(0, FF_GROUPS - 1) as q:
                ff_group(q, False)
            ff_group(FF_GROUPS - 1, True)
            sumsq_of(3)

        @block.vector
        def _(dve):
            link = Links(dve, dve_step)

            def split(g, slot):
                dve.wait_ge(hi_ready, g + 1)
                dve.tensor_tensor(w_lo[:, slot, :], raw[:, slot, :], w_hi[:, slot, :].bitcast(F32), ALU.subtract)\
                    .then_inc(lo_ready, 1)

            def ahead(g, slot0=0, n=UC):
                for c in range(RING, RING + n):
                    split(g + c, (slot0 + c) % RING)

            def lo_from_aux(dst, src, hi, a):
                dve.wait_ge(aux_hi, a)
                dve.tensor_tensor(dst, src, hi.bitcast(F32), ALU.subtract).then_inc(aux_free, 1)

            aux8 = aux[:, :, :].rearrange("p b (k s) -> p (b k) s", s=SEQ)
            aux4 = aux[:, 0:2, :].rearrange("p b (h s) -> p (b h) s", s=SEQ)

            def wide(ap, n):
                return ap.unsqueeze(1).to_broadcast([P, n, ap.shape[1]])

            dve.wait_ge(c_ready, 1)
            link(dve.tensor_tensor(cc[:, 2, :], cc[:, 0, :], cc[:, 1, :], ALU.mult))
            cw = cc[:, 2, :].unsqueeze(2).to_broadcast([P, KT, P])
            link(dve.tensor_copy(cb_hi[:, :, :], cw))
            dve.tensor_tensor(cb_lo[:, :, :], cw, cb_hi[:, :, :].bitcast(F32), ALU.subtract).then_inc(cb_ready, 1)
            for s in range(RING):
                split(s, s)
            link(dve.tensor_tensor(lprod[:, :, :], lamb[:, 0:4:2, :], lamb[:, 1:4:2, :], ALU.mult))
            dve.tensor_reduce(lsum[:, 0:2], lprod[:, :, :], AX_X, ALU.add).then_inc(lam_sum, 1)
            for b, n0, n1 in t5_runs():
                link.step(dve.tensor_copy(dist[:, SEQ - n1:SEQ - n0], tabT[:, b:b + 1].to_broadcast([8, n1 - n0])))
            link(dve.tensor_copy(dist[:, SEQ:LOG_COLS], tabT[:, 0:1].to_broadcast([8, LOG_COLS - SEQ])))
            dve.tensor_scalar(gsub[:, :], gsub[:, :], 1.0 - LAM_INIT, None, ALU.mult).then_inc(dist_ready, 1)
            dve.wait_ge(lam_exp, 1)
            link(dve.tensor_tensor(nlam[:, :], lsum[:, 3:4], lsum[:, 2:3], ALU.subtract))
            link(dve.tensor_scalar(nlam[:, :], nlam[:, :], -LAM_INIT, None, ALU.add))

            def variance(n):
                dve.wait_ge(sumsq, NT * n)
                dve.tensor_scalar(ss[:, :], ss[:, :], 1.0 / D, EPS, ALU.mult, ALU.add).then_inc(var_ready, 1)
                dve.wait_ge(root, n)
                link(dve.reciprocal(rstd[:, :], rstd[:, :]))

            variance(1)

            def evac_begin(v_end):
                dve.wait_ge(used, v_end)

            with dve.Fori(0, 2) as i:
                for b in range(2):
                    g = (2 * i + b) * UC
                    ahead(g)
                    evac_begin(g + UC)
                    dve.wait_ge(brow_in[b], 16 * i + 16)
                    dve.tensor_tensor(sh1[:, bass.ts(2 * i + b, NB)], ps[:, b, 0, :], brow[:, b, :], ALU.add)\
                        .then_inc(evacuated, 1)
            dve.wait_ge(x_loaded, 32)
            with dve.Fori(0, 2) as i:
                link.enter(i, 2)
                for b in range(2):
                    g = 4 * UC + (2 * i + b) * UC
                    ahead(g)
                    evac_begin(g + UC)
                    dve.wait_ge(brow_in[b], 16 * i + 48)
                    dve.tensor_tensor(zt[:, 0, 0, :], ps[:, b, 0, :], brow[:, b, :], ALU.add).then_inc(evacuated, 1)
                    dve.wait_ge(evacuated, 5 + 2 * i + b)
                    col = bass.ts(2 * i + b, NB)
                    link(dve.scalar_tensor_tensor(gs1[:, col], zt[:, 0, 0, :], 1.0, gs1[:, col], ALU.add, ALU.mult))
            link.leave(2)
            for t in range(NT):
                link.step(dve.scalar_tensor_tensor(x1[:, t, :], x1[:, t, :], rstd[:, t:t + 1], gs1[:, :],
                                                   ALU.mult, ALU.mult))
            link.wait()
            for t in range(NT):
                h_add = dve.tensor_tensor(x1[:, t, :], x1[:, t, :], sh1[:, :], ALU.add)
                if t == NT - 1:
                    h_add.then_inc(h_ready, 1)

            def mod_rows(i, dst, i0):
                for b in range(2):
                    g = (2 * i + b) * UC
                    ahead(g)
                    evac_begin(g + UC)
                    dve.wait_ge(brow_in[b], 16 * i + 16)
                    dve.tensor_tensor(dst[:, bass.ts(2 * i + b - 2 * i0, NB)], ps[0:1, b, 0, :], brow[0:1, b, :], ALU.add)\
                        .then_inc(evacuated, 1)

            with dve.Fori(4, 8) as i:
                mod_rows(i, rows_a, 4)
            lo_from_aux(act_lo[:, 0:8, :], aux8, act_hi[:, 0:8, :], 1)
            with dve.Fori(8, 10) as i:
                mod_rows(i, rows_b, 8)
            lo_from_aux(act_lo[:, 8:16, :], aux8, act_hi[:, 8:16, :], 2)
            with dve.Fori(10, 12) as i:
                mod_rows(i, rows_b, 8)

            def win(u, pair, slot):
                ahead(G_WIN + u * UC)
                evac_begin(G_WIN + (u + 1) * UC)
                dve.tensor_scalar(proj[:, slot], ps[:, pair], 1.0, None, ALU.mult).then_inc(evacuated, 1)

            def softmax_max(buf, c):
                link.step(dve.tensor_reduce(nmax[:, c, 0, :], buf[:, :, 0:P], AX_X, ALU.max, negate=True))
                dve.tensor_reduce(nmax[:, c, 1, :], buf[:, :, P:LOG_COLS], AX_X, ALU.max, negate=True)\
                    .then_inc(neg_max, 1)

            def weigh(buf, r, last=None):
                for t, (c0, c1) in enumerate(((0, P), (P, LOG_COLS))):
                    f = r[:, t, :].unsqueeze(2).to_broadcast([P, NH, c1 - c0])
                    ins = dve.tensor_tensor(buf[:, :, c0:c1], buf[:, :, c0:c1], f, ALU.mult)
                    if t == 0 or last is None:
                        link.step(ins)
                if last is not None:
                    ins.then_inc(last, 1)

            def logits(buf, scale, head0, a):
                dve.wait_ge(aux_full, a + 1)
                link.step(dve.scalar_tensor_tensor(buf[:, :, 0:P], aux[:, :, 0:P], scale,
                                                   Bm[:, head0:head0 + NH, P:SEQ], ALU.mult, ALU.add))
                dve.scalar_tensor_tensor(buf[:, :, P:LOG_COLS], aux[:, :, P:LOG_COLS], scale,
                                         Bm[:, head0:head0 + NH, :], ALU.mult, ALU.add).then_inc(aux_free, 1)
                link.wait()
                dve.wait_ge(aux_free, a + 1)

            win(0, 0, MISC)
            with dve.Fori(0, 2) as i:
                for b in range(2):
                    g = G_WIN + UC + (2 * i + b) * UC
                    ahead(g)
                    evac_begin(g + UC)
                    dve.tensor_scalar(proj[:, 1 + 2 * i + b], ps[:, 1 - b], 1.0, None, ALU.mult)\
                        .then_inc(evacuated, 1)
            dve.wait_ge(evacuated, V_WIN + 5)
            link(dve.tensor_scalar(iws[:, :, :], proj[:, MISC, :, IW0:IW0 + NH], IDX_SCALE, None, ALU.mult))
            link(dve.tensor_tensor(lsig[:, :, :], proj[:, MISC, :, FD0:FD0 + NH], wide(bf[:, :], NT), ALU.add))
            link(dve.tensor_scalar(lsig2[:, :, :], lsig[:, :, :], -1.0, None, ALU.mult))
            dve.tensor_tensor(lsig2[:, :, :], lsig2[:, :, :], lsig[:, :, :], ALU.max).then_inc(f_abs, 1)
            dve.wait_ge(aux_free, 4)
            spans = ((0, P), (P, LOG_COLS))
            for t, (c0, c1) in enumerate(spans):
                link.step(dve.tensor_scalar(score[:, c0:c1], pr[:, 0, c0:c1], iws[:, t, 0:1], 0.0, ALU.mult, ALU.add))
            link.wait()
            for h in range(1, NH):
                for t, (c0, c1) in enumerate(spans):
                    ins = dve.scalar_tensor_tensor(score[:, c0:c1], pr[:, h, c0:c1], iws[:, t, h:h + 1],
                                                   score[:, c0:c1], ALU.mult, ALU.add)
                    if h < NH - 1 or t == 0:
                        link.step(ins)
                    else:
                        ins.then_inc(score_ready, 1)
                link.wait()
            dve.wait_ge(score_masked, 1)
            for r in range(K_TOP // 8):
                src = score if r == 0 else work
                for t, (c0, c1) in enumerate(spans):
                    link.step(dve.max(m8[:, t, :], src[:, c0:c1]))
                link.wait()
                for t, (c0, c1) in enumerate(spans):
                    link.step(dve.match_replace(work[:, c0:c1], m8[:, t, :], src[:, c0:c1], TAKEN))
                link.wait()
            link(dve.tensor_scalar(selm[:, :], work[:, :], TAKEN / 2, NEG, ALU.is_gt, ALU.mult))
            win(5, 1, KB)
            win(6, 0, VB)
            dve.wait_ge(bm_ready, 1)
            logits(pr, HD ** -0.5, 0, 5)
            for t, (c0, c1) in enumerate(spans):
                link.step(dve.tensor_tensor(pr[:, :, c0:c1], pr[:, :, c0:c1],
                                            selm[:, c0:c1].unsqueeze(1).to_broadcast([P, NH, c1 - c0]), ALU.add))
            link.wait()
            softmax_max(pr, 0)
            dve.wait_ge(exps, 1 * NT * NH)
            link(dve.reciprocal(rec[:, 0, :, :], esum[:, 0, :, :]))
            weigh(pr, rec[:, 0], p_ready)
            win(7, 1, BG)
            win(8, 0, CG)
            dve.wait_ge(f_log, 1)
            link(dve.tensor_scalar(lsig[:, :, :], lsig[:, :, :], 0.0, None, ALU.min))
            dve.tensor_tensor(lsig[:, :, :], lsig[:, :, :], lsig2[:, :, :], ALU.subtract).then_inc(ls_ready, 1)
            win(9, 1, XIN)
            win(10, 0, QD)
            lo_from_aux(y_lo[:, 0, :, :], aux4, y_hi[:, 0, :, :], 3)
            for c, buf in enumerate((pr, pr2)):
                logits(buf, DD ** -0.5, NH, 9 + c)
                softmax_max(buf, c)
            dve.wait_ge(exps, 2 * NT * NH)
            link(dve.reciprocal(rec[:, 0, :, :], esum[:, 0, :, :]))
            weigh(pr, rec[:, 0])
            dve.wait_ge(exps, 3 * NT * NH)
            link(dve.reciprocal(rec[:, 1, :, :], esum[:, 1, :, :]))
            link(dve.tensor_scalar(rec[:, 1, :, :], rec[:, 1, :, :], nlam[:, 0:1], None, ALU.mult))
            weigh(pr2, rec[:, 1])
            link.wait()
            dve.tensor_tensor(pr[:, :, :], pr[:, :, :], pr2[:, :, :], ALU.add).then_inc(p_ready, 1)
            dve.wait_ge(evacuated, V_WIN + 10)
            dve.tensor_tensor(proj[:, CG], proj[:, CG], proj[:, XIN], ALU.mult).then_inc(u_ready, 1)
            win(11, 1, KD)
            win(12, 0, VD)
            dve.wait_ge(aux_free, 13)
            for k in range(NH):
                link.step(dve.tensor_scalar(pr[:, k, 0:SEQ], qkT[:, 0, k, :], convw[:, k, 2:3], None, ALU.mult))
            link.wait()
            for d in (1, 2):
                for k in range(NH):
                    link.step(dve.scalar_tensor_tensor(pr[:, k, d:SEQ], qkT[:, 0, k, 0:SEQ - d],
                                                       convw[:, k, 2 - d:3 - d], pr[:, k, d:SEQ],
                                                       ALU.mult, ALU.add))
                link.wait()
            dve.tensor_tensor(pr[:, :, 0:SEQ], pr[:, :, 0:SEQ], qkT[:, 1, :, :], ALU.mult).then_inc(yc_raw, 1)
            dve.wait_ge(yc_hi, 1)
            dve.tensor_tensor(y_lo[:, 2, :, :], pr[:, :, 0:SEQ], y_hi[:, 2, :, :].bitcast(F32), ALU.subtract)\
                .then_inc(yc_ready, 1)

            def gate_stage(m):
                g0 = G_GATE + m * DB * (UC + BC)
                with dve.Fori(0, DB // 2) as i:
                    for b in range(2):
                        n = 2 * i + b
                        g, s = g0 + n * (UC + BC), b * (UC + BC)
                        ahead(g, s)
                        evac_begin(g + UC)
                        dve.wait_ge(brow_in[b], (ADA_UNITS + m * DB) * 8 + 16 * i + 16)
                        dve.tensor_tensor(zt[:, 0], ps[:, 1], wide(brow[:, b, :], NT), ALU.add).then_inc(evacuated, 1)
                        ahead(g + UC, s + UC, BC)
                        evac_begin(g + UC + BC)
                        dve.wait_ge(gate_ready, m * DB + n + 1)
                        col = bass.ts(n, NB)
                        if m == 0:
                            dve.tensor_tensor(merged[:, :, col], ps[:, 0], zt[:, 0], ALU.mult).then_inc(evacuated, 1)
                        else:
                            dve.tensor_tensor(zt[:, 1], ps[:, 0], zt[:, 0], ALU.mult).then_inc(evacuated, 1)
                            dve.wait_ge(evacuated, V_GATE + 2 * (m * DB + n) + 2)
                            if m > 1:
                                dve.wait_ge(merged_ready, (m - 2) * DB + n + 1)
                            dve.tensor_tensor(merged[:, :, col], merged[:, :, col], zt[:, 1], ALU.add)\
                                .then_inc(merged_ready, 1)

            gate_stage(0)
            dve.wait_ge(aux_free, 14)
            sq = zt[:, 1].rearrange("p t (h d) -> p t h d", h=NH)
            link(dve.tensor_tensor(sq, ob[:, :, :, :], ob[:, :, :, :], ALU.mult))
            link(dve.tensor_reduce(rec[:, 0, :, :], sq, AX_X, ALU.add))
            dve.tensor_scalar(rec[:, 0, :, :], rec[:, 0, :, :], 1.0 / HD, EPS, ALU.mult, ALU.add).then_inc(yb_var, 1)
            dve.wait_ge(yb_root, 1)
            link(dve.reciprocal(rec[:, 1, :, :], rec[:, 1, :, :]))
            obv = ob[:, :, :, :].rearrange("p t h d -> p (t h) d")
            rv = rec[:, 1, :, :].rearrange("p t h -> p (t h)")
            link(dve.tensor_tensor(obv, obv, rv.unsqueeze(2).to_broadcast([P, NT * NH, HD]), ALU.mult))
            dve.tensor_tensor(obv, obv, wide(gsub[:, :], NT * NH), ALU.mult).then_inc(yb_ready, 1)
            dve.wait_ge(aux_full, 16)
            link(dve.tensor_scalar(Ftok[:, :, :].rearrange("p t h -> p (t h)"), aux[:, 2, 0:2 * NH], 1.0, None,
                                   ALU.mult))
            for h in range(NH):
                for t, (c0, c1) in enumerate(spans):
                    ins = dve.tensor_scalar(pr[:, h, c0:c1], aux4[:, h, 0:c1 - c0], -1.0, Ftok[:, t, h:h + 1],
                                            ALU.mult, ALU.add)
                    if (h, t) == (NH - 1, 1):
                        ins.then_inc(aux_free, 1)
                    else:
                        link.step(ins)
            link.wait()
            dve.wait_ge(aux_free, 16)
            dve.wait_ge(dm_ready, 1)
            dve.wait_ge(aux_full, 17)
            link.step(dve.scalar_tensor_tensor(pr[:, :, 0:P], aux[:, :, 0:P], HD ** -0.5, pr[:, :, 0:P],
                                               ALU.mult, ALU.add))
            dve.scalar_tensor_tensor(pr[:, :, P:LOG_COLS], aux[:, :, P:LOG_COLS], HD ** -0.5, pr[:, :, P:LOG_COLS],
                                     ALU.mult, ALU.add).then_inc(aux_free, 1)
            link.wait()
            dve.wait_ge(aux_free, 17)
            softmax_max(pr, 0)
            dve.wait_ge(exps, 4 * NT * NH)
            link(dve.reciprocal(rec[:, 0, :, :], esum[:, 0, :, :]))
            weigh(pr, rec[:, 0], p_ready)
            gate_stage(1)
            lo_from_aux(y_lo[:, 1, :, :], aux4, y_hi[:, 1, :, :], 4)
            gate_stage(2)
            lo_from_aux(y_lo[:, 3, :, :], aux4, y_hi[:, 3, :, :], 5)
            gate_stage(3)
            for r in range(2):
                lo_from_aux(act_lo[:, 8 * r:8 * r + 8, :], aux8, act_hi[:, 8 * r:8 * r + 8, :], 6 + r)
            dve.wait_ge(late_in, 16 * 6)
            dve.scalar_tensor_tensor(gs2[:, :], gs2[:, :], 1.0, gnb[:, :], ALU.add, ALU.mult).then_inc(gs2_ready, 1)

            def add_to_x(v, col, pair, b, gate, added=None):
                dve.tensor_tensor(zt[:, b], ps[:, pair], wide(gate[:, col], NT), ALU.mult)\
                    .then_inc(evacuated, 1)
                dve.wait_ge(evacuated, v + 1)
                if added is not None:
                    dve.wait_ge(x_added, added)
                dve.tensor_tensor(x3[:, :, col], x3[:, :, col], zt[:, b], ALU.add).then_inc(x_added, 1)

            with dve.Fori(0, 2) as i:
                for b in range(2):
                    g = G_WO + (2 * i + b) * UC
                    ahead(g)
                    evac_begin(g + UC)
                    add_to_x(V_WO + 2 * i + b, bass.ts(2 * i + b, NB), 1 - b, b, gt1b)
            dve.wait_ge(x_added, DB)
            variance(2)
            dve.wait_ge(gs2_ready, 1)
            for t in range(NT):
                link.step(dve.scalar_tensor_tensor(h2[:, t, :], x3[:, t, :], rstd[:, t:t + 1], gs2[:, :],
                                                   ALU.mult, ALU.mult))
            link.wait()
            for t in range(NT):
                h_add = dve.tensor_tensor(h2[:, t, :], h2[:, t, :], sh2b[:, :], ALU.add)
                if t == NT - 1:
                    h_add.then_inc(h_ready, 1)
            for r in range(2):
                lo_from_aux(act_lo[:, 8 * r:8 * r + 8, :], aux8, act_hi[:, 8 * r:8 * r + 8, :], 8 + r)

            def hidden_lo(q, j):
                dve.wait_ge(aux_hi, 9 + 4 * q + j + 1)
                dve.tensor_tensor(a_lo[:, 4 * j:4 * j + 4, :], aux4, a_hi[:, 4 * j:4 * j + 4, :].bitcast(F32),
                                  ALU.subtract).then_inc(aux_free, 1)

            def ff_group(q, last):
                v, g = V_FF + 2 * DB * q, G_FF + 2 * DB * UC * q
                for j in range(DB):
                    ahead(g + j * UC)
                    evac_begin(g + (j + 1) * UC)
                    dve.tensor_scalar(zt[:, j % 2], ps[:, (1 + j) % 2], 0.0, None, ALU.max).then_inc(evacuated, 1)
                    if j:
                        hidden_lo(q, j - 1)
                v, g = v + DB, g + DB * UC
                for j in range(DB):
                    for c in range(RING, RING + UC):
                        if j == 0 and c == RING + 3:
                            hidden_lo(q, DB - 1)
                        if not (last and j == DB - 1 and c >= UC):
                            split(g + j * UC + c, c % RING)
                    evac_begin(g + (j + 1) * UC)
                    add_to_x(v + j, slice(j * NB, (j + 1) * NB), (1 + j) % 2, j % 2, gt2b,
                             DB * (1 + q) + j)

            with dve.Fori(0, FF_GROUPS - 1) as q:
                ff_group(q, False)
            ff_group(FF_GROUPS - 1, True)
            dve.wait_ge(x_added, DB * (1 + FF_GROUPS))
            variance(3)
            dve.wait_ge(gfin_in, 16)
            for t in range(NT):
                dve.scalar_tensor_tensor(x3[:, t, :], x3[:, t, :], rstd[:, t:t + 1], gnb[:, :], ALU.mult, ALU.mult)\
                    .then_inc(fin_ready, 1)

        @block.gpsimd
        def _(pool):
            link = Links(pool, pool_step)
            for dst, src in ((cc[:, 0, :], c_cols), (convw[:, :, :], conv_cols), (tabT[:, :], tab),
                             (bf[:, :], bcast_rows(b_f[0:1, :])), (gsub[:, :], bcast_rows(g_subln[0:1, :])),
                             (lamb[:, :, :].rearrange("p a d -> p (a d)"), bcast_rows(lam[0:1, :]))):
                pool.dma_start(dst, src).then_inc(small_in, 16)
            link(pool.memset(ident[:, :], 0.0))
            pool.affine_select(out=ident[:, :], in_=ident[:, :], compare_op=ALU.not_equal, fill=1.0, base=0,
                               pattern=[[-1, P]], channel_multiplier=1).then_inc(consts, 1)
            link(pool.memset(mirror[:, :], 0.0))
            pool.affine_select(out=mirror[:, :], in_=mirror[:, :], compare_op=ALU.not_equal, fill=1.0, base=1 - P,
                               pattern=[[1, P]], channel_multiplier=1).then_inc(consts, 1)
            link(pool.memset(triones[:, :], 1.0))
            pool.affine_select(out=triones[:, :], in_=triones[:, :], compare_op=ALU.is_ge, fill=0.0, base=0,
                               pattern=[[1, SEQ]], channel_multiplier=-1).then_inc(consts, 1)

            def bias_of(r):
                return bcast_rows(bias_rows[bass.ds(r, 1), :])

            for b in range(2):
                pool.dma_start(brow[:, b, :], bcast_rows(bias_rows[b:b + 1, :])).then_inc(brow_in[b], 16)
            pool.wait_ge(dist_ready, 1)
            pool.dma_start(dist_d.ap(), dist[:, :]).then_inc(dist_out, 16)

            def ada_rows(i):
                for b in range(2):
                    pool.wait_ge(evacuated, 2 * i + b - 1)
                    pool.dma_start(brow[:, b, :], bias_of(2 * i + b)).then_inc(brow_in[b], 16)

            with pool.Fori(1, 4) as i:
                ada_rows(i)
            pool.wait_ge(dist_out, 16)
            pool.dma_start(steps[:, :, :], bass.AP(tensor=dist_d, offset=0,
                                                   ap=[[1, P], [LOG_COLS, 2 * NH], [1, SEQ]])).then_inc(steps_in, 16)
            with pool.Fori(4, 8) as i:
                ada_rows(i)
            pool.wait_ge(bias_turned, 1)
            pool.affine_select(out=Bm[:, :, :], in_=Bm[:, :, :], compare_op=ALU.is_ge, fill=NEG, base=P,
                               pattern=[[0, 2 * NH], [-1, SEQ]], channel_multiplier=1).then_inc(bm_ready, 1)
            with pool.Fori(8, ADA_UNITS // 2) as i:
                ada_rows(i)
            pool.wait_ge(evacuated, ADA_UNITS)
            pool.dma_start(mods_d.ap()[:, 0:8 * NB], rows_a[:, :]).then_inc(rows_out, 16)
            pool.dma_start(mods_d.ap()[:, 8 * NB:16 * NB], rows_b[:, :]).then_inc(rows_out, 16)

            def causal(t0, t1, pat, sem_out):
                link.step(pool.affine_select(out=t0, in_=t0, compare_op=ALU.is_ge, fill=NEG,
                                             base=0, pattern=pat + [[-1, P]], channel_multiplier=1))
                link.wait()
                pool.affine_select(out=t1, in_=t1, compare_op=ALU.is_ge, fill=NEG, base=P, pattern=pat + [[-1, SEQ]], channel_multiplier=1)\
                    .then_inc(sem_out, 1)

            pool.wait_ge(score_ready, 1)
            causal(score[:, 0:P], score[:, P:LOG_COLS], [], score_masked)

            def gate_rows(m):
                with pool.Fori(0, DB // 2) as i:
                    for b in range(2):
                        n = 2 * i + b
                        pool.wait_ge(evacuated, V_GATE + 2 * (m * DB + n) - 3)
                        pool.dma_start(brow[:, b, :], bias_of(ADA_UNITS + m * DB + n)).then_inc(brow_in[b], 16)

            gate_rows(0)
            pool.wait_ge(aux_free, 16)
            causal(pr[:, :, 0:P], pr[:, :, P:LOG_COLS], [[0, NH]], dm_ready)
            for m in (1, 2, 3):
                gate_rows(m)
            pool.wait_ge(rows_out, 32)
            pool.wait_ge(aux_free, 20)
            pool.dma_start(x3[:, :, :], x_v).then_inc(late_in, 16)
            for dst, k in ((gt1b, 0), (sh2b, 1), (gs2, 2), (gt2b, 3)):
                pool.dma_start(dst[:, :], bcast_rows(mods_d.ap()[0:1, k * D:(k + 1) * D])).then_inc(late_in, 16)
            pool.dma_start(gnb[:, :], bcast_rows(g_norm2[0:1, :])).then_inc(late_in, 16)
            pool.wait_ge(gs2_ready, 1)
            pool.dma_start(gnb[:, :], bcast_rows(g_final[0:1, :])).then_inc(gfin_in, 16)
            pool.wait_ge(gfin_in, 16)


def tiles(w):
    import numpy as np
    k, n = w.shape
    return np.ascontiguousarray(w.reshape(k // (CK * P), CK, P, n // NB, NB).transpose(3, 0, 2, 1, 4))\
        .reshape(-1, P, CK * NB)


def kernel(**inputs):
    import numpy as np
    import concourse.bacc as bacc
    from concourse.bass_utils import run_bass_kernel_spmd

    i = {k: np.asarray(v) for k, v in inputs.items()}
    w_in = i["w_in"][0]
    cuts = np.cumsum([0, 512, 512, 512, 256, 64, 4, 512, 512, 512, 512, 512, 512, 512, 512, 512, 4])
    qa, ka, va, iq, ik, iw, qb, kb, vb, bg, cg, xin, qd, kd, vd, fd = (
        w_in[:, a:b] for a, b in zip(cuts[:-1], cuts[1:]))
    pad = np.zeros((D, NB - IK0 - IDX_DIM - 2 * NH), w_in.dtype)
    stream = [tiles(i["w_ada"][0])]
    stream += [tiles(np.concatenate([iq, ik, iw, fd, pad], axis=1))]
    stream += [tiles(w) for w in (qa, ka, va, qb, kb, vb, bg, cg, xin, qd, kd, vd)]
    for m in MIXERS:
        gate = tiles(i["w_gate"][0][:, m * D:(m + 1) * D]).reshape(DB, UC, P, CK * NB)
        branch = tiles(i["w_branch"][0, m]).reshape(DB, BC, P, CK * NB)
        stream += [np.concatenate([gate, branch], axis=1).reshape(-1, P, CK * NB)]
    stream += [tiles(i["w_o"][0])]
    for q in range(FF_GROUPS):
        stream += [tiles(i["w_ff1"][0][:, q * D:(q + 1) * D]), tiles(i["w_ff2"][0][q * D:(q + 1) * D, :])]
    stream = np.concatenate(stream, axis=0)
    b_gate = i["b_gate"][0].reshape(4, DB, NB)
    arrays = {
        "stream": stream,
        "bias_rows": np.concatenate([i["b_ada"][0].reshape(-1, NB)] + [b_gate[m] for m in MIXERS], axis=0),
        "x": i["x"][0],
        "c_cols": np.ascontiguousarray(i["c"][0].reshape(KT, P).T),
        "conv_cols": np.ascontiguousarray(i["conv_w"][0].reshape(3, NH, P).transpose(2, 1, 0)),
        "lam": i["lam"].reshape(1, 4 * DD),
        "g_subln": i["g_subln"].reshape(1, HD),
        "tab": np.ascontiguousarray(i["rel_bias"].T),
        "b_f": i["b_f"].reshape(1, NH),
        "g_norm1": i["g_norm1"].reshape(1, D),
        "g_norm2": i["g_norm2"].reshape(1, D),
        "g_final": i["g_final"].reshape(1, D),
    }
    nc = bacc.Bacc("TRN2", target_bir_lowering=False, num_devices=1)
    args = [nc.dram_tensor(f"in_{k}", a.shape, mybir.dt.from_np(a.dtype), kind="ExternalInput").ap()
            for k, a in arrays.items()]
    args.append(nc.dram_tensor("out_x", (SEQ, D), F32, kind="ExternalOutput").ap())
    build(nc, *args)
    r = run_bass_kernel_spmd(nc, [{f"in_{k}": a for k, a in arrays.items()}], core_ids=[0])
    return r.results[0]["out_x"].reshape(1, SEQ, D)
```

```python
import math
from contextlib import ExitStack

import concourse.bass as bass
from concourse import mybir

F32 = mybir.dt.float32
F32R = mybir.dt.float32r
ALU = mybir.AluOpType
ACT = mybir.ActivationFunctionType
AX_X = mybir.AxisListType.X

P = 128
D = 2048
SEQ = 256
NT = SEQ // P
KT = D // P
NB = 512
DB = D // NB
HD = 128
NH = 4
DD = HD // 2
IDX_DIM = 64
K_TOP = 64
N_BUCKETS = 32
MAX_DIST = 128
EPS = 1e-6
NEG = -1e30
TAKEN = -3e38
IDX_SCALE = (IDX_DIM ** -0.5) * (NH ** -0.5)
LAM_INIT = 0.8 - 0.6 * math.exp(0.0)
LOG_COLS = P + SEQ

RING = 4
CK = 2
UC = KT // CK
BC = NH // CK
ADA_UNITS = 2 * DB
WIN_UNITS = 13
GATE_UNITS = 2 * 4 * DB
MIXERS = (2, 0, 1, 3)
G_WIN = ADA_UNITS * UC
G_GATE = G_WIN + WIN_UNITS * UC
G_WO = G_GATE + 4 * DB * (UC + BC)
G_FF = G_WO + DB * UC
CHUNKS = G_FF + 32 * UC
V_WIN = ADA_UNITS
V_GATE = V_WIN + WIN_UNITS
V_WO = V_GATE + GATE_UNITS
V_FF = V_WO + DB
FF_GROUPS = 4
MOD_W = 2 * NB
MOD_BLOCKS = 4 * D // MOD_W
MOD_STEPS = MOD_BLOCKS * KT

ROUNDS = ["h0", "h1", "h2", "h3", "idx_T", "mod0", "idx_dots", "A_qk", "A_dots", "B_qk", "A_pT", "A_y",
          "B_dots0", "B_dots1", "mod1", "row0", "B_pT", "C_T", "B_o", "D_qk", "D_sums", "D_dots", "mod2",
          "D_pT", "mod3", "row1", "B_y", "mod4", "D_y", "mod5", "row2", "mod6", "m0", "m1", "m2", "m3",
          "mod7", "row3", "n0", "n1", "n2", "n3"]
RND = {name: i for i, name in enumerate(ROUNDS)}
HI_ROUNDS = [r for r in ROUNDS if r[0] in "hmn" and len(r) == 2 or r in ("A_y", "B_y", "D_y")]

MISC, QA, KA, VA, QB, KB, VB, BG, CG, XIN = range(10)
QD, KD, VD = QA, KA, VA
IK0 = 4 * IDX_DIM
IW0 = IK0 + IDX_DIM
FD0 = IW0 + NH


class Links:

    def __init__(self, eng, sem):
        self.eng, self.sem, self.base, self.n = eng, sem, 0, 0

    def enter(self, i, per):
        self.base0, self.per = self.base + self.n, per
        self.base, self.n = self.base0 + i * per, 0

    def leave(self, times):
        assert self.n == self.per, (self.n, self.per)
        self.base, self.n = self.base0 + times * self.per, 0

    def step(self, ins):
        ins.then_inc(self.sem, 1)
        self.n += 1

    def wait(self):
        self.eng.wait_ge(self.sem, self.base + self.n)

    def __call__(self, ins):
        self.step(ins)
        self.wait()


def t5_runs():
    exact = N_BUCKETS // 2
    of = [n if n < exact else min(N_BUCKETS - 1, exact + int(math.log(n / exact) / math.log(MAX_DIST / exact)
                                                            * (N_BUCKETS - exact))) for n in range(SEQ)]
    return [(b, of.index(b), SEQ - of[::-1].index(b)) for b in sorted(set(of))]


def build(nc, stream, mod_stream, bias_rows, x_in, c_cols, conv_cols, lam, g_subln, tab, b_f, bada_cols, g_norm1, g_norm2, g_final, out):
    base = (nc.sbuf_base + 31) // 32 * 32
    K = 1024

    def at(name, off, shape, dt=F32):
        return nc.alloc_sbuf_tensor_at(name, shape, dt, offset=base + int(off))

    raw = at("raw", 0, [P, RING, CK * NB])
    w_hi = at("w_hi", 16 * K, [P, RING, CK * NB], F32R)
    w_lo = at("w_lo", 32 * K, [P, RING, CK * NB], F32R)
    act_hi = at("act_hi", 48 * K, [P, KT, SEQ], F32R)
    act_lo = at("act_lo", 64 * K, [P, KT, SEQ], F32R)
    sq_junk = at("sq_junk", 48 * K, [P, D])
    Z = 80 * K
    ident = at("ident", Z, [P, P])
    triones = at("triones", Z + 512, [P, SEQ])
    so = [Z + 1536]

    def small(name, shape):
        n = 1
        for s in shape[1:]:
            n *= s
        t = at(name, (so[0] + 31) // 32 * 32, shape)
        so[0] = (so[0] + 31) // 32 * 32 + 4 * n
        return t

    gsub = small("gsub", [P, HD])
    convw = small("convw", [P, NH, 3])
    bf = small("bf", [P, NH])
    nlam = small("nlam", [P, 1])
    ss = small("ss", [P, 2])
    rstd = small("rstd", [P, 2])
    iws = small("iws", [P, NT, NH])
    lsig = small("lsig", [P, NT, NH])
    lsig2 = small("lsig2", [P, NT, NH])
    Ftok = small("Ftok", [P, NT, NH])
    nmax = small("nmax", [P, 2, NT, NH])
    esum = small("esum", [P, 2, NT, NH])
    rec = small("rec", [P, 2, NT, NH])
    m8 = small("m8", [P, NT, 8])
    ss4 = small("ss4", [P, NT, DB])
    csil = small("csil", [P, KT])
    assert so[0] <= Z + 3 * K
    brow = at("brow", Z + 3 * K, [P, 2, NB])
    zt = at("zt", Z + 7 * K, [P, 2, NT, NB])
    x1 = at("x1", Z + 15 * K, [P, NT, D])
    sh1 = at("sh1", Z + 31 * K, [P, D])
    gs1 = at("gs1", Z + 39 * K, [P, D])
    cb_hi = at("cb_hi", Z + 47 * K, [P, KT, P], F32R)
    cb_lo = at("cb_lo", Z + 55 * K, [P, KT, P], F32R)
    steps = at("steps", Z + 79 * K, [P, 2 * NH, SEQ])
    lamb = at("lamb", Z + 87 * K, [P, 4, DD])
    lprod = at("lprod", Z + 88 * K, [P, 2, DD])
    lsum = at("lsum", Z + 88.5 * K, [P, 4])
    tabT = at("tabT", Z + 88.75 * K, [8, N_BUCKETS])
    dist = at("dist", Z + 89 * K, [8, LOG_COLS])
    cc = at("cc", Z + 90.5 * K, [P, 3, KT])
    mirror = at("mirror", Z + 115 * K, [P, P])
    proj = at("proj", Z + 15 * K, [P, 10, NT, NB])
    merged = at("merged", Z + 43 * K, [P, NT, D])
    y_hi = at("y_hi", Z + 59 * K, [P, 4, NH, SEQ], F32R)
    y_lo = at("y_lo", Z + 75 * K, [P, 4, NH, SEQ], F32R)
    Bm = at("Bm", Z + 91 * K, [P, 2 * NH, SEQ])
    qkT = at("qkT", Z + 99 * K, [P, 2, NH, SEQ])
    pr = at("pr", Z + 107 * K, [P, NH, LOG_COLS])
    pr2 = at("pr2", Z + 113 * K, [P, NH, LOG_COLS])
    iqT = at("iqT", Z + 113 * K, [IDX_DIM, NH + 1, SEQ])
    ob = at("ob", Z + 113 * K, [P, NT, NH, HD])
    pT = at("pT", Z + 119 * K, [P, NH, LOG_COLS])
    score = at("score", Z + 122.5 * K, [P, LOG_COLS])
    bada = at("bada", Z + 125 * K, [P, 4 * KT])
    modc = at("modc", Z + 125.25 * K, [P, 4 * KT])
    modr = at("modr", Z + 125.5 * K, [KT, P])
    mod_raw = [at(f"mod_raw{i}", o, [P, MOD_W]) for i, o in
               enumerate((Z + 63 * K, Z + 71 * K, Z + 79 * K, Z + 87 * K))]
    mod_raw2 = [at(f"mod_late{i}", Z + (99 + 4 * i) * K, [P, MOD_W]) for i in range(2)]
    acc = zt[:, 1].rearrange("p t n -> p (t n)")
    work = at("work", Z + 119 * K, [P, LOG_COLS])
    selm = at("selm", Z + 121 * K, [P, LOG_COLS])
    x3 = at("x3", Z + 15 * K, [P, NT, D])
    gt1b = at("gt1b", Z + 31 * K, [P, D])
    a_hi = at("a_hi", Z + 59 * K, [P, KT, SEQ], F32R)
    a_lo = at("a_lo", Z + 75 * K, [P, KT, SEQ], F32R)
    gs2 = at("gs2", Z + 91 * K, [P, D])
    sh2b = at("sh2b", Z + 107 * K, [P, D])
    gt2b = at("gt2b", Z + 31 * K, [P, D])
    gnb = at("gnb", Z + 115 * K, [P, D])
    h2 = at("h2", Z + 43 * K, [P, NT, D])

    dist_d = nc.dram_tensor("dist_d", (8, LOG_COLS), F32, kind="Internal")
    mods_d = nc.dram_tensor("mods_d", (4, KT, P), F32, kind="Internal")
    x_v = x_in.rearrange("(t p) d -> p t d", p=P)
    out_v = out.rearrange("(t p) d -> p t d", p=P)

    SMALL_LOADS = 6
    OUT_PARTS = [(t, slice(k * D // 2, (k + 1) * D // 2)) for t in range(NT) for k in range(2)]

    def bcast_rows(ap, n=P):
        return ap.partition_broadcast(n)

    with ExitStack() as ctx:
        def sem(name):
            return ctx.enter_context(nc.semaphore(name))

        ps = ctx.enter_context(nc.psum_tensor("ps", [P, 2, NT, NB], F32))
        aux = ctx.enter_context(nc.psum_tensor("aux", [P, 4, NB], F32))

        loaded = [sem(f"loaded{i}") for i in range(RING)]
        hi_ready = sem("hi_ready")
        lo_ready = sem("lo_ready")
        used = sem("used")
        evacuated = sem("evacuated")
        aux_full = sem("aux_full")
        aux_free = sem("aux_free")
        aux_hi = sem("aux_hi")
        brow_in = [sem("brow_in0"), sem("brow_in1")]
        brow_used = sem("brow_used")
        consts = sem("consts")
        small_in = sem("small_in")
        x_loaded = sem("x_loaded")
        c_ready = sem("c_ready")
        cb_ready = sem("cb_ready")
        sumsq = sem("sumsq")
        root = sem("root")
        var_ready = sem("var_ready")
        h_ready = sem("h_ready")
        mod_in = [sem(f"mod_in{i}") for i in range(4)]
        mod_in2 = [sem(f"mod_late_in{i}") for i in range(2)]
        mod_used = sem("mod_used")
        row_out = sem("row_out")
        c_in = sem("c_in")
        dist_ready = sem("dist_ready")
        dist_out = sem("dist_out")
        steps_in = sem("steps_in")
        bias_full = sem("bias_full")
        bias_turned = sem("bias_turned")
        bm_ready = sem("bm_ready")
        lam_sum = sem("lam_sum")
        lam_exp = sem("lam_exp")
        score_ready = sem("score_ready")
        score_masked = sem("score_masked")
        neg_max = sem("neg_max")
        exps = sem("exps")
        p_ready = sem("p_ready")
        u_ready = sem("u_ready")
        yc_raw = sem("yc_raw")
        yc_hi = sem("yc_hi")
        yc_ready = sem("yc_ready")
        yb_var = sem("yb_var")
        yb_root = sem("yb_root")
        yb_ready = sem("yb_ready")
        f_abs = sem("f_abs")
        f_log = sem("f_log")
        ls_ready = sem("ls_ready")
        dm_ready = sem("dm_ready")
        gate_ready = sem("gate_ready")
        merged_ready = sem("merged_ready")
        x_in_again = sem("x_in_again")
        shift_in = sem("shift_in")
        scale_in = sem("scale_in")
        gate_in = sem("gate_in")
        squared = sem("squared")
        gfin_in = sem("gfin_in")
        gs2_ready = sem("gs2_ready")
        x_added = sem("x_added")
        a_ready = sem("a_ready")
        dve_step = sem("dve_step")
        act_step = sem("act_step")
        pool_step = sem("pool_step")
        y_out = sem("y_out")
        fin_ready = sem("fin_ready")

        block = ctx.enter_context(nc.Block())

        @block.sync
        def _(sp):
            def load(g, slot, first=False):
                if not first:
                    sp.wait_ge(lo_ready, g - RING + 1)
                sp.dma_start(raw[:, slot, :], stream[g]).then_inc(loaded[slot], 16)

            def load_mod(j, k, late=False):
                ring, sems = (mod_raw2, mod_in2) if late else (mod_raw, mod_in)
                if not (isinstance(j, int) and j < len(ring)):
                    sp.wait_ge(mod_used, j - len(ring) + 2)
                sp.dma_start(ring[k][:, :], mod_stream[j]).then_inc(sems[k], 16)

            def load_ahead(g, j, slot0=0, n=UC, late=False):
                k = 0
                for c in range(n):
                    load(g + RING + c, (slot0 + c) % RING)
                    if k < 4 and c == min(2 * k + (2 if late else 0), UC - 1):
                        load_mod(j + k, k % (2 if late else 4), late)
                        k += 1

            for s in range(RING):
                load(s, s, True)
            with sp.Fori(1, (G_WIN + UC) // RING + 1) as i:
                for s in range(RING):
                    load(i * RING + s, s)
            load_ahead(G_WIN + UC, 0)
            with sp.Fori(1, WIN_UNITS - 1) as i:
                load_ahead(G_WIN + UC + UC * i, 4 * i)
            for late, lo, hi in ((False, 0, 4), (True, 4, 8)):
                with sp.Fori(lo, hi) as i:
                    for b in range(2):
                        load_ahead(G_GATE + (2 * i + b) * (UC + BC), 3 * KT + (2 * i + b) * 4, b * (UC + BC),
                                   UC + BC, late)
            with sp.Fori(0, DB) as i:
                load_ahead(G_WO + UC * i, 7 * KT + 4 * i, late=True)
            with sp.Fori(G_FF // RING + 1, CHUNKS // RING) as i:
                for s in range(RING):
                    load(i * RING + s, s)
            for k, (t, col) in enumerate(OUT_PARTS):
                sp.wait_ge(fin_ready, k + 1)
                sp.dma_start(out_v[:, t, col], x3[:, t, col]).then_inc(y_out, 16)
            sp.wait_ge(y_out, 16 * len(OUT_PARTS))

        @block.tensor
        def _(pe):
            def products(dst, acts, kt, t, slot, j, first, last, one_tile=False):
                a_h, a_l = (a[:, kt, 0:P] if one_tile else a[:, kt, t * P:(t + 1) * P] for a in acts)
                wh, wl = (w[:, slot, j * NB:(j + 1) * NB] for w in (w_hi, w_lo))
                pe.matmul(dst, a_h, wh, start=first, stop=False)
                pe.matmul(dst, a_h, wl, start=False, stop=False)
                return pe.matmul(dst, a_l, wh, start=False, stop=last)

            def chunk(v_pair, acts, g, slot, c, n, tiles=NT, one_tile=False):
                pe.wait_ge(lo_ready, g + 1)
                for j in range(CK):
                    kt = c * CK + j
                    for t in range(tiles):
                        mm = products(ps[:, v_pair, t, :], acts, kt, t, slot, j, kt == 0, kt == n * CK - 1,
                                      one_tile)
                mm.then_inc(used, 1)

            def unit(v, pair, acts, g, slot0=0, n=UC, before={}, **kw):
                if not (isinstance(v, int) and v < 2):
                    pe.wait_ge(evacuated, v - 1)
                for c in range(n):
                    for step in before.get(c, ()):
                        step()
                    chunk(pair, acts, g + c, (slot0 + c) % RING, c, n, **kw)

            def pair_of_units(v, p0, acts, g, **kw):
                unit(v, p0, acts, g, **kw)
                unit(v + 1, 1 - p0, acts, g + UC, **kw)

            rounds = [0]

            def open_aux(name, halves=False):
                assert ROUNDS[rounds[0]] == name
                if rounds[0] - halves > 0:
                    pe.wait_ge(aux_free, rounds[0] - halves)
                rounds[0] += 1

            def taken(name):
                pe.wait_ge(aux_free, RND[name] + 1)

            def T(dst, src):
                k, m = src.shape[0], src.shape[1]
                return pe.transpose(dst, src, ident[0:k, 0:k])

            def block_T(src, rnd, n, ready):
                open_aux(f"{rnd}{n}", halves=n > 0)
                pe.wait_ge(*ready)
                v = aux[:, 2 * (n % 2):2 * (n % 2) + 2, :].rearrange("p b (k s) -> p (b k) s", s=SEQ)
                for k in range(4):
                    for t in range(NT):
                        mm = T(v[:, k, t * P:(t + 1) * P], src[:, t, (4 * n + k) * P:(4 * n + k + 1) * P])
                mm.then_inc(aux_full, 1)

            def mod_sum(d):
                open_aux(f"mod{d}")
                pe.wait_ge(mod_used, 1 + KT * (d + 1))
                for k in range(MOD_W // P):
                    mm = pe.matmul(aux[:, 0, k:k + 1], acc[:, k * P:(k + 1) * P], triones[:, SEQ - 1:SEQ],
                                   start=True, stop=True)
                mm.then_inc(aux_full, 1)

            def mod_row(r):
                open_aux(f"row{r}")
                T(aux[0:KT, 0, 0:P], modc[:, KT * r:KT * (r + 1)]).then_inc(aux_full, 1)

            def heads_T(name, first, second):
                open_aux(name)
                v = aux[:, :, :].rearrange("p (q b) (h s) -> p q (b h) s", q=2, s=SEQ)
                for q, slot in enumerate((first, second)):
                    for h in range(NH):
                        for t in range(NT):
                            mm = T(v[:, q, h, t * P:(t + 1) * P], proj[:, slot, t, h * HD:(h + 1) * HD])
                mm.then_inc(aux_full, 1)

            def scores(name, rows_of, keys_of):
                open_aux(name)
                for h in range(NH):
                    q, k = rows_of(h), keys_of(h)
                    pe.matmul(aux[:, h, 0:P], q[:, 0:P], k[:, 0:P], start=True, stop=True)
                    mm = pe.matmul(aux[:, h, P:LOG_COLS], q[:, P:SEQ], k, start=True, stop=True)
                mm.then_inc(aux_full, 1)

            def probs_T(name):
                open_aux(name)
                for h in range(NH):
                    for b in range(3):
                        mm = T(aux[:, h, b * P:(b + 1) * P], pr[:, h, b * P:(b + 1) * P])
                mm.then_inc(aux_full, 1)

            def values_T(name, slot):
                open_aux(name)
                v = aux[:, 0:2, :].rearrange("p b (h s) -> p (b h) s", s=SEQ)
                for h in range(NH):
                    pe.matmul(v[:, h, :], proj[:, slot, 0, h * HD:(h + 1) * HD], pT[:, h, 0:SEQ],
                              start=True, stop=False)
                    mm = pe.matmul(v[:, h, P:SEQ], proj[:, slot, 1, h * HD:(h + 1) * HD], pT[:, h, SEQ:LOG_COLS],
                                   start=False, stop=True)
                mm.then_inc(aux_full, 1)

            cb = (cb_hi, cb_lo)
            hT = (act_hi, act_lo)
            pe.wait_ge(consts, 3)
            pe.wait_ge(cb_ready, 1)
            ada = dict(tiles=1, one_tile=True)
            pair_of_units(0, 0, cb, 0, **ada)
            with pe.Fori(1, 3) as i:
                pair_of_units(2 * i, 0, cb, 2 * UC * i, **ada)
            pe.wait_ge(steps_in, 16)
            for b in range(4):
                mm = pe.matmul(aux[:, b, :], mirror[:, :], steps[:, 2 * b:2 * b + 2, :], start=True, stop=True)
            mm.then_inc(bias_full, 1)
            pe.wait_ge(bias_turned, 1)
            block_T(x1, "h", 0, (h_ready, 1))
            unit(6, 0, cb, 6 * UC, **ada)
            block_T(x1, "h", 1, (h_ready, 2))
            unit(7, 1, cb, 7 * UC, **ada)
            block_T(x1, "h", 2, (h_ready, 3))

            def late_blocks(src, rnd, ready):
                return {0: (lambda: taken(rnd + "0"),),
                        2: (lambda: block_T(src, rnd, 2, ready(2)), lambda: taken(rnd + "1")),
                        4: (lambda: block_T(src, rnd, 3, ready(3)), lambda: taken(rnd + "2")),
                        6: (lambda: taken(rnd + "3"),)}

            unit(V_WIN, 0, hT, G_WIN, before={
                0: (lambda: taken("h0"),), 2: (lambda: taken("h1"),),
                4: (lambda: block_T(x1, "h", 3, (h_ready, 4)), lambda: taken("h2")), 6: (lambda: taken("h3"),)})
            with pe.Fori(0, 2) as i:
                pair_of_units(V_WIN + 1 + 2 * i, 1, hT, G_WIN + UC + 2 * UC * i)

            def idx_T():
                open_aux("idx_T")
                vi = aux[0:IDX_DIM, :, :].rearrange("p b (k s) -> p (b k) s", s=SEQ)
                for h in range(NH + 1):
                    for t in range(NT):
                        mm = T(vi[:, h, t * P:(t + 1) * P], proj[:, MISC, t, h * IDX_DIM:(h + 1) * IDX_DIM])
                mm.then_inc(aux_full, 1)

            def idx_dots():
                scores("idx_dots", lambda h: iqT[:, h, :], lambda h: iqT[:, NH, :])

            def qk_dots(name):
                scores(name, lambda h: qkT[:, 0, h, :], lambda h: qkT[:, 1, h, :])

            def diff_dots(half):
                lo = half * DD
                scores(f"B_dots{half}", lambda h: qkT[lo:lo + DD, 0, h, :], lambda h: qkT[lo:lo + DD, 1, h, :])

            def weights_T(name, n):
                pe.wait_ge(p_ready, n)
                probs_T(name)

            def conv_T():
                pe.wait_ge(u_ready, 1)
                heads_T("C_T", CG, BG)

            def diff_values():
                open_aux("B_o")
                vo = aux[:, 0:2, :].rearrange("p t (h d) -> p t h d", h=NH)
                for h in range(NH):
                    v0, v1 = (proj[:, VB, t, h * HD:(h + 1) * HD] for t in range(NT))
                    pe.matmul(vo[:, 0, h, :], pT[:, h, 0:P], v0, start=True, stop=True)
                    pe.matmul(vo[:, 1, h, :], pT[:, h, P:SEQ], v0, start=True, stop=False)
                    mm = pe.matmul(vo[:, 1, h, :], pT[:, h, SEQ:LOG_COLS], v1, start=False, stop=True)
                mm.then_inc(aux_full, 1)

            def forget_T():
                pe.wait_ge(evacuated, V_WIN + 12)
                heads_T("D_qk", QD, KD)

            def forget_sums():
                pe.wait_ge(ls_ready, 1)
                open_aux("D_sums")
                vf = aux[:, 0:2, :].rearrange("p b (h s) -> p (b h) s", s=SEQ)
                for h in range(NH):
                    pe.matmul(vf[:, h, :], lsig[:, 0, h:h + 1].to_broadcast([P, P]), triones[:, :],
                              start=True, stop=False)
                    pe.matmul(vf[:, h, P:SEQ], lsig[:, 1, h:h + 1].to_broadcast([P, P]), triones[:, 0:P],
                              start=False, stop=True)
                pe.matmul(aux[:, 2, 0:NH], triones[:, 0:P], lsig[:, 0, :], start=True, stop=True)
                pe.matmul(aux[:, 2, NH:2 * NH], triones[:, P:SEQ], lsig[:, 0, :], start=True, stop=False)
                pe.matmul(aux[:, 2, NH:2 * NH], triones[:, 0:P], lsig[:, 1, :], start=False, stop=True)\
                    .then_inc(aux_full, 1)

            mixer_steps = {
                5: {0: (idx_T,), 1: (lambda: mod_sum(0),), 3: (idx_dots,), 5: (lambda: heads_T("A_qk", QA, KA),)},
                7: {0: (lambda: qk_dots("A_dots"),), 2: (lambda: heads_T("B_qk", QB, KB),)},
                8: {0: (lambda: weights_T("A_pT", 1),), 2: (lambda: values_T("A_y", VA),),
                    4: (lambda: diff_dots(0),), 6: (lambda: diff_dots(1),)},
                9: {1: (lambda: mod_sum(1),), 2: (lambda: mod_row(0),), 6: (lambda: weights_T("B_pT", 2),)},
                10: {1: (conv_T,), 4: (diff_values,)},
                12: {1: (forget_T,), 3: (forget_sums,), 5: (lambda: qk_dots("D_dots"),)},
            }
            for u in range(5, WIN_UNITS):
                unit(V_WIN + u, u % 2, hT, G_WIN + u * UC, before=mixer_steps.get(u, {}))
            mod_sum(2)

            def gate_stage(m):
                yT = (y_hi[:, MIXERS[m]], y_lo[:, MIXERS[m]])
                g0, v0 = G_GATE + m * DB * (UC + BC), V_GATE + m * 2 * DB
                with pe.Fori(0, DB // 2) as i:
                    for b in range(2):
                        g = g0 + (2 * i + b) * (UC + BC)
                        v = v0 + 2 * (2 * i + b)
                        unit(v, 1, hT, g, slot0=b * (UC + BC))
                        if b == 0:
                            if m == 0:
                                pe.wait_ge(yc_ready, 1)
                            else:
                                taken({1: "A_y", 2: "B_y", 3: "D_y"}[m])
                        unit(v + 1, 0, yT, g + UC, slot0=b * (UC + BC) + UC, n=BC)

            gate_stage(0)
            weights_T("D_pT", 3)
            mod_sum(3)
            mod_row(1)
            gate_stage(1)
            pe.wait_ge(yb_ready, 1)
            open_aux("B_y")
            vb = aux[:, 0:2, :].rearrange("p b (h s) -> p (b h) s", s=SEQ)
            for h in range(NH):
                for t in range(NT):
                    mm = T(vb[:, h, t * P:(t + 1) * P], ob[:, t, h, :])
            mm.then_inc(aux_full, 1)
            mod_sum(4)
            gate_stage(2)
            values_T("D_y", VD)
            mod_sum(5)
            mod_row(2)
            gate_stage(3)
            mod_sum(6)

            merged_of = lambda n: (merged_ready, 2 * DB + n + 1)
            for n in range(2):
                block_T(merged, "m", n, merged_of(n))
            unit(V_WO, 1, hT, G_WO, before=late_blocks(merged, "m", merged_of))
            unit(V_WO + 1, 0, hT, G_WO + UC)
            pair_of_units(V_WO + 2, 1, hT, G_WO + 2 * UC)
            mod_sum(7)
            mod_row(3)
            normed = lambda n: (h_ready, DB + n + 1)
            for n in range(2):
                block_T(h2, "n", n, normed(n))
            late_h2 = late_blocks(h2, "n", normed)

            def hidden_T(q, j):
                pe.wait_ge(aux_free, len(ROUNDS) + 4 * q + j)
                pe.wait_ge(a_ready, 4 * q + j + 1)
                for k in range(4):
                    for t in range(NT):
                        mm = T(vb[:, k, t * P:(t + 1) * P], zt[:, j % 2, t, k * P:(k + 1) * P])
                mm.then_inc(aux_full, 1)

            aT = (a_hi, a_lo)

            def group(q, first=False):
                v, g = V_FF + 2 * DB * q, G_FF + 2 * DB * UC * q
                for j in range(DB):
                    before = {3: (lambda: hidden_T(q, j - 1),)} if j else late_h2 if first else {}
                    unit(v + j, (1 + j) % 2, hT, g + j * UC, before=before)
                v, g = v + DB, g + DB * UC
                stands = lambda n: pe.wait_ge(aux_free, len(ROUNDS) + 4 * q + n)
                for j in range(DB):
                    before = {} if j else {0: (lambda: stands(3),), 3: (lambda: hidden_T(q, DB - 1),),
                                           6: (lambda: stands(4),)}
                    unit(v + j, (1 + j) % 2, aT, g + j * UC, before=before)

            group(0, True)
            with pe.Fori(1, FF_GROUPS) as q:
                group(q)

        @block.scalar
        def _(act):
            link = Links(act, act_step)

            def split(g, slot):
                act.wait_ge(loaded[slot], (g - slot) * 4 + 16)
                if not (isinstance(g, int) and g < RING):
                    act.wait_ge(used, g - RING + 1)
                act.activation(w_hi[:, slot, :], raw[:, slot, :], ACT.Copy).then_inc(hi_ready, 1)

            def ahead(g, slot0=0, n=UC, before={}, last=False):
                for c in range(n):
                    for step in before.get(c, ()):
                        step()
                    if not (last and c >= n - RING):
                        split(g + RING + c, (slot0 + c) % RING)

            act.dma_start(cc[:, 0, :], c_cols).then_inc(c_in, 16)
            act.dma_start(x1[:, :, :], x_v).then_inc(x_loaded, 16)
            act.dma_start(gs1[:, :], bcast_rows(g_norm1[0:1, :])).then_inc(x_loaded, 16)
            act.wait_ge(c_in, 16)
            act.activation(cc[:, 1, :], cc[:, 0, :], ACT.Sigmoid).then_inc(c_ready, 1)
            for s in range(RING):
                split(s, s)
            act.wait_ge(lam_sum, 1)
            act.activation(lsum[:, 2:4], lsum[:, 0:2], ACT.Exp).then_inc(lam_exp, 1)
            ahead(0)
            act.wait_ge(x_loaded, 32)
            for t in range(NT):
                if t:
                    act.wait_ge(sumsq, t)
                act.activation(sq_junk[:, :], x1[:, t, :], ACT.Square, accum_out=ss[:, t:t + 1]).then_inc(sumsq, 1)
            act.wait_ge(var_ready, 1)
            act.activation(rstd[:, :], ss[:, :], ACT.Sqrt).then_inc(root, 1)
            ahead(UC)
            with act.Fori(1, 3) as i:
                for b in range(2):
                    ahead((2 * i + b) * UC)

            auxw = aux[:, :, :].rearrange("p b n -> p (b n)")
            aux8 = aux[:, :, :].rearrange("p b (k s) -> p (b k) s", s=SEQ)
            aux4 = aux[:, 0:2, :].rearrange("p b (h s) -> p (b h) s", s=SEQ)

            def hi_from_aux(dst, src, name):
                act.wait_ge(aux_full, RND[name] + 1)
                act.activation(dst, src, ACT.Copy).then_inc(aux_hi, 1)

            def block_hi(rnd, n):
                hi_from_aux(act_hi[:, 4 * n:4 * n + 4, :], aux8[:, 4 * (n % 2):4 * (n % 2) + 4, :], f"{rnd}{n}")

            def take_aux(dst, src, name, func=ACT.Copy):
                act.wait_ge(aux_full, RND[name] + 1)
                act.activation(dst, src, func).then_inc(aux_free, 1)

            def take_qk(name):
                take_aux(qkT[:, :, :, :].rearrange("p q h s -> p (q h s)"), auxw, name)

            def take_pT(name):
                take_aux(pT[:, :, :], aux[:, :, 0:LOG_COLS], name)

            def take_row(r):
                if r:
                    act.wait_ge(row_out, 16 * r)
                take_aux(modr[:, :], aux[0:KT, 0, 0:P], f"row{r}")
                act.wait_ge(aux_free, RND[f"row{r}"] + 1)
                act.dma_start(mods_d.ap()[r], modr[:, :]).then_inc(row_out, 16)

            def exps_of(buf, c, n, heads):
                act.wait_ge(neg_max, n)
                for h in heads:
                    for t, (c0, c1) in enumerate(((0, P), (P, LOG_COLS))):
                        act.activation(buf[:, h, c0:c1], buf[:, h, c0:c1], ACT.Exp, bias=nmax[:, c, t, h:h + 1],
                                       accum_out=esum[:, c, t, h:h + 1]).then_inc(exps, 1)

            act.wait_ge(bias_full, 1)
            act.activation(Bm[:, :, :], aux8, ACT.Copy).then_inc(bias_turned, 1)
            block_hi("h", 0)
            ahead(6 * UC)
            block_hi("h", 1)
            ahead(7 * UC)
            block_hi("h", 2)

            def log_f():
                act.wait_ge(f_abs, 1)
                link(act.activation(lsig2[:, :, :], lsig2[:, :, :], ACT.Exp, scale=-1.0))
                act.activation(lsig2[:, :, :], lsig2[:, :, :], ACT.Ln, bias=1.0).then_inc(f_log, 1)

            def conv_hi():
                act.wait_ge(yc_raw, 1)
                act.activation(y_hi[:, 2, :, :], pr[:, :, 0:SEQ], ACT.Copy).then_inc(yc_hi, 1)

            def norm_root():
                act.wait_ge(yb_var, 1)
                act.activation(rec[:, 1, :, :], rec[:, 0, :, :], ACT.Sqrt).then_inc(yb_root, 1)

            G = G_WIN
            ahead(G, before={4: (lambda: block_hi("h", 3),)})
            with act.Fori(0, 2) as i:
                for b in range(2):
                    ahead(G + UC + (2 * i + b) * UC)
            first, second = (0, 1), (2, 3)
            mixer_steps = {
                5: {0: (lambda: take_aux(iqT[:, :, :], aux8[0:IDX_DIM, 0:NH + 1, :], "idx_T"),),
                    3: (lambda: take_aux(pr[:, :, :], aux[:, :, 0:LOG_COLS], "idx_dots", ACT.Relu),),
                    5: (lambda: take_qk("A_qk"),)},
                6: {0: (log_f,)},
                7: {2: (lambda: take_qk("B_qk"),), 3: (lambda: exps_of(pr, 0, 1, first),),
                    5: (lambda: exps_of(pr, 0, 1, second),)},
                8: {0: (lambda: take_pT("A_pT"),), 2: (lambda: hi_from_aux(y_hi[:, 0, :, :], aux4, "A_y"),),
                    5: (lambda: exps_of(pr, 0, 2, first),), 7: (lambda: exps_of(pr, 0, 2, second),)},
                9: {0: (lambda: exps_of(pr2, 1, 3, first),), 1: (lambda: exps_of(pr2, 1, 3, second),),
                    2: (lambda: take_row(0),), 6: (lambda: take_pT("B_pT"),)},
                10: {1: (lambda: take_qk("C_T"),),
                     4: (lambda: take_aux(ob[:, :, :, :].rearrange("p t h d -> p (t h d)"), auxw[:, 0:NT * NB],
                                          "B_o"),), 7: (norm_root,)},
                11: {2: (conv_hi,)},
                12: {1: (lambda: take_qk("D_qk"),)},
            }
            for u in range(5, WIN_UNITS):
                ahead(G + u * UC, before=mixer_steps.get(u, {}))
                act.wait_ge(used, G + (u + 1) * UC)
                act.wait_ge(evacuated, V_WIN + u)
                act.activation(proj[:, (0, QA, KA, VA, QB, KB, VB, BG, CG, XIN, QD, KD, VD)[u]], ps[:, u % 2],
                               ACT.Copy).then_inc(evacuated, 1)
            exps_of(pr, 0, 4, range(NH))

            def gate_stage(m):
                g0 = G_GATE + m * DB * (UC + BC)
                with act.Fori(0, DB // 2) as i:
                    for b in range(2):
                        g, s = g0 + (2 * i + b) * (UC + BC), b * (UC + BC)
                        ahead(g, s)
                        act.wait_ge(evacuated, V_GATE + 2 * (m * DB + 2 * i + b) + 1)
                        act.activation(zt[:, 0], zt[:, 0], ACT.Sigmoid).then_inc(gate_ready, 1)
                        ahead(g + UC, s + UC, BC)

            gate_stage(0)
            take_pT("D_pT")
            take_row(1)
            gate_stage(1)
            hi_from_aux(y_hi[:, 1, :, :], aux4, "B_y")
            gate_stage(2)
            hi_from_aux(y_hi[:, 3, :, :], aux4, "D_y")
            take_row(2)
            gate_stage(3)
            for n in range(2):
                block_hi("m", n)

            def squares(n, added):
                act.wait_ge(x_added, added)
                for t in range(NT):
                    sq = act.activation(h2[:, t, n * NB:(n + 1) * NB], x3[:, t, n * NB:(n + 1) * NB], ACT.Square,
                                        accum_out=ss4[:, t, n:n + 1])
                sq.then_inc(squared, 1)

            def norm_root_of(n):
                act.wait_ge(var_ready, n)
                act.activation(rstd[:, :], ss[:, :], ACT.Sqrt).then_inc(root, 1)

            def late_hi(rnd):
                return {2: (lambda: block_hi(rnd, 2),), 4: (lambda: block_hi(rnd, 3),)}

            for n in range(DB):
                ahead(G_WO + n * UC, before={} if n else late_hi("m"))
                squares(n, n + 1)
            take_row(3)
            norm_root_of(2)
            for n in range(2):
                block_hi("n", n)

            def square(q, j):
                act.wait_ge(evacuated, V_FF + 2 * DB * q + j + 1)
                act.activation(zt[:, j % 2], zt[:, j % 2], ACT.Square).then_inc(a_ready, 1)

            def hidden_hi(q, j):
                act.wait_ge(aux_full, len(ROUNDS) + 4 * q + j + 1)
                act.activation(a_hi[:, 4 * j:4 * j + 4, :], aux4, ACT.Copy).then_inc(aux_hi, 1)

            def ff_group(q, start=False, last=False):
                g = G_FF + 2 * DB * UC * q
                for j in range(DB):
                    ahead(g + j * UC, before={3: (lambda: hidden_hi(q, j - 1),)} if j else
                          late_hi("n") if start else {})
                    square(q, j)
                g = g + DB * UC
                for j in range(DB):
                    ahead(g + j * UC, before={} if j else {3: (lambda: hidden_hi(q, DB - 1),)},
                          last=last and j == DB - 1)
                    if last:
                        squares(j, DB * FF_GROUPS + j + 1)

            ff_group(0, start=True)
            with act.Fori(1, FF_GROUPS - 1) as q:
                ff_group(q)
            ff_group(FF_GROUPS - 1, last=True)
            norm_root_of(3)

        @block.vector
        def _(dve):
            link = Links(dve, dve_step)

            def split(g, slot):
                dve.wait_ge(hi_ready, g + 1)
                dve.tensor_tensor(w_lo[:, slot, :], raw[:, slot, :], w_hi[:, slot, :].bitcast(F32), ALU.subtract)\
                    .then_inc(lo_ready, 1)

            def ahead(g, slot0=0, n=UC, before={}, after={}, last=False):
                for c in range(n):
                    for step in before.get(c, ()):
                        step()
                    if not (last and c >= n - RING):
                        split(g + RING + c, (slot0 + c) % RING)
                    for step in after.get(c, ()):
                        step()

            def mod_step(j, kt, k, late=False):
                ring, sems = (mod_raw2, mod_in2) if late else (mod_raw, mod_in)
                nth = j - k - (5 * KT if late else 0)
                dve.wait_ge(sems[k], nth * (16 // len(ring)) + 16)
                dve.wait_ge(mod_used, j + 1)
                dve.scalar_tensor_tensor(acc, ring[k][:, :], csil[:, bass.ds(kt, 1)], acc, ALU.mult, ALU.add)\
                    .then_inc(mod_used, 1)

            def mod_steps(j, kt, late=False):
                return {2 * k + 1: (lambda k=k: mod_step(j + k, kt + k, k % (2 if late else 4), late),)
                        for k in range(4)}

            def take_mod(d):
                dve.wait_ge(aux_full, RND[f"mod{d}"] + 1)
                n = MOD_W // P
                dve.tensor_tensor(modc[:, n * d:n * (d + 1)], aux[:, 0, 0:n], bada[:, n * d:n * (d + 1)], ALU.add)\
                    .then_inc(aux_free, 1)
                if d < MOD_BLOCKS - 1:
                    link(dve.memset(acc, 0.0))

            def lo_from_aux(dst, src, hi, name):
                dve.wait_ge(aux_hi, HI_ROUNDS.index(name) + 1)
                dve.tensor_tensor(dst, src, hi.bitcast(F32), ALU.subtract).then_inc(aux_free, 1)

            aux8 = aux[:, :, :].rearrange("p b (k s) -> p (b k) s", s=SEQ)
            aux4 = aux[:, 0:2, :].rearrange("p b (h s) -> p (b h) s", s=SEQ)

            def block_lo(rnd, n):
                lo_from_aux(act_lo[:, 4 * n:4 * n + 4, :], aux8[:, 4 * (n % 2):4 * (n % 2) + 4, :],
                            act_hi[:, 4 * n:4 * n + 4, :], f"{rnd}{n}")

            def wide(ap, n):
                return ap.unsqueeze(1).to_broadcast([P, n, ap.shape[1]])

            dve.wait_ge(c_ready, 1)
            link(dve.tensor_tensor(csil[:, :], cc[:, 0, :], cc[:, 1, :], ALU.mult))
            cw = csil[:, :].unsqueeze(2).to_broadcast([P, KT, P])
            link(dve.tensor_copy(cb_hi[:, :, :], cw))
            dve.tensor_tensor(cb_lo[:, :, :], cw, cb_hi[:, :, :].bitcast(F32), ALU.subtract).then_inc(cb_ready, 1)
            for s in range(RING):
                split(s, s)
            dve.wait_ge(small_in, 16 * SMALL_LOADS)
            link(dve.tensor_tensor(lprod[:, :, :], lamb[:, 0:4:2, :], lamb[:, 1:4:2, :], ALU.mult))
            dve.tensor_reduce(lsum[:, 0:2], lprod[:, :, :], AX_X, ALU.add).then_inc(lam_sum, 1)
            for b, n0, n1 in t5_runs():
                link.step(dve.tensor_copy(dist[:, SEQ - n1:SEQ - n0], tabT[:, b:b + 1].to_broadcast([8, n1 - n0])))
            link(dve.tensor_copy(dist[:, SEQ:LOG_COLS], tabT[:, 0:1].to_broadcast([8, LOG_COLS - SEQ])))
            dve.tensor_scalar(gsub[:, :], gsub[:, :], 1.0 - LAM_INIT, None, ALU.mult).then_inc(dist_ready, 1)
            dve.wait_ge(lam_exp, 1)
            link(dve.tensor_tensor(nlam[:, :], lsum[:, 3:4], lsum[:, 2:3], ALU.subtract))
            link(dve.tensor_scalar(nlam[:, :], nlam[:, :], -LAM_INIT, None, ALU.add))

            def variance(n):
                dve.tensor_scalar(ss[:, :], ss[:, :], 1.0 / D, EPS, ALU.mult, ALU.add).then_inc(var_ready, 1)
                dve.wait_ge(root, n)
                link(dve.reciprocal(rstd[:, :], rstd[:, :]))

            def evac_begin(v_end):
                dve.wait_ge(used, v_end)

            def norm_block(dst, src, n, scale, shift):
                col = slice(n * NB, (n + 1) * NB)
                for t in range(NT):
                    link.step(dve.scalar_tensor_tensor(dst[:, t, col], src[:, t, col], rstd[:, t:t + 1],
                                                       scale[:, col], ALU.mult, ALU.mult))
                link.wait()
                dve.tensor_tensor(dst[:, :, col], dst[:, :, col], wide(shift[:, col], NT), ALU.add)\
                    .then_inc(h_ready, 1)

            def ada_evac(u, dst, i):
                b = u % 2 if isinstance(u, int) else None
                dve.wait_ge(brow_in[b], 16 * i + 16)
                dve.tensor_tensor(dst, ps[:, b, 0, :], brow[:, b, :], ALU.add).then_inc(evacuated, 1)

            for u in range(DB):
                ahead(u * UC)
                if u == 0:
                    dve.wait_ge(sumsq, NT)
                    variance(1)
                evac_begin((u + 1) * UC)
                ada_evac(u, sh1[:, u * NB:(u + 1) * NB], u // 2)
            dve.wait_ge(x_loaded, 32)
            dve.memset(acc, 0.0).then_inc(mod_used, 1)
            for n in range(DB):
                u = DB + n
                ahead(u * UC)
                evac_begin((u + 1) * UC)
                ada_evac(u, zt[:, 0, 0, :], u // 2)
                dve.wait_ge(evacuated, u + 1)
                col = slice(n * NB, (n + 1) * NB)
                link(dve.scalar_tensor_tensor(gs1[:, col], zt[:, 0, 0, :], 1.0, gs1[:, col], ALU.add, ALU.mult))
                norm_block(x1, x1, n, gs1, sh1)
                if n:
                    block_lo("h", n - 1)

            def softmax_max(buf, c):
                link.step(dve.tensor_reduce(nmax[:, c, 0, :], buf[:, :, 0:P], AX_X, ALU.max, negate=True))
                dve.tensor_reduce(nmax[:, c, 1, :], buf[:, :, P:LOG_COLS], AX_X, ALU.max, negate=True)\
                    .then_inc(neg_max, 1)

            def weigh(buf, r, last=None):
                for t, (c0, c1) in enumerate(((0, P), (P, LOG_COLS))):
                    f = r[:, t, :].unsqueeze(2).to_broadcast([P, NH, c1 - c0])
                    ins = dve.tensor_tensor(buf[:, :, c0:c1], buf[:, :, c0:c1], f, ALU.mult)
                    if t == 0 or last is None:
                        link.step(ins)
                if last is not None:
                    ins.then_inc(last, 1)

            def logits(buf, scale, head0, name):
                dve.wait_ge(aux_full, RND[name] + 1)
                link.step(dve.scalar_tensor_tensor(buf[:, :, 0:P], aux[:, :, 0:P], scale,
                                                   Bm[:, head0:head0 + NH, P:SEQ], ALU.mult, ALU.add))
                dve.scalar_tensor_tensor(buf[:, :, P:LOG_COLS], aux[:, :, P:LOG_COLS], scale,
                                         Bm[:, head0:head0 + NH, :], ALU.mult, ALU.add).then_inc(aux_free, 1)
                link.wait()
                dve.wait_ge(aux_free, RND[name] + 1)

            ahead(G_WIN, before={4: (lambda: block_lo("h", 3),)})
            evac_begin(G_WIN + UC)
            dve.tensor_scalar(proj[:, MISC], ps[:, 0], 1.0, None, ALU.mult).then_inc(evacuated, 1)
            with dve.Fori(0, 2) as i:
                for b in range(2):
                    g = G_WIN + UC + (2 * i + b) * UC
                    ahead(g, after=mod_steps(8 * i + 4 * b, 8 * i + 4 * b))
                    evac_begin(g + UC)
                    dve.tensor_scalar(proj[:, 1 + 2 * i + b], ps[:, 1 - b], 1.0, None, ALU.mult)\
                        .then_inc(evacuated, 1)
            spans = ((0, P), (P, LOG_COLS))

            def small_inputs():
                dve.wait_ge(evacuated, V_WIN + 1)
                link(dve.tensor_scalar(iws[:, :, :], proj[:, MISC, :, IW0:IW0 + NH], IDX_SCALE, None, ALU.mult))
                link(dve.tensor_tensor(lsig[:, :, :], proj[:, MISC, :, FD0:FD0 + NH], wide(bf[:, :], NT), ALU.add))
                link(dve.tensor_scalar(lsig2[:, :, :], lsig[:, :, :], -1.0, None, ALU.mult))
                dve.tensor_tensor(lsig2[:, :, :], lsig2[:, :, :], lsig[:, :, :], ALU.max).then_inc(f_abs, 1)

            def index_scores():
                dve.wait_ge(aux_free, RND["idx_dots"] + 1)
                for t, (c0, c1) in enumerate(spans):
                    link.step(dve.tensor_scalar(score[:, c0:c1], pr[:, 0, c0:c1], iws[:, t, 0:1], 0.0,
                                                ALU.mult, ALU.add))
                link.wait()
                for h in range(1, NH):
                    for t, (c0, c1) in enumerate(spans):
                        ins = dve.scalar_tensor_tensor(score[:, c0:c1], pr[:, h, c0:c1], iws[:, t, h:h + 1],
                                                       score[:, c0:c1], ALU.mult, ALU.add)
                        if h < NH - 1 or t == 0:
                            link.step(ins)
                        else:
                            ins.then_inc(score_ready, 1)
                    link.wait()

            def top8(r):
                if r == 0:
                    dve.wait_ge(score_masked, 1)
                src = score if r == 0 else work
                for t, (c0, c1) in enumerate(spans):
                    link.step(dve.max(m8[:, t, :], src[:, c0:c1]))
                link.wait()
                for t, (c0, c1) in enumerate(spans):
                    link.step(dve.match_replace(work[:, c0:c1], m8[:, t, :], src[:, c0:c1], TAKEN))
                link.wait()

            def select():
                link(dve.tensor_scalar(selm[:, :], work[:, :], TAKEN / 2, NEG, ALU.is_gt, ALU.mult))

            def sparse_logits():
                dve.wait_ge(bm_ready, 1)
                logits(pr, HD ** -0.5, 0, "A_dots")
                for t, (c0, c1) in enumerate(spans):
                    link.step(dve.tensor_tensor(pr[:, :, c0:c1], pr[:, :, c0:c1],
                                                selm[:, c0:c1].unsqueeze(1).to_broadcast([P, NH, c1 - c0]), ALU.add))
                link.wait()
                softmax_max(pr, 0)

            def softmax_end(n):
                dve.wait_ge(exps, n * NT * NH)
                link(dve.reciprocal(rec[:, 0, :, :], esum[:, 0, :, :]))
                weigh(pr, rec[:, 0], p_ready)

            def log_forget():
                dve.wait_ge(f_log, 1)
                link(dve.tensor_scalar(lsig[:, :, :], lsig[:, :, :], 0.0, None, ALU.min))
                dve.tensor_tensor(lsig[:, :, :], lsig[:, :, :], lsig2[:, :, :], ALU.subtract).then_inc(ls_ready, 1)

            def diff_logits(c, buf):
                logits(buf, DD ** -0.5, NH, f"B_dots{c}")
                softmax_max(buf, c)

            def diff_weights0():
                dve.wait_ge(exps, 2 * NT * NH)
                link(dve.reciprocal(rec[:, 0, :, :], esum[:, 0, :, :]))
                weigh(pr, rec[:, 0])

            def diff_weights1():
                dve.wait_ge(exps, 3 * NT * NH)
                link(dve.reciprocal(rec[:, 1, :, :], esum[:, 1, :, :]))
                link(dve.tensor_scalar(rec[:, 1, :, :], rec[:, 1, :, :], nlam[:, 0:1], None, ALU.mult))
                weigh(pr2, rec[:, 1])
                link.wait()
                dve.tensor_tensor(pr[:, :, :], pr[:, :, :], pr2[:, :, :], ALU.add).then_inc(p_ready, 1)

            def diff_norm():
                dve.wait_ge(aux_free, RND["B_o"] + 1)
                sq = zt[:, 0].rearrange("p t (h d) -> p t h d", h=NH)
                link(dve.tensor_tensor(sq, ob[:, :, :, :], ob[:, :, :, :], ALU.mult))
                link(dve.tensor_reduce(rec[:, 0, :, :], sq, AX_X, ALU.add))
                dve.tensor_scalar(rec[:, 0, :, :], rec[:, 0, :, :], 1.0 / HD, EPS, ALU.mult, ALU.add)\
                    .then_inc(yb_var, 1)

            def diff_scale():
                dve.wait_ge(yb_root, 1)
                link(dve.reciprocal(rec[:, 1, :, :], rec[:, 1, :, :]))
                obv = ob[:, :, :, :].rearrange("p t h d -> p (t h) d")
                rv = rec[:, 1, :, :].rearrange("p t h -> p (t h)")
                link(dve.tensor_tensor(obv, obv, rv.unsqueeze(2).to_broadcast([P, NT * NH, HD]), ALU.mult))
                dve.tensor_tensor(obv, obv, wide(gsub[:, :], NT * NH), ALU.mult).then_inc(yb_ready, 1)

            def conv_input():
                dve.wait_ge(evacuated, V_WIN + 10)
                dve.tensor_tensor(proj[:, CG], proj[:, CG], proj[:, XIN], ALU.mult).then_inc(u_ready, 1)

            def conv_tap(d):
                if d == 0:
                    dve.wait_ge(aux_free, RND["C_T"] + 1)
                for k in range(NH):
                    if d == 0:
                        ins = dve.tensor_scalar(pr[:, k, 0:SEQ], qkT[:, 0, k, :], convw[:, k, 2:3], None, ALU.mult)
                    else:
                        ins = dve.scalar_tensor_tensor(pr[:, k, d:SEQ], qkT[:, 0, k, 0:SEQ - d],
                                                       convw[:, k, 2 - d:3 - d], pr[:, k, d:SEQ], ALU.mult, ALU.add)
                    link.step(ins)
                link.wait()

            def conv_end():
                dve.tensor_tensor(pr[:, :, 0:SEQ], pr[:, :, 0:SEQ], qkT[:, 1, :, :], ALU.mult).then_inc(yc_raw, 1)

            def conv_lo():
                dve.wait_ge(yc_hi, 1)
                dve.tensor_tensor(y_lo[:, 2, :, :], pr[:, :, 0:SEQ], y_hi[:, 2, :, :].bitcast(F32), ALU.subtract)\
                    .then_inc(yc_ready, 1)

            def forget_terms():
                dve.wait_ge(aux_full, RND["D_sums"] + 1)
                link(dve.tensor_scalar(Ftok[:, :, :].rearrange("p t h -> p (t h)"), aux[:, 2, 0:2 * NH], 1.0, None,
                                       ALU.mult))
                for h in range(NH):
                    for t, (c0, c1) in enumerate(spans):
                        ins = dve.tensor_scalar(pr[:, h, c0:c1], aux4[:, h, 0:c1 - c0], -1.0, Ftok[:, t, h:h + 1],
                                                ALU.mult, ALU.add)
                        if (h, t) == (NH - 1, 1):
                            ins.then_inc(aux_free, 1)
                        else:
                            link.step(ins)

            def forget_logits():
                link.wait()
                dve.wait_ge(aux_free, RND["D_sums"] + 1)
                dve.wait_ge(dm_ready, 1)
                dve.wait_ge(aux_full, RND["D_dots"] + 1)
                link.step(dve.scalar_tensor_tensor(pr[:, :, 0:P], aux[:, :, 0:P], HD ** -0.5, pr[:, :, 0:P],
                                                   ALU.mult, ALU.add))
                dve.scalar_tensor_tensor(pr[:, :, P:LOG_COLS], aux[:, :, P:LOG_COLS], HD ** -0.5,
                                         pr[:, :, P:LOG_COLS], ALU.mult, ALU.add).then_inc(aux_free, 1)
                link.wait()
                dve.wait_ge(aux_free, RND["D_dots"] + 1)
                softmax_max(pr, 0)

            mixer_steps = {
                5: {0: (small_inputs,), 1: (lambda: take_mod(0),), 4: (index_scores,), 6: (lambda: top8(0),),
                    7: (lambda: top8(1),)},
                6: {**{c: (lambda c=c: top8(c + 2),) for c in range(6)}, 6: (select,)},
                7: {0: (sparse_logits,), 7: (lambda: softmax_end(1),)},
                8: {1: (log_forget,), 2: (lambda: lo_from_aux(y_lo[:, 0, :, :], aux4, y_hi[:, 0, :, :], "A_y"),),
                    4: (lambda: diff_logits(0, pr),), 6: (lambda: diff_logits(1, pr2),)},
                9: {1: (lambda: take_mod(1),), 3: (diff_weights0,), 4: (diff_weights1,)},
                10: {0: (conv_input,), 2: (lambda: conv_tap(0),), 3: (lambda: conv_tap(1),),
                     4: (lambda: conv_tap(2), conv_end), 6: (diff_norm,)},
                11: {1: (diff_scale,), 3: (conv_lo,)},
                12: {3: (forget_terms,), 6: (forget_logits,)},
            }
            for u in range(5, WIN_UNITS):
                ahead(G_WIN + u * UC, before=mixer_steps[u], after=mod_steps(4 * (u - 1), 4 * (u - 1) % KT))
            take_mod(2)
            softmax_end(4)
            dve.wait_ge(evacuated, V_GATE)

            def gate_stage(m):
                g0 = G_GATE + m * DB * (UC + BC)
                with dve.Fori(0, DB // 2) as i:
                    for b in range(2):
                        n = 2 * i + b
                        g, s = g0 + n * (UC + BC), b * (UC + BC)
                        ahead(g, s, after=mod_steps(3 * KT + 4 * (m * DB + n), 8 * i + 4 * b, m > 1))
                        evac_begin(g + UC)
                        dve.wait_ge(brow_in[b], (ADA_UNITS + m * DB) * 8 + 16 * i + 16)
                        dve.tensor_tensor(zt[:, 0], ps[:, 1], wide(brow[:, b, :], NT), ALU.add).then_inc(evacuated, 1)
                        ahead(g + UC, s + UC, BC)
                        evac_begin(g + UC + BC)
                        dve.wait_ge(gate_ready, m * DB + n + 1)
                        col = bass.ts(n, NB)
                        if m == 0:
                            dve.tensor_tensor(merged[:, :, col], ps[:, 0], zt[:, 0], ALU.mult).then_inc(evacuated, 1)
                        else:
                            dve.tensor_tensor(zt[:, 0], ps[:, 0], zt[:, 0], ALU.mult).then_inc(evacuated, 1)
                            dve.wait_ge(evacuated, V_GATE + 2 * (m * DB + n) + 2)
                            if m > 1:
                                dve.wait_ge(merged_ready, (m - 2) * DB + n + 1)
                            dve.tensor_tensor(merged[:, :, col], merged[:, :, col], zt[:, 0], ALU.add)\
                                .then_inc(merged_ready, 1)

            gate_stage(0)
            take_mod(3)
            gate_stage(1)
            lo_from_aux(y_lo[:, 1, :, :], aux4, y_hi[:, 1, :, :], "B_y")
            take_mod(4)
            gate_stage(2)
            lo_from_aux(y_lo[:, 3, :, :], aux4, y_hi[:, 3, :, :], "D_y")
            take_mod(5)
            gate_stage(3)
            take_mod(6)
            for n in range(2):
                block_lo("m", n)

            def add_to_x(v, col, pair, b, gate, added=None):
                dve.tensor_tensor(zt[:, b], ps[:, pair], wide(gate[:, col], NT), ALU.mult)\
                    .then_inc(evacuated, 1)
                dve.wait_ge(evacuated, v + 1)
                if added is not None:
                    dve.wait_ge(x_added, added)
                dve.tensor_tensor(x3[:, :, col], x3[:, :, col], zt[:, b], ALU.add).then_inc(x_added, 1)

            def scale_rows():
                dve.wait_ge(scale_in, 32)
                dve.scalar_tensor_tensor(gs2[:, :], gs2[:, :], 1.0, gnb[:, :], ALU.add, ALU.mult).then_inc(gs2_ready, 1)

            def late_lo(rnd):
                return {2: (lambda: block_lo(rnd, 2),), 4: (lambda: block_lo(rnd, 3),)}

            for n in range(DB):
                g = G_WO + n * UC
                ahead(g, before={0: late_lo("m"), 2: {4: (scale_rows,)}}.get(n, {}),
                      after=mod_steps(7 * KT + 4 * n, 4 * n, True))
                evac_begin(g + UC)
                if n == 0:
                    dve.wait_ge(x_in_again, 32)
                else:
                    dve.wait_ge(x_added, n)
                add_to_x(V_WO + n, slice(n * NB, (n + 1) * NB), (n + 1) % 2, 0, gt1b)
            take_mod(7)

            def row_sums(n):
                dve.wait_ge(squared, DB * n)
                link(dve.tensor_reduce(ss[:, :], ss4[:, :, :], AX_X, ALU.add))

            row_sums(1)
            variance(2)
            dve.wait_ge(gs2_ready, 1)
            dve.wait_ge(shift_in, 16)
            norm_block(h2, x3, 0, gs2, sh2b)
            for n in range(1, DB):
                norm_block(h2, x3, n, gs2, sh2b)
                if n < 3:
                    block_lo("n", n - 1)

            def hidden_lo(q, j):
                dve.wait_ge(aux_hi, len(HI_ROUNDS) + 4 * q + j + 1)
                dve.tensor_tensor(a_lo[:, 4 * j:4 * j + 4, :], aux4, a_hi[:, 4 * j:4 * j + 4, :].bitcast(F32),
                                  ALU.subtract).then_inc(aux_free, 1)

            def ff_group(q, start=False, last=False):
                v, g = V_FF + 2 * DB * q, G_FF + 2 * DB * UC * q
                for j in range(DB):
                    ahead(g + j * UC, before={3: (lambda: hidden_lo(q, j - 1),)} if j else
                          late_lo("n") if start else {})
                    evac_begin(g + (j + 1) * UC)
                    dve.tensor_scalar(zt[:, j % 2], ps[:, (1 + j) % 2], 0.0, None, ALU.max).then_inc(evacuated, 1)
                v, g = v + DB, g + DB * UC
                for j in range(DB):
                    ahead(g + j * UC, before={} if j else {3: (lambda: hidden_lo(q, DB - 1),)},
                          last=last and j == DB - 1)
                    evac_begin(g + (j + 1) * UC)
                    if start and j == 0:
                        dve.wait_ge(gate_in, 16)
                    add_to_x(v + j, slice(j * NB, (j + 1) * NB), (1 + j) % 2, j % 2, gt2b,
                             DB * (1 + q) + j)

            ff_group(0, start=True)
            with dve.Fori(1, FF_GROUPS - 1) as q:
                ff_group(q)
            ff_group(FF_GROUPS - 1, last=True)
            row_sums(2)
            variance(3)
            dve.wait_ge(gfin_in, 16)
            for t, col in OUT_PARTS:
                dve.scalar_tensor_tensor(x3[:, t, col], x3[:, t, col], rstd[:, t:t + 1], gnb[:, col], ALU.mult, ALU.mult)\
                    .then_inc(fin_ready, 1)

        @block.gpsimd
        def _(pool):
            link = Links(pool, pool_step)
            for dst, src in ((bada[:, :], bada_cols), (convw[:, :, :], conv_cols), (tabT[:, :], tab),
                             (bf[:, :], bcast_rows(b_f[0:1, :])), (gsub[:, :], bcast_rows(g_subln[0:1, :])),
                             (lamb[:, :, :].rearrange("p a d -> p (a d)"), bcast_rows(lam[0:1, :]))):
                pool.dma_start(dst, src).then_inc(small_in, 16)
            link(pool.memset(ident[:, :], 0.0))
            pool.affine_select(out=ident[:, :], in_=ident[:, :], compare_op=ALU.not_equal, fill=1.0, base=0,
                               pattern=[[-1, P]], channel_multiplier=1).then_inc(consts, 1)
            link(pool.memset(mirror[:, :], 0.0))
            pool.affine_select(out=mirror[:, :], in_=mirror[:, :], compare_op=ALU.not_equal, fill=1.0, base=1 - P,
                               pattern=[[1, P]], channel_multiplier=1).then_inc(consts, 1)
            link(pool.memset(triones[:, :], 1.0))
            pool.affine_select(out=triones[:, :], in_=triones[:, :], compare_op=ALU.is_ge, fill=0.0, base=0,
                               pattern=[[1, SEQ]], channel_multiplier=-1).then_inc(consts, 1)

            def bias_of(r):
                return bcast_rows(bias_rows[bass.ds(r, 1), :])

            for b in range(2):
                pool.dma_start(brow[:, b, :], bcast_rows(bias_rows[b:b + 1, :])).then_inc(brow_in[b], 16)
            pool.wait_ge(dist_ready, 1)
            pool.dma_start(dist_d.ap(), dist[:, :]).then_inc(dist_out, 16)

            def ada_rows(i):
                for b in range(2):
                    pool.wait_ge(evacuated, 2 * i + b - 1)
                    pool.dma_start(brow[:, b, :], bias_of(2 * i + b)).then_inc(brow_in[b], 16)

            ada_rows(1)
            pool.wait_ge(dist_out, 16)
            pool.dma_start(steps[:, :, :], bass.AP(tensor=dist_d, offset=0,
                                                   ap=[[1, P], [LOG_COLS, 2 * NH], [1, SEQ]])).then_inc(steps_in, 16)
            with pool.Fori(2, 4) as i:
                ada_rows(i)
            pool.wait_ge(bias_turned, 1)
            pool.affine_select(out=Bm[:, :, :], in_=Bm[:, :, :], compare_op=ALU.is_ge, fill=NEG, base=P,
                               pattern=[[0, 2 * NH], [-1, SEQ]], channel_multiplier=1).then_inc(bm_ready, 1)

            def causal(t0, t1, pat, sem_out):
                link.step(pool.affine_select(out=t0, in_=t0, compare_op=ALU.is_ge, fill=NEG,
                                             base=0, pattern=pat + [[-1, P]], channel_multiplier=1))
                link.wait()
                pool.affine_select(out=t1, in_=t1, compare_op=ALU.is_ge, fill=NEG, base=P, pattern=pat + [[-1, SEQ]], channel_multiplier=1)\
                    .then_inc(sem_out, 1)

            pool.wait_ge(score_ready, 1)
            causal(score[:, 0:P], score[:, P:LOG_COLS], [], score_masked)

            def gate_row(m, n, b):
                pool.wait_ge(evacuated, V_GATE + 2 * (m * DB + n) - 3)
                pool.dma_start(brow[:, b, :], bias_of(ADA_UNITS + m * DB + n)).then_inc(brow_in[b], 16)

            def gate_rows(m):
                with pool.Fori(0, DB // 2) as i:
                    for b in range(2):
                        gate_row(m, 2 * i + b, b)

            def mod_of(r):
                return bcast_rows(mods_d.ap()[r].rearrange("k p -> (k p)").unsqueeze(0))

            pool.wait_ge(row_out, 16)
            pool.dma_start(gt1b[:, :], mod_of(0)).then_inc(x_in_again, 16)
            for b in range(2):
                gate_row(0, b, b)
            pool.wait_ge(aux_free, RND["D_sums"] + 1)
            causal(pr[:, :, 0:P], pr[:, :, P:LOG_COLS], [[0, NH]], dm_ready)
            for b in range(2):
                gate_row(0, 2 + b, b)
            for m in (1, 2):
                gate_rows(m)
            pool.wait_ge(aux_free, RND["D_y"] + 1)
            pool.dma_start(x3[:, :, :], x_v).then_inc(x_in_again, 16)
            for b in range(2):
                gate_row(3, b, b)
            pool.wait_ge(row_out, 48)
            pool.dma_start(sh2b[:, :], mod_of(1)).then_inc(shift_in, 16)
            for b in range(2):
                gate_row(3, 2 + b, b)
            pool.dma_start(gs2[:, :], mod_of(2)).then_inc(scale_in, 16)
            pool.dma_start(gnb[:, :], bcast_rows(g_norm2[0:1, :])).then_inc(scale_in, 16)
            pool.wait_ge(x_added, DB)
            pool.wait_ge(row_out, 64)
            pool.dma_start(gt2b[:, :], mod_of(3)).then_inc(gate_in, 16)
            pool.wait_ge(gs2_ready, 1)
            pool.dma_start(gnb[:, :], bcast_rows(g_final[0:1, :])).then_inc(gfin_in, 16)
            pool.wait_ge(gfin_in, 16)


def tiles(w):
    import numpy as np
    k, n = w.shape
    return np.ascontiguousarray(w.reshape(k // (CK * P), CK, P, n // NB, NB).transpose(3, 0, 2, 1, 4))\
        .reshape(-1, P, CK * NB)


def kernel(**inputs):
    import numpy as np
    import concourse.bacc as bacc
    from concourse.bass_utils import run_bass_kernel_spmd

    i = {k: np.asarray(v) for k, v in inputs.items()}
    w_in = i["w_in"][0]
    cuts = np.cumsum([0, 512, 512, 512, 256, 64, 4, 512, 512, 512, 512, 512, 512, 512, 512, 512, 4])
    qa, ka, va, iq, ik, iw, qb, kb, vb, bg, cg, xin, qd, kd, vd, fd = (
        w_in[:, a:b] for a, b in zip(cuts[:-1], cuts[1:]))
    pad = np.zeros((D, NB - IK0 - IDX_DIM - 2 * NH), w_in.dtype)
    w_ada, b_ada = i["w_ada"][0], i["b_ada"][0]
    stream = [tiles(w_ada[:, :2 * D])]
    stream += [tiles(np.concatenate([iq, ik, iw, fd, pad], axis=1))]
    stream += [tiles(w) for w in (qa, ka, va, qb, kb, vb, bg, cg, xin, qd, kd, vd)]
    for m in MIXERS:
        gate = tiles(i["w_gate"][0][:, m * D:(m + 1) * D]).reshape(DB, UC, P, CK * NB)
        branch = tiles(i["w_branch"][0, m]).reshape(DB, BC, P, CK * NB)
        stream += [np.concatenate([gate, branch], axis=1).reshape(-1, P, CK * NB)]
    stream += [tiles(i["w_o"][0])]
    for q in range(FF_GROUPS):
        stream += [tiles(i["w_ff1"][0][:, q * D:(q + 1) * D]), tiles(i["w_ff2"][0][q * D:(q + 1) * D, :])]
    stream = np.concatenate(stream, axis=0)
    b_gate = i["b_gate"][0].reshape(4, DB, NB)
    arrays = {
        "stream": stream,
        "mod_stream": np.ascontiguousarray(w_ada[:, 2 * D:].reshape(KT, P, MOD_BLOCKS, MOD_W).transpose(2, 0, 1, 3))
        .reshape(MOD_STEPS, P, MOD_W),
        "bias_rows": np.concatenate([b_ada[:2 * D].reshape(-1, NB)] + [b_gate[m] for m in MIXERS], axis=0),
        "x": i["x"][0],
        "c_cols": np.ascontiguousarray(i["c"][0].reshape(KT, P).T),
        "conv_cols": np.ascontiguousarray(i["conv_w"][0].reshape(3, NH, P).transpose(2, 1, 0)),
        "lam": i["lam"].reshape(1, 4 * DD),
        "g_subln": i["g_subln"].reshape(1, HD),
        "tab": np.ascontiguousarray(i["rel_bias"].T),
        "b_f": i["b_f"].reshape(1, NH),
        "bada_cols": np.ascontiguousarray(b_ada[2 * D:].reshape(4 * KT, P).T),
        "g_norm1": i["g_norm1"].reshape(1, D),
        "g_norm2": i["g_norm2"].reshape(1, D),
        "g_final": i["g_final"].reshape(1, D),
    }
    nc = bacc.Bacc("TRN2", target_bir_lowering=False, num_devices=1)
    args = [nc.dram_tensor(f"in_{k}", a.shape, mybir.dt.from_np(a.dtype), kind="ExternalInput").ap()
            for k, a in arrays.items()]
    args.append(nc.dram_tensor("out_x", (SEQ, D), F32, kind="ExternalOutput").ap())
    build(nc, *args)
    r = run_bass_kernel_spmd(nc, [{f"in_{k}": a for k, a in arrays.items()}], core_ids=[0])
    return r.results[0]["out_x"].reshape(1, SEQ, D)
```

```python
import math
from contextlib import ExitStack

import concourse.bass as bass
from concourse import mybir

F32 = mybir.dt.float32
F32R = mybir.dt.float32r
ALU = mybir.AluOpType
ACT = mybir.ActivationFunctionType
AX_X = mybir.AxisListType.X

P = 128
D = 2048
SEQ = 256
NT = SEQ // P
KT = D // P
NB = 512
DB = D // NB
HD = 128
NH = 4
DD = HD // 2
IDX_DIM = 64
K_TOP = 64
N_BUCKETS = 32
MAX_DIST = 128
EPS = 1e-6
NEG = -1e30
TAKEN = -3e38
IDX_SCALE = (IDX_DIM ** -0.5) * (NH ** -0.5)
LAM_INIT = 0.8 - 0.6 * math.exp(0.0)
LOG_COLS = P + SEQ

RING = 4
CK = 2
UC = KT // CK
BC = NH // CK
ADA_UNITS = 2 * DB
WIN_UNITS = 13
GATE_UNITS = 2 * 4 * DB
MIXERS = (2, 0, 1, 3)
G_WIN = ADA_UNITS * UC
G_GATE = G_WIN + WIN_UNITS * UC
G_WO = G_GATE + 4 * DB * (UC + BC)
G_FF = G_WO + DB * UC
CHUNKS = G_FF + 32 * UC
V_WIN = ADA_UNITS
V_GATE = V_WIN + WIN_UNITS
V_WO = V_GATE + GATE_UNITS
V_FF = V_WO + DB
FF_GROUPS = 4
MOD_W = 2 * NB
MOD_BLOCKS = 4 * D // MOD_W
MOD_STEPS = MOD_BLOCKS * KT

ROUNDS = ["h0", "h1", "h2", "h3", "mod0", "idx_T", "idx_dots", "A_qk", "A_dots", "B_qk", "A_pT", "A_y",
          "B_dots0", "B_dots1", "mod1", "B_pT", "C_T", "B_o", "D_sums", "D_qk", "D_dots", "mod2",
          "mod3", "D_pT",  "mod4", "B_y", "mod5", "D_y",  "mod6", "m0", "m1", "m2", "m3",
          "mod7",  "n0", "n1", "n2", "n3"]
RND = {name: i for i, name in enumerate(ROUNDS)}
HI_ROUNDS = [r for r in ROUNDS if r[0] in "hmn" and len(r) == 2 or r in ("A_y", "B_y", "D_y")]

MISC, QA, KA, VA, QB, KB, VB, BG, CG, XIN = range(10)
QD, KD, VD = QA, KA, VA
IK0 = 4 * IDX_DIM
IW0 = IK0 + IDX_DIM
FD0 = IW0 + NH


class Links:

    def __init__(self, eng, sem):
        self.eng, self.sem, self.base, self.n = eng, sem, 0, 0

    def enter(self, i, per):
        self.base0, self.per = self.base + self.n, per
        self.base, self.n = self.base0 + i * per, 0

    def leave(self, times):
        assert self.n == self.per, (self.n, self.per)
        self.base, self.n = self.base0 + times * self.per, 0

    def step(self, ins):
        ins.then_inc(self.sem, 1)
        self.n += 1

    def wait(self):
        self.eng.wait_ge(self.sem, self.base + self.n)

    def __call__(self, ins):
        self.step(ins)
        self.wait()


def t5_runs():
    exact = N_BUCKETS // 2
    of = [n if n < exact else min(N_BUCKETS - 1, exact + int(math.log(n / exact) / math.log(MAX_DIST / exact)
                                                            * (N_BUCKETS - exact))) for n in range(SEQ)]
    return [(b, of.index(b), SEQ - of[::-1].index(b)) for b in sorted(set(of))]


def build(nc, stream, mod_stream, bias_rows, x_in, c_cols, conv_cols, lam, g_subln, tab, b_f, mod_bias, g_norm1, g_norm2, g_final, out):
    base = (nc.sbuf_base + 31) // 32 * 32
    K = 1024

    def at(name, off, shape, dt=F32):
        return nc.alloc_sbuf_tensor_at(name, shape, dt, offset=base + int(off))

    raw = at("raw", 0, [P, RING, CK * NB])
    w_hi = at("w_hi", 16 * K, [P, RING, CK * NB], F32R)
    w_lo = at("w_lo", 32 * K, [P, RING, CK * NB], F32R)
    act_hi = at("act_hi", 48 * K, [P, KT, SEQ], F32R)
    act_lo = at("act_lo", 64 * K, [P, KT, SEQ], F32R)
    sq_junk = at("sq_junk", 48 * K, [P, D])
    Z = 80 * K
    ident = at("ident", Z, [P, P])
    triones = at("triones", Z + 512, [P, SEQ])
    so = [Z + 1536]

    def small(name, shape, dt=F32):
        n = 1
        for s in shape[1:]:
            n *= s
        t = at(name, (so[0] + 31) // 32 * 32, shape, dt)
        so[0] = (so[0] + 31) // 32 * 32 + 4 * n
        return t

    gsub = small("gsub", [P, HD])
    convw = small("convw", [P, NH, 3])
    bf = small("bf", [P, NH])
    nlam = small("nlam", [P, 1])
    ss = small("ss", [P, 2])
    rstd = small("rstd", [P, 2])
    iws = small("iws", [P, NT, NH])
    lsig = small("lsig", [P, NT, NH])
    lsig2 = small("lsig2", [P, NT, NH])
    Ftok = small("Ftok", [P, NT, NH])
    nmax = small("nmax", [P, 2, NT, NH])
    esum = small("esum", [P, 2, NT, NH])
    rec = small("rec", [P, 2, NT, NH])
    m8 = small("m8", [P, NT, 8])
    ss4 = small("ss4", [P, NT, DB])
    spare = small("spare", [P, 1])
    csil = small("csil", [P, KT])
    csil_hi = small("csil_hi", [P, KT], F32R)
    csil_lo = small("csil_lo", [P, KT], F32R)
    assert so[0] <= Z + 3 * K
    brow = at("brow", Z + 3 * K, [P, 2, NB])
    zt = at("zt", Z + 7 * K, [P, 2, NT, NB])
    x1 = at("x1", Z + 15 * K, [P, NT, D])
    sh1 = at("sh1", Z + 31 * K, [P, D])
    gs1 = at("gs1", Z + 39 * K, [P, D])
    steps = at("steps", Z + 79 * K, [P, 2 * NH, SEQ])
    lamb = at("lamb", Z + 87 * K, [P, 4, DD])
    lprod = at("lprod", Z + 88 * K, [P, 2, DD])
    lsum = at("lsum", Z + 88.5 * K, [P, 4])
    tabT = at("tabT", Z + 88.75 * K, [8, N_BUCKETS])
    dist = at("dist", Z + 89 * K, [8, LOG_COLS])
    cc = at("cc", Z + 90.5 * K, [P, 3, KT])
    mirror = at("mirror", Z + 115 * K, [P, P])
    proj = at("proj", Z + 15 * K, [P, 10, NT, NB])
    merged = at("merged", Z + 43 * K, [P, NT, D])
    y_hi = at("y_hi", Z + 59 * K, [P, 4, NH, SEQ], F32R)
    y_lo = at("y_lo", Z + 75 * K, [P, 4, NH, SEQ], F32R)
    Bm = at("Bm", Z + 91 * K, [P, 2 * NH, SEQ])
    qkT = at("qkT", Z + 99 * K, [P, 2, NH, SEQ])
    pr = at("pr", Z + 107 * K, [P, NH, LOG_COLS])
    pr2 = at("pr2", Z + 113 * K, [P, NH, LOG_COLS])
    iqT = at("iqT", Z + 113 * K, [IDX_DIM, NH + 1, SEQ])
    ob = at("ob", Z + 113 * K, [P, NT, NH, HD])
    pT = at("pT", Z + 119 * K, [P, NH, LOG_COLS])
    score = at("score", Z + 122.5 * K, [P, LOG_COLS])
    mod_lines = at("mod_lines", Z + 125 * K, [P, NB])
    mod_raw = [at(f"mod_raw{i}", o, [P, MOD_W]) for i, o in
               enumerate((Z + 63 * K, Z + 71 * K, Z + 79 * K, Z + 87 * K))]
    mod_raw2 = [at(f"mod_late{i}", Z + (99 + 4 * i) * K, [P, MOD_W]) for i in range(2)]
    acc = zt[:, 1].rearrange("p t n -> p (t n)")
    work = at("work", Z + 119 * K, [P, LOG_COLS])
    selm = at("selm", Z + 121 * K, [P, LOG_COLS])
    x3 = at("x3", Z + 15 * K, [P, NT, D])
    gt1b = at("gt1b", Z + 31 * K, [P, D])
    a_hi = at("a_hi", Z + 59 * K, [P, KT, SEQ], F32R)
    a_lo = at("a_lo", Z + 75 * K, [P, KT, SEQ], F32R)
    gs2 = at("gs2", Z + 91 * K, [P, D])
    sh2b = at("sh2b", Z + 107 * K, [P, D])
    gt2b = at("gt2b", Z + 31 * K, [P, D])
    gnb = at("gnb", Z + 115 * K, [P, D])
    h2 = at("h2", Z + 43 * K, [P, NT, D])

    dist_d = nc.dram_tensor("dist_d", (8, LOG_COLS), F32, kind="Internal")
    mods_d = nc.dram_tensor("mods_d", (MOD_BLOCKS, 2, NB), F32, kind="Internal")
    x_v = x_in.rearrange("(t p) d -> p t d", p=P)
    out_v = out.rearrange("(t p) d -> p t d", p=P)

    SMALL_LOADS = 6
    OUT_PARTS = [(t, slice(k * D // 2, (k + 1) * D // 2)) for t in range(NT) for k in range(2)]

    def bcast_rows(ap, n=P):
        return ap.partition_broadcast(n)

    with ExitStack() as ctx:
        def sem(name):
            return ctx.enter_context(nc.semaphore(name))

        ps = ctx.enter_context(nc.psum_tensor("ps", [P, 2, NT, NB], F32))
        aux = ctx.enter_context(nc.psum_tensor("aux", [P, 4, NB], F32))

        loaded = [sem(f"loaded{i}") for i in range(RING)]
        hi_ready = sem("hi_ready")
        lo_ready = sem("lo_ready")
        used = sem("used")
        evacuated = sem("evacuated")
        aux_full = sem("aux_full")
        aux_free = sem("aux_free")
        aux_hi = sem("aux_hi")
        brow_in = [sem("brow_in0"), sem("brow_in1")]
        brow_used = sem("brow_used")
        consts = sem("consts")
        small_in = sem("small_in")
        x_loaded = sem("x_loaded")
        g_in = sem("g_in")
        c_ready = sem("c_ready")
        cb_ready = sem("cb_ready")
        sumsq = sem("sumsq")
        root = sem("root")
        var_ready = sem("var_ready")
        h_ready = sem("h_ready")
        mod_in = [sem(f"mod_in{i}") for i in range(4)]
        mod_in2 = [sem(f"mod_late_in{i}") for i in range(2)]
        mod_used = sem("mod_used")
        acc_ready = sem("acc_ready")
        row_out = sem("row_out")
        c_in = sem("c_in")
        dist_ready = sem("dist_ready")
        dist_out = sem("dist_out")
        steps_in = sem("steps_in")
        bias_full = sem("bias_full")
        bias_turned = sem("bias_turned")
        bm_ready = sem("bm_ready")
        lam_sum = sem("lam_sum")
        lam_exp = sem("lam_exp")
        score_ready = sem("score_ready")
        score_masked = sem("score_masked")
        neg_max = sem("neg_max")
        exps = sem("exps")
        p_ready = sem("p_ready")
        u_ready = sem("u_ready")
        yc_raw = sem("yc_raw")
        yc_hi = sem("yc_hi")
        yc_ready = sem("yc_ready")
        yb_var = sem("yb_var")
        yb_root = sem("yb_root")
        yb_ready = sem("yb_ready")
        f_abs = sem("f_abs")
        f_log = sem("f_log")
        ls_ready = sem("ls_ready")
        dm_ready = sem("dm_ready")
        gate_ready = sem("gate_ready")
        merged_ready = sem("merged_ready")
        x_in_again = sem("x_in_again")
        shift_in = sem("shift_in")
        scale_in = sem("scale_in")
        gate_in = sem("gate_in")
        squared = sem("squared")
        gfin_in = sem("gfin_in")
        gs2_ready = sem("gs2_ready")
        x_added = sem("x_added")
        a_ready = sem("a_ready")
        dve_step = sem("dve_step")
        act_step = sem("act_step")
        pool_step = sem("pool_step")
        y_out = sem("y_out")
        fin_ready = sem("fin_ready")

        block = ctx.enter_context(nc.Block())

        @block.sync
        def _(sp):
            def load(g, slot, first=False):
                if not first:
                    sp.wait_ge(lo_ready, g - RING + 1)
                sp.dma_start(raw[:, slot, :], stream[g]).then_inc(loaded[slot], 16)

            def load_mod(j, k, late=False):
                ring, sems = (mod_raw2, mod_in2) if late else (mod_raw, mod_in)
                if not (isinstance(j, int) and j < len(ring)):
                    sp.wait_ge(mod_used, j - len(ring) + 2)
                sp.dma_start(ring[k][:, :], mod_stream[j]).then_inc(sems[k], 16)

            def load_ahead(g, j, slot0=0, n=UC, late=False):
                k = 0
                for c in range(n):
                    load(g + RING + c, (slot0 + c) % RING)
                    if k < 4 and c == 2 * k + late:
                        load_mod(j + k, k % (2 if late else 4), late)
                        k += 1

            for s in range(RING):
                load(s, s, True)
            with sp.Fori(1, (G_WIN + UC) // RING + 1) as i:
                for s in range(RING):
                    load(i * RING + s, s)
            load_ahead(G_WIN + UC, 0)
            with sp.Fori(1, WIN_UNITS - 1) as i:
                load_ahead(G_WIN + UC + UC * i, 4 * i)
            for late, lo, hi in ((False, 0, 4), (True, 4, 8)):
                with sp.Fori(lo, hi) as i:
                    for b in range(2):
                        load_ahead(G_GATE + (2 * i + b) * (UC + BC), 3 * KT + (2 * i + b) * 4, b * (UC + BC),
                                   UC + BC, late)
            with sp.Fori(0, DB) as i:
                load_ahead(G_WO + UC * i, 7 * KT + 4 * i, late=True)
            with sp.Fori(G_FF // RING + 1, CHUNKS // RING) as i:
                for s in range(RING):
                    load(i * RING + s, s)
            for k, (t, col) in enumerate(OUT_PARTS):
                sp.wait_ge(fin_ready, k + 1)
                sp.dma_start(out_v[:, t, col], x3[:, t, col]).then_inc(y_out, 16)
            sp.wait_ge(y_out, 16 * len(OUT_PARTS))

        @block.tensor
        def _(pe):
            def products(dst, acts, kt, t, slot, j, first, last, one_tile=False):
                a_h, a_l = (a[:, kt:kt + 1].to_broadcast([P, P]) if one_tile else a[:, kt, t * P:(t + 1) * P] for a in acts)
                wh, wl = (w[:, slot, j * NB:(j + 1) * NB] for w in (w_hi, w_lo))
                pe.matmul(dst, a_h, wh, start=first, stop=False)
                pe.matmul(dst, a_h, wl, start=False, stop=False)
                return pe.matmul(dst, a_l, wh, start=False, stop=last)

            def chunk(v_pair, acts, g, slot, c, n, tiles=NT, one_tile=False):
                pe.wait_ge(lo_ready, g + 1)
                for j in range(CK):
                    kt = c * CK + j
                    for t in range(tiles):
                        mm = products(ps[:, v_pair, t, :], acts, kt, t, slot, j, kt == 0, kt == n * CK - 1,
                                      one_tile)
                mm.then_inc(used, 1)

            def unit(v, pair, acts, g, slot0=0, n=UC, before={}, **kw):
                if not (isinstance(v, int) and v < 2):
                    pe.wait_ge(evacuated, v - 1)
                for c in range(n):
                    for step in before.get(c, ()):
                        step()
                    chunk(pair, acts, g + c, (slot0 + c) % RING, c, n, **kw)

            def pair_of_units(v, p0, acts, g, **kw):
                unit(v, p0, acts, g, **kw)
                unit(v + 1, 1 - p0, acts, g + UC, **kw)

            rounds = [0]

            def open_aux(name, halves=False):
                assert ROUNDS[rounds[0]] == name
                if rounds[0] - halves > 0:
                    pe.wait_ge(aux_free, rounds[0] - halves)
                rounds[0] += 1

            def taken(name):
                pe.wait_ge(aux_free, RND[name] + 1)

            def T(dst, src):
                k, m = src.shape[0], src.shape[1]
                return pe.transpose(dst, src, ident[0:k, 0:k])

            def block_T(src, rnd, n, ready):
                open_aux(f"{rnd}{n}", halves=n > 0 or rnd != "h")
                pe.wait_ge(*ready)
                v = aux[:, 2 * (n % 2):2 * (n % 2) + 2, :].rearrange("p b (k s) -> p (b k) s", s=SEQ)
                for k in range(4):
                    for t in range(NT):
                        mm = T(v[:, k, t * P:(t + 1) * P], src[:, t, (4 * n + k) * P:(4 * n + k + 1) * P])
                mm.then_inc(aux_full, 1)

            def mod_sum(d, halves=False):
                open_aux(f"mod{d}", halves)
                pe.wait_ge(mod_used, 1 + KT * (d + 1))
                ones = triones[:, SEQ - 1:SEQ].to_broadcast([P, P])
                for k in range(2):
                    mm = pe.matmul(aux[:, 2 + k, :], ones, acc[:, k * NB:(k + 1) * NB], start=True, stop=True)
                mm.then_inc(aux_full, 1)

            def heads_T(name, first, second):
                open_aux(name)
                v = aux[:, :, :].rearrange("p (q b) (h s) -> p q (b h) s", q=2, s=SEQ)
                for q, slot in enumerate((first, second)):
                    for h in range(NH):
                        for t in range(NT):
                            mm = T(v[:, q, h, t * P:(t + 1) * P], proj[:, slot, t, h * HD:(h + 1) * HD])
                mm.then_inc(aux_full, 1)

            def scores(name, rows_of, keys_of):
                open_aux(name)
                for h in range(NH):
                    q, k = rows_of(h), keys_of(h)
                    pe.matmul(aux[:, h, 0:P], q[:, 0:P], k[:, 0:P], start=True, stop=True)
                    mm = pe.matmul(aux[:, h, P:LOG_COLS], q[:, P:SEQ], k, start=True, stop=True)
                mm.then_inc(aux_full, 1)

            def probs_T(name):
                open_aux(name)
                for h in range(NH):
                    for b in range(3):
                        mm = T(aux[:, h, b * P:(b + 1) * P], pr[:, h, b * P:(b + 1) * P])
                mm.then_inc(aux_full, 1)

            def values_T(name, slot, halves=False):
                open_aux(name, halves)
                v = aux[:, 0:2, :].rearrange("p b (h s) -> p (b h) s", s=SEQ)
                for h in range(NH):
                    pe.matmul(v[:, h, :], proj[:, slot, 0, h * HD:(h + 1) * HD], pT[:, h, 0:SEQ],
                              start=True, stop=False)
                    mm = pe.matmul(v[:, h, P:SEQ], proj[:, slot, 1, h * HD:(h + 1) * HD], pT[:, h, SEQ:LOG_COLS],
                                   start=False, stop=True)
                mm.then_inc(aux_full, 1)

            cb = (csil_hi, csil_lo)
            hT = (act_hi, act_lo)
            pe.wait_ge(cb_ready, 1)
            ada = dict(tiles=1, one_tile=True)
            pair_of_units(0, 0, cb, 0, **ada)
            with pe.Fori(1, 3) as i:
                pair_of_units(2 * i, 0, cb, 2 * UC * i, **ada)
            pe.wait_ge(consts, 3)
            pe.wait_ge(steps_in, 16)
            for b in range(4):
                mm = pe.matmul(aux[:, b, :], mirror[:, :], steps[:, 2 * b:2 * b + 2, :], start=True, stop=True)
            mm.then_inc(bias_full, 1)
            pe.wait_ge(bias_turned, 1)
            block_T(x1, "h", 0, (h_ready, 1))
            unit(6, 0, cb, 6 * UC, **ada)
            block_T(x1, "h", 1, (h_ready, 2))
            unit(7, 1, cb, 7 * UC, **ada)
            block_T(x1, "h", 2, (h_ready, 3))

            def late_blocks(src, rnd, ready):
                return {0: (lambda: taken(rnd + "0"),),
                        2: (lambda: block_T(src, rnd, 2, ready(2)), lambda: taken(rnd + "1")),
                        4: (lambda: block_T(src, rnd, 3, ready(3)), lambda: taken(rnd + "2")),
                        6: (lambda: taken(rnd + "3"),)}

            unit(V_WIN, 0, hT, G_WIN, before={
                0: (lambda: taken("h0"),), 2: (lambda: taken("h1"),),
                4: (lambda: block_T(x1, "h", 3, (h_ready, 4)), lambda: taken("h2")), 6: (lambda: taken("h3"),)})
            with pe.Fori(0, 2) as i:
                pair_of_units(V_WIN + 1 + 2 * i, 1, hT, G_WIN + UC + 2 * UC * i)

            def idx_T():
                open_aux("idx_T")
                vi = aux[0:IDX_DIM, :, :].rearrange("p b (k s) -> p (b k) s", s=SEQ)
                for h in range(NH + 1):
                    for t in range(NT):
                        mm = T(vi[:, h, t * P:(t + 1) * P], proj[:, MISC, t, h * IDX_DIM:(h + 1) * IDX_DIM])
                mm.then_inc(aux_full, 1)

            def idx_dots():
                scores("idx_dots", lambda h: iqT[:, h, :], lambda h: iqT[:, NH, :])

            def qk_dots(name):
                scores(name, lambda h: qkT[:, 0, h, :], lambda h: qkT[:, 1, h, :])

            def diff_dots(half):
                lo = half * DD
                scores(f"B_dots{half}", lambda h: qkT[lo:lo + DD, 0, h, :], lambda h: qkT[lo:lo + DD, 1, h, :])

            def weights_T(name, n):
                pe.wait_ge(p_ready, n)
                probs_T(name)

            def conv_T():
                pe.wait_ge(u_ready, 1)
                heads_T("C_T", CG, BG)

            def diff_values():
                open_aux("B_o")
                vo = aux[:, 0:2, :].rearrange("p t (h d) -> p t h d", h=NH)
                for h in range(NH):
                    v0, v1 = (proj[:, VB, t, h * HD:(h + 1) * HD] for t in range(NT))
                    pe.matmul(vo[:, 0, h, :], pT[:, h, 0:P], v0, start=True, stop=True)
                    pe.matmul(vo[:, 1, h, :], pT[:, h, P:SEQ], v0, start=True, stop=False)
                    mm = pe.matmul(vo[:, 1, h, :], pT[:, h, SEQ:LOG_COLS], v1, start=False, stop=True)
                mm.then_inc(aux_full, 1)

            def forget_T():
                pe.wait_ge(evacuated, V_WIN + 12)
                heads_T("D_qk", QD, KD)

            def forget_sums():
                pe.wait_ge(ls_ready, 1)
                open_aux("D_sums")
                vf = aux[:, 0:2, :].rearrange("p b (h s) -> p (b h) s", s=SEQ)
                for h in range(NH):
                    pe.matmul(vf[:, h, :], lsig[:, 0, h:h + 1].to_broadcast([P, P]), triones[:, :],
                              start=True, stop=False)
                    pe.matmul(vf[:, h, P:SEQ], lsig[:, 1, h:h + 1].to_broadcast([P, P]), triones[:, 0:P],
                              start=False, stop=True)
                pe.matmul(aux[:, 2, 0:NH], triones[:, 0:P], lsig[:, 0, :], start=True, stop=True)
                pe.matmul(aux[:, 2, NH:2 * NH], triones[:, P:SEQ], lsig[:, 0, :], start=True, stop=False)
                pe.matmul(aux[:, 2, NH:2 * NH], triones[:, 0:P], lsig[:, 1, :], start=False, stop=True)\
                    .then_inc(aux_full, 1)

            mixer_steps = {
                5: {0: (lambda: mod_sum(0),), 1: (idx_T,), 3: (idx_dots,), 5: (lambda: heads_T("A_qk", QA, KA),)},
                7: {0: (lambda: qk_dots("A_dots"),), 2: (lambda: heads_T("B_qk", QB, KB),)},
                8: {1: (lambda: weights_T("A_pT", 1),), 3: (lambda: values_T("A_y", VA),),
                    5: (lambda: diff_dots(0),), 7: (lambda: diff_dots(1),)},
                9: {0: (lambda: mod_sum(1),), 7: (lambda: weights_T("B_pT", 2),)},
                10: {2: (conv_T,), 4: (diff_values,)},
                11: {4: (forget_sums,)},
                12: {1: (forget_T,), 3: (lambda: qk_dots("D_dots"),)},
            }
            for u in range(5, WIN_UNITS):
                unit(V_WIN + u, u % 2, hT, G_WIN + u * UC, before=mixer_steps.get(u, {}))
            mod_sum(2)

            def gate_stage(m):
                yT = (y_hi[:, MIXERS[m]], y_lo[:, MIXERS[m]])
                g0, v0 = G_GATE + m * DB * (UC + BC), V_GATE + m * 2 * DB
                with pe.Fori(0, DB // 2) as i:
                    for b in range(2):
                        g = g0 + (2 * i + b) * (UC + BC)
                        v = v0 + 2 * (2 * i + b)
                        unit(v, 1, hT, g, slot0=b * (UC + BC))
                        if b == 0:
                            if m == 0:
                                pe.wait_ge(yc_ready, 1)
                            else:
                                taken({1: "A_y", 2: "B_y", 3: "D_y"}[m])
                        unit(v + 1, 0, yT, g + UC, slot0=b * (UC + BC) + UC, n=BC)

            gate_stage(0)
            mod_sum(3)
            weights_T("D_pT", 3)
            gate_stage(1)
            mod_sum(4)
            pe.wait_ge(yb_ready, 1)
            open_aux("B_y", halves=True)
            vb = aux[:, 0:2, :].rearrange("p b (h s) -> p (b h) s", s=SEQ)
            for h in range(NH):
                for t in range(NT):
                    mm = T(vb[:, h, t * P:(t + 1) * P], ob[:, t, h, :])
            mm.then_inc(aux_full, 1)
            gate_stage(2)
            mod_sum(5)
            values_T("D_y", VD, halves=True)
            gate_stage(3)
            mod_sum(6)

            merged_of = lambda n: (merged_ready, 2 * DB + n + 1)
            for n in range(2):
                block_T(merged, "m", n, merged_of(n))
            unit(V_WO, 1, hT, G_WO, before=late_blocks(merged, "m", merged_of))
            unit(V_WO + 1, 0, hT, G_WO + UC)
            pair_of_units(V_WO + 2, 1, hT, G_WO + 2 * UC)
            mod_sum(7)
            normed = lambda n: (h_ready, DB + n + 1)
            for n in range(2):
                block_T(h2, "n", n, normed(n))
            late_h2 = late_blocks(h2, "n", normed)

            def hidden_T(q, j):
                pe.wait_ge(aux_free, len(ROUNDS) + 4 * q + j)
                pe.wait_ge(a_ready, 4 * q + j + 1)
                for k in range(4):
                    for t in range(NT):
                        mm = T(vb[:, k, t * P:(t + 1) * P], zt[:, j % 2, t, k * P:(k + 1) * P])
                mm.then_inc(aux_full, 1)

            aT = (a_hi, a_lo)

            def group(q, first=False):
                v, g = V_FF + 2 * DB * q, G_FF + 2 * DB * UC * q
                for j in range(DB):
                    before = {3: (lambda: hidden_T(q, j - 1),)} if j else late_h2 if first else {}
                    unit(v + j, (1 + j) % 2, hT, g + j * UC, before=before)
                v, g = v + DB, g + DB * UC
                stands = lambda n: pe.wait_ge(aux_free, len(ROUNDS) + 4 * q + n)
                for j in range(DB):
                    before = {} if j else {0: (lambda: stands(3),), 3: (lambda: hidden_T(q, DB - 1),),
                                           6: (lambda: stands(4),)}
                    unit(v + j, (1 + j) % 2, aT, g + j * UC, before=before)

            group(0, True)
            with pe.Fori(1, FF_GROUPS) as q:
                group(q)

        @block.scalar
        def _(act):
            link = Links(act, act_step)

            def split(g, slot):
                act.wait_ge(loaded[slot], (g - slot) * 4 + 16)
                if not (isinstance(g, int) and g < RING):
                    act.wait_ge(used, g - RING + 1)
                act.activation(w_hi[:, slot, :], raw[:, slot, :], ACT.Copy).then_inc(hi_ready, 1)

            def ahead(g, slot0=0, n=UC, before={}, last=False):
                for c in range(n):
                    for step in before.get(c, ()):
                        step()
                    if not (last and c >= n - RING):
                        split(g + RING + c, (slot0 + c) % RING)

            act.dma_start(cc[:, 0, :], c_cols).then_inc(c_in, 16)
            act.wait_ge(c_in, 16)
            act.activation(cc[:, 1, :], cc[:, 0, :], ACT.Sigmoid).then_inc(c_ready, 1)
            for s in range(RING):
                split(s, s)

            def load_x(t, k):
                half = slice(k * D // 2, (k + 1) * D // 2)
                act.dma_start(x1[:, t, half], x_v[:, t, half]).then_inc(x_loaded, 16)

            def load_g(k):
                half = slice(k * D // 2, (k + 1) * D // 2)
                act.dma_start(gs1[:, half], bcast_rows(g_norm1[0:1, half])).then_inc(g_in, 16)

            def lambda_exp():
                act.wait_ge(lam_sum, 1)
                act.activation(lsum[:, 2:4], lsum[:, 0:2], ACT.Exp).then_inc(lam_exp, 1)

            def x_squares(t):
                act.wait_ge(*((sumsq, t) if t else (x_loaded, 16 * 4)))
                act.activation(sq_junk[:, :], x1[:, t, :], ACT.Square, accum_out=ss[:, t:t + 1]).then_inc(sumsq, 1)

            def norm_root_of(n):
                act.wait_ge(var_ready, n)
                act.activation(rstd[:, :], ss[:, :], ACT.Sqrt).then_inc(root, 1)

            norm_steps = {0: {0: (lambda: load_x(0, 0),), 4: (lambda: load_x(0, 1),)},
                          1: {0: (lambda: load_x(1, 0),), 4: (lambda: load_x(1, 1), lambda_exp)},
                          2: {0: (lambda: load_g(0),), 3: (lambda: load_g(1),), 4: (lambda: x_squares(0),),
                              7: (lambda: x_squares(1),)},
                          3: {3: (lambda: norm_root_of(1),)}}
            for u in range(6):
                ahead(u * UC, before=norm_steps.get(u, {}))

            auxw = aux[:, :, :].rearrange("p b n -> p (b n)")
            aux8 = aux[:, :, :].rearrange("p b (k s) -> p (b k) s", s=SEQ)
            aux4 = aux[:, 0:2, :].rearrange("p b (h s) -> p (b h) s", s=SEQ)

            def hi_from_aux(dst, src, name):
                act.wait_ge(aux_full, RND[name] + 1)
                act.activation(dst, src, ACT.Copy).then_inc(aux_hi, 1)

            def block_hi(rnd, n):
                hi_from_aux(act_hi[:, 4 * n:4 * n + 4, :], aux8[:, 4 * (n % 2):4 * (n % 2) + 4, :], f"{rnd}{n}")

            def take_aux(dst, src, name, func=ACT.Copy):
                act.wait_ge(aux_full, RND[name] + 1)
                act.activation(dst, src, func).then_inc(aux_free, 1)

            def take_qk(name):
                take_aux(qkT[:, :, :, :].rearrange("p q h s -> p (q h s)"), auxw, name)

            def take_pT(name):
                take_aux(pT[:, :, :], aux[:, :, 0:LOG_COLS], name)

            def take_mod(d):
                if d:
                    act.wait_ge(row_out, 16 * d)
                act.wait_ge(aux_full, RND[f"mod{d}"] + 1)
                act.activation(mod_lines[32:33, :], aux[32:33, 2, :], ACT.Copy)
                act.activation(mod_lines[64:65, :], aux[64:65, 3, :], ACT.Copy).then_inc(aux_free, 1)
                act.wait_ge(aux_free, RND[f"mod{d}"] + 1)
                act.dma_start(mods_d.ap()[d], mod_lines[32:65:32, :]).then_inc(row_out, 16)

            def exps_of(buf, c, n, heads):
                act.wait_ge(neg_max, n)
                for h in heads:
                    for t, (c0, c1) in enumerate(((0, P), (P, LOG_COLS))):
                        act.activation(buf[:, h, c0:c1], buf[:, h, c0:c1], ACT.Exp, bias=nmax[:, c, t, h:h + 1],
                                       accum_out=esum[:, c, t, h:h + 1]).then_inc(exps, 1)

            act.wait_ge(bias_full, 1)
            act.activation(Bm[:, :, :], aux8, ACT.Copy).then_inc(bias_turned, 1)
            block_hi("h", 0)
            ahead(6 * UC)
            block_hi("h", 1)
            ahead(7 * UC)
            block_hi("h", 2)

            def log_f():
                act.wait_ge(f_abs, 1)
                link(act.activation(lsig2[:, :, :], lsig2[:, :, :], ACT.Exp, scale=-1.0))
                act.activation(lsig2[:, :, :], lsig2[:, :, :], ACT.Ln, bias=1.0).then_inc(f_log, 1)

            def conv_hi():
                act.wait_ge(yc_raw, 1)
                act.activation(y_hi[:, 2, :, :], pr[:, :, 0:SEQ], ACT.Copy).then_inc(yc_hi, 1)

            def norm_root():
                act.wait_ge(yb_var, 1)
                act.activation(rec[:, 1, :, :], rec[:, 0, :, :], ACT.Sqrt).then_inc(yb_root, 1)

            G = G_WIN
            ahead(G, before={4: (lambda: block_hi("h", 3),)})
            with act.Fori(0, 2) as i:
                for b in range(2):
                    ahead(G + UC + (2 * i + b) * UC)
            first, second = (0, 1), (2, 3)
            mixer_steps = {
                5: {0: (lambda: take_mod(0),), 1: (lambda: take_aux(iqT[:, :, :], aux8[0:IDX_DIM, 0:NH + 1, :], "idx_T"),),
                    3: (lambda: take_aux(pr[:, :, :], aux[:, :, 0:LOG_COLS], "idx_dots", ACT.Relu),),
                    5: (lambda: take_qk("A_qk"),)},
                6: {0: (log_f,)},
                7: {2: (lambda: take_qk("B_qk"),), 3: (lambda: exps_of(pr, 0, 1, first),),
                    5: (lambda: exps_of(pr, 0, 1, second),)},
                8: {1: (lambda: take_pT("A_pT"),), 3: (lambda: hi_from_aux(y_hi[:, 0, :, :], aux4, "A_y"),),
                    6: (lambda: exps_of(pr, 0, 2, first),), 7: (lambda: exps_of(pr, 0, 2, second),)},
                9: {0: (lambda: take_mod(1),), 1: (lambda: exps_of(pr2, 1, 3, first),),
                    2: (lambda: exps_of(pr2, 1, 3, second),), 7: (lambda: take_pT("B_pT"),)},
                10: {2: (lambda: take_qk("C_T"),),
                     4: (lambda: take_aux(ob[:, :, :, :].rearrange("p t h d -> p (t h d)"), auxw[:, 0:NT * NB],
                                          "B_o"),)},
                11: {0: (norm_root,), 2: (conv_hi,)},
                12: {1: (lambda: take_qk("D_qk"),), 7: (lambda: exps_of(pr, 0, 4, first),)},
            }
            for u in range(5, WIN_UNITS):
                ahead(G + u * UC, before=mixer_steps.get(u, {}))
                act.wait_ge(used, G + (u + 1) * UC)
                act.wait_ge(evacuated, V_WIN + u)
                act.activation(proj[:, (0, QA, KA, VA, QB, KB, VB, BG, CG, XIN, QD, KD, VD)[u]], ps[:, u % 2],
                               ACT.Copy).then_inc(evacuated, 1)
            def gate_stage(m):
                g0 = G_GATE + m * DB * (UC + BC)
                with act.Fori(0, DB // 2) as i:
                    for b in range(2):
                        g, s = g0 + (2 * i + b) * (UC + BC), b * (UC + BC)
                        ahead(g, s)
                        act.wait_ge(evacuated, V_GATE + 2 * (m * DB + 2 * i + b) + 1)
                        act.activation(zt[:, 0], zt[:, 0], ACT.Sigmoid).then_inc(gate_ready, 1)
                        ahead(g + UC, s + UC, BC)

            take_mod(2)
            exps_of(pr, 0, 4, second)
            gate_stage(0)
            take_mod(3)
            take_pT("D_pT")
            gate_stage(1)
            take_mod(4)
            hi_from_aux(y_hi[:, 1, :, :], aux4, "B_y")
            gate_stage(2)
            take_mod(5)
            hi_from_aux(y_hi[:, 3, :, :], aux4, "D_y")
            gate_stage(3)
            take_mod(6)
            for n in range(2):
                block_hi("m", n)

            def squares(n, added):
                act.wait_ge(x_added, added)
                for t in range(NT):
                    sq = act.activation(h2[:, t, n * NB:(n + 1) * NB], x3[:, t, n * NB:(n + 1) * NB], ACT.Square,
                                        accum_out=ss4[:, t, n:n + 1])
                sq.then_inc(squared, 1)

            def squares_last(n, added):
                act.activation(spare[:, :], rstd[:, 0:1], ACT.Sqrt)
                squares(n, added)

            def late_hi(rnd):
                return {2: (lambda: block_hi(rnd, 2),), 4: (lambda: block_hi(rnd, 3),)}

            for n in range(DB):
                ahead(G_WO + n * UC, before={} if n else late_hi("m"))
                (squares if n < DB - 1 else squares_last)(n, n + 1)
            norm_root_of(2)
            take_mod(7)
            for n in range(2):
                block_hi("n", n)

            def square(q, j):
                act.wait_ge(evacuated, V_FF + 2 * DB * q + j + 1)
                act.activation(zt[:, j % 2], zt[:, j % 2], ACT.Square).then_inc(a_ready, 1)

            def hidden_hi(q, j):
                act.wait_ge(aux_full, len(ROUNDS) + 4 * q + j + 1)
                act.activation(a_hi[:, 4 * j:4 * j + 4, :], aux4, ACT.Copy).then_inc(aux_hi, 1)

            def ff_group(q, start=False, last=False):
                g = G_FF + 2 * DB * UC * q
                for j in range(DB):
                    ahead(g + j * UC, before={3: (lambda: hidden_hi(q, j - 1),)} if j else
                          late_hi("n") if start else {})
                    square(q, j)
                g = g + DB * UC
                for j in range(DB):
                    ahead(g + j * UC, before={} if j else {3: (lambda: hidden_hi(q, DB - 1),)},
                          last=last and j == DB - 1)
                    if last:
                        (squares if j < DB - 1 else squares_last)(j, DB * FF_GROUPS + j + 1)

            ff_group(0, start=True)
            with act.Fori(1, FF_GROUPS - 1) as q:
                ff_group(q)
            ff_group(FF_GROUPS - 1, last=True)
            norm_root_of(3)

        @block.vector
        def _(dve):
            link = Links(dve, dve_step)

            def split(g, slot):
                dve.wait_ge(hi_ready, g + 1)
                dve.tensor_tensor(w_lo[:, slot, :], raw[:, slot, :], w_hi[:, slot, :].bitcast(F32), ALU.subtract)\
                    .then_inc(lo_ready, 1)

            def ahead(g, slot0=0, n=UC, before={}, after={}, last=False):
                for c in range(n):
                    for step in before.get(c, ()):
                        step()
                    if not (last and c >= n - RING):
                        split(g + RING + c, (slot0 + c) % RING)
                    for step in after.get(c, ()):
                        step()

            def mod_step(j, kt, k, late=False):
                ring, sems = (mod_raw2, mod_in2) if late else (mod_raw, mod_in)
                nth = j - k - (5 * KT if late else 0)
                dve.wait_ge(sems[k], nth * (16 // len(ring)) + 16)
                dve.wait_ge(mod_used, j + 1)
                dve.scalar_tensor_tensor(acc, ring[k][:, :], csil[:, bass.ds(kt, 1)], acc, ALU.mult, ALU.add)\
                    .then_inc(mod_used, 1)

            def mod_steps(j, kt, late=False):
                return {2 * k: (lambda k=k: mod_step(j + k, kt + k, k % (2 if late else 4), late),)
                        for k in range(4)}

            def next_block(d):
                dve.wait_ge(acc_ready, d)

            def lo_from_aux(dst, src, hi, name):
                dve.wait_ge(aux_hi, HI_ROUNDS.index(name) + 1)
                dve.tensor_tensor(dst, src, hi.bitcast(F32), ALU.subtract).then_inc(aux_free, 1)

            aux8 = aux[:, :, :].rearrange("p b (k s) -> p (b k) s", s=SEQ)
            aux4 = aux[:, 0:2, :].rearrange("p b (h s) -> p (b h) s", s=SEQ)

            def block_lo(rnd, n):
                lo_from_aux(act_lo[:, 4 * n:4 * n + 4, :], aux8[:, 4 * (n % 2):4 * (n % 2) + 4, :],
                            act_hi[:, 4 * n:4 * n + 4, :], f"{rnd}{n}")

            def wide(ap, n):
                return ap.unsqueeze(1).to_broadcast([P, n, ap.shape[1]])

            dve.wait_ge(c_ready, 1)
            link(dve.tensor_tensor(csil[:, :], cc[:, 0, :], cc[:, 1, :], ALU.mult))
            link(dve.tensor_copy(csil_hi[:, :], csil[:, :]))
            dve.tensor_tensor(csil_lo[:, :], csil[:, :], csil_hi[:, :].bitcast(F32), ALU.subtract).then_inc(cb_ready, 1)
            for s in range(RING):
                split(s, s)

            def lambda_sums():
                dve.wait_ge(small_in, 16 * SMALL_LOADS)
                link(dve.tensor_tensor(lprod[:, :, :], lamb[:, 0:4:2, :], lamb[:, 1:4:2, :], ALU.mult))
                dve.tensor_reduce(lsum[:, 0:2], lprod[:, :, :], AX_X, ALU.add).then_inc(lam_sum, 1)

            def distance_bias(part):
                runs = t5_runs()
                for b, n0, n1 in runs[part::4]:
                    link.step(dve.tensor_copy(dist[:, SEQ - n1:SEQ - n0], tabT[:, b:b + 1].to_broadcast([8, n1 - n0])))

            def distance_end():
                link(dve.tensor_copy(dist[:, SEQ:LOG_COLS], tabT[:, 0:1].to_broadcast([8, LOG_COLS - SEQ])))
                dve.tensor_scalar(gsub[:, :], gsub[:, :], 1.0 - LAM_INIT, None, ALU.mult).then_inc(dist_ready, 1)

            def lambda_end():
                dve.wait_ge(lam_exp, 1)
                link(dve.tensor_tensor(nlam[:, :], lsum[:, 3:4], lsum[:, 2:3], ALU.subtract))
                link(dve.tensor_scalar(nlam[:, :], nlam[:, :], -LAM_INIT, None, ALU.add))

            def mean_squares():
                dve.tensor_scalar(ss[:, :], ss[:, :], 1.0 / D, EPS, ALU.mult, ALU.add).then_inc(var_ready, 1)

            def inverse_root(n):
                dve.wait_ge(root, n)
                link(dve.reciprocal(rstd[:, :], rstd[:, :]))

            def first_means():
                dve.wait_ge(sumsq, NT)
                mean_squares()

            def evac_begin(v_end):
                dve.wait_ge(used, v_end)

            def norm_mult(dst, src, n, scale):
                col = slice(n * NB, (n + 1) * NB)
                for t in range(NT):
                    link.step(dve.scalar_tensor_tensor(dst[:, t, col], src[:, t, col], rstd[:, t:t + 1],
                                                       scale[:, col], ALU.mult, ALU.mult))

            def norm_shift(dst, n, shift):
                col = slice(n * NB, (n + 1) * NB)
                link.wait()
                dve.tensor_tensor(dst[:, :, col], dst[:, :, col], wide(shift[:, col], NT), ALU.add)\
                    .then_inc(h_ready, 1)

            def ada_evac(u, dst, i):
                b = u % 2 if isinstance(u, int) else None
                dve.wait_ge(brow_in[b], 16 * i + 16)
                dve.tensor_tensor(dst, ps[:, b, 0, :], brow[:, b, :], ALU.add).then_inc(evacuated, 1)

            norm_steps = {
                1: {0: (lambda_sums,), **{2 + k: (lambda k=k: distance_bias(k),) for k in range(4)}, 6: (distance_end,)},
                2: {2: (lambda_end,)},
                3: {1: (first_means,), 5: (lambda: inverse_root(1),)},
            }
            for u in range(DB):
                ahead(u * UC, before=norm_steps.get(u, {}))
                evac_begin((u + 1) * UC)
                ada_evac(u, sh1[:, u * NB:(u + 1) * NB], u // 2)

            def scale_block(n):
                dve.wait_ge(evacuated, DB + n + 1)
                col = slice(n * NB, (n + 1) * NB)
                link(dve.scalar_tensor_tensor(gs1[:, col], zt[:, 0, 0, :], 1.0, gs1[:, col], ALU.add, ALU.mult))

            def h_block(n):
                low = ((lambda: block_lo("h", n - 1)),) if n else ()
                return {0: (lambda: scale_block(n),), 1: (lambda: norm_mult(x1, x1, n, gs1),),
                        2: (lambda: norm_shift(x1, n, sh1),), 3: low}

            dve.wait_ge(g_in, 32)
            for n in range(DB):
                u = DB + n
                ahead(u * UC, before=h_block(n - 1) if n else {})
                evac_begin((u + 1) * UC)
                ada_evac(u, zt[:, 0, 0, :], u // 2)

            def softmax_max(buf, c):
                link.step(dve.tensor_reduce(nmax[:, c, 0, :], buf[:, :, 0:P], AX_X, ALU.max, negate=True))
                dve.tensor_reduce(nmax[:, c, 1, :], buf[:, :, P:LOG_COLS], AX_X, ALU.max, negate=True)\
                    .then_inc(neg_max, 1)

            def weigh(buf, r, last=None):
                for t, (c0, c1) in enumerate(((0, P), (P, LOG_COLS))):
                    f = r[:, t, :].unsqueeze(2).to_broadcast([P, NH, c1 - c0])
                    ins = dve.tensor_tensor(buf[:, :, c0:c1], buf[:, :, c0:c1], f, ALU.mult)
                    if t == 0 or last is None:
                        link.step(ins)
                if last is not None:
                    ins.then_inc(last, 1)

            def logits(buf, scale, head0, name):
                dve.wait_ge(aux_full, RND[name] + 1)
                link.step(dve.scalar_tensor_tensor(buf[:, :, 0:P], aux[:, :, 0:P], scale,
                                                   Bm[:, head0:head0 + NH, P:SEQ], ALU.mult, ALU.add))
                dve.scalar_tensor_tensor(buf[:, :, P:LOG_COLS], aux[:, :, P:LOG_COLS], scale,
                                         Bm[:, head0:head0 + NH, :], ALU.mult, ALU.add).then_inc(aux_free, 1)
                link.wait()
                dve.wait_ge(aux_free, RND[name] + 1)

            ahead(G_WIN, before={**h_block(DB - 1), 4: (lambda: block_lo("h", 3),)})
            evac_begin(G_WIN + UC)
            dve.tensor_scalar(proj[:, MISC], ps[:, 0], 1.0, None, ALU.mult).then_inc(evacuated, 1)
            with dve.Fori(0, 2) as i:
                for b in range(2):
                    g = G_WIN + UC + (2 * i + b) * UC
                    ahead(g, after=mod_steps(8 * i + 4 * b, 8 * i + 4 * b))
                    evac_begin(g + UC)
                    dve.tensor_scalar(proj[:, 1 + 2 * i + b], ps[:, 1 - b], 1.0, None, ALU.mult)\
                        .then_inc(evacuated, 1)
            spans = ((0, P), (P, LOG_COLS))

            def small_inputs():
                dve.wait_ge(evacuated, V_WIN + 1)
                link(dve.tensor_scalar(iws[:, :, :], proj[:, MISC, :, IW0:IW0 + NH], IDX_SCALE, None, ALU.mult))
                link(dve.tensor_tensor(lsig[:, :, :], proj[:, MISC, :, FD0:FD0 + NH], wide(bf[:, :], NT), ALU.add))
                link(dve.tensor_scalar(lsig2[:, :, :], lsig[:, :, :], -1.0, None, ALU.mult))
                dve.tensor_tensor(lsig2[:, :, :], lsig2[:, :, :], lsig[:, :, :], ALU.max).then_inc(f_abs, 1)

            def index_scores():
                dve.wait_ge(aux_free, RND["idx_dots"] + 1)
                for t, (c0, c1) in enumerate(spans):
                    link.step(dve.tensor_scalar(score[:, c0:c1], pr[:, 0, c0:c1], iws[:, t, 0:1], 0.0,
                                                ALU.mult, ALU.add))
                link.wait()
                for h in range(1, NH):
                    for t, (c0, c1) in enumerate(spans):
                        ins = dve.scalar_tensor_tensor(score[:, c0:c1], pr[:, h, c0:c1], iws[:, t, h:h + 1],
                                                       score[:, c0:c1], ALU.mult, ALU.add)
                        if h < NH - 1 or t == 0:
                            link.step(ins)
                        else:
                            ins.then_inc(score_ready, 1)
                    link.wait()

            def top8(r):
                if r == 0:
                    dve.wait_ge(score_masked, 1)
                src = score if r == 0 else work
                for t, (c0, c1) in enumerate(spans):
                    link.step(dve.max(m8[:, t, :], src[:, c0:c1]))
                link.wait()
                for t, (c0, c1) in enumerate(spans):
                    link.step(dve.match_replace(work[:, c0:c1], m8[:, t, :], src[:, c0:c1], TAKEN))
                link.wait()

            def select():
                link(dve.tensor_scalar(selm[:, :], work[:, :], TAKEN / 2, NEG, ALU.is_gt, ALU.mult))

            def sparse_logits():
                dve.wait_ge(bm_ready, 1)
                logits(pr, HD ** -0.5, 0, "A_dots")
                for t, (c0, c1) in enumerate(spans):
                    link.step(dve.tensor_tensor(pr[:, :, c0:c1], pr[:, :, c0:c1],
                                                selm[:, c0:c1].unsqueeze(1).to_broadcast([P, NH, c1 - c0]), ALU.add))
                link.wait()
                softmax_max(pr, 0)

            def softmax_end(n):
                dve.wait_ge(exps, n * NT * NH)
                link(dve.reciprocal(rec[:, 0, :, :], esum[:, 0, :, :]))
                weigh(pr, rec[:, 0], p_ready)

            def log_forget():
                dve.wait_ge(f_log, 1)
                link(dve.tensor_scalar(lsig[:, :, :], lsig[:, :, :], 0.0, None, ALU.min))
                dve.tensor_tensor(lsig[:, :, :], lsig[:, :, :], lsig2[:, :, :], ALU.subtract).then_inc(ls_ready, 1)

            def diff_logits(c, buf):
                logits(buf, DD ** -0.5, NH, f"B_dots{c}")
                softmax_max(buf, c)

            def diff_weights0():
                dve.wait_ge(exps, 2 * NT * NH)
                link(dve.reciprocal(rec[:, 0, :, :], esum[:, 0, :, :]))
                weigh(pr, rec[:, 0])

            def diff_weights1():
                dve.wait_ge(exps, 3 * NT * NH)
                link(dve.reciprocal(rec[:, 1, :, :], esum[:, 1, :, :]))
                link(dve.tensor_scalar(rec[:, 1, :, :], rec[:, 1, :, :], nlam[:, 0:1], None, ALU.mult))
                weigh(pr2, rec[:, 1])
                link.wait()
                dve.tensor_tensor(pr[:, :, :], pr[:, :, :], pr2[:, :, :], ALU.add).then_inc(p_ready, 1)

            def diff_norm():
                dve.wait_ge(aux_free, RND["B_o"] + 1)
                sq = zt[:, 0].rearrange("p t (h d) -> p t h d", h=NH)
                link(dve.tensor_tensor(sq, ob[:, :, :, :], ob[:, :, :, :], ALU.mult))
                link(dve.tensor_reduce(rec[:, 0, :, :], sq, AX_X, ALU.add))
                dve.tensor_scalar(rec[:, 0, :, :], rec[:, 0, :, :], 1.0 / HD, EPS, ALU.mult, ALU.add)\
                    .then_inc(yb_var, 1)

            def diff_scale():
                dve.wait_ge(yb_root, 1)
                link(dve.reciprocal(rec[:, 1, :, :], rec[:, 1, :, :]))
                obv = ob[:, :, :, :].rearrange("p t h d -> p (t h) d")
                rv = rec[:, 1, :, :].rearrange("p t h -> p (t h)")
                link(dve.tensor_tensor(obv, obv, rv.unsqueeze(2).to_broadcast([P, NT * NH, HD]), ALU.mult))
                dve.tensor_tensor(obv, obv, wide(gsub[:, :], NT * NH), ALU.mult).then_inc(yb_ready, 1)

            def conv_input():
                dve.wait_ge(evacuated, V_WIN + 10)
                dve.tensor_tensor(proj[:, CG], proj[:, CG], proj[:, XIN], ALU.mult).then_inc(u_ready, 1)

            def conv_tap(d):
                if d == 0:
                    dve.wait_ge(aux_free, RND["C_T"] + 1)
                for k in range(NH):
                    if d == 0:
                        ins = dve.tensor_scalar(pr[:, k, 0:SEQ], qkT[:, 0, k, :], convw[:, k, 2:3], None, ALU.mult)
                    else:
                        ins = dve.scalar_tensor_tensor(pr[:, k, d:SEQ], qkT[:, 0, k, 0:SEQ - d],
                                                       convw[:, k, 2 - d:3 - d], pr[:, k, d:SEQ], ALU.mult, ALU.add)
                    link.step(ins)
                link.wait()

            def conv_end():
                dve.tensor_tensor(pr[:, :, 0:SEQ], pr[:, :, 0:SEQ], qkT[:, 1, :, :], ALU.mult).then_inc(yc_raw, 1)

            def conv_lo():
                dve.wait_ge(yc_hi, 1)
                dve.tensor_tensor(y_lo[:, 2, :, :], pr[:, :, 0:SEQ], y_hi[:, 2, :, :].bitcast(F32), ALU.subtract)\
                    .then_inc(yc_ready, 1)

            def forget_terms():
                dve.wait_ge(aux_full, RND["D_sums"] + 1)
                link(dve.tensor_scalar(Ftok[:, :, :].rearrange("p t h -> p (t h)"), aux[:, 2, 0:2 * NH], 1.0, None,
                                       ALU.mult))
                for h in range(NH):
                    for t, (c0, c1) in enumerate(spans):
                        ins = dve.tensor_scalar(pr[:, h, c0:c1], aux4[:, h, 0:c1 - c0], -1.0, Ftok[:, t, h:h + 1],
                                                ALU.mult, ALU.add)
                        if (h, t) == (NH - 1, 1):
                            ins.then_inc(aux_free, 1)
                        else:
                            link.step(ins)

            def forget_logits():
                link.wait()
                dve.wait_ge(aux_free, RND["D_sums"] + 1)
                dve.wait_ge(dm_ready, 1)
                dve.wait_ge(aux_full, RND["D_dots"] + 1)
                link.step(dve.scalar_tensor_tensor(pr[:, :, 0:P], aux[:, :, 0:P], HD ** -0.5, pr[:, :, 0:P],
                                                   ALU.mult, ALU.add))
                dve.scalar_tensor_tensor(pr[:, :, P:LOG_COLS], aux[:, :, P:LOG_COLS], HD ** -0.5,
                                         pr[:, :, P:LOG_COLS], ALU.mult, ALU.add).then_inc(aux_free, 1)
                link.wait()
                dve.wait_ge(aux_free, RND["D_dots"] + 1)
                softmax_max(pr, 0)

            mixer_steps = {
                5: {0: (lambda: next_block(1),), 1: (small_inputs,), 4: (index_scores,), 6: (lambda: top8(0),),
                    7: (lambda: top8(1),)},
                6: {**{c: (lambda c=c: top8(c + 2),) for c in range(6)}, 6: (select,)},
                7: {0: (sparse_logits,), 7: (lambda: softmax_end(1),)},
                8: {1: (log_forget,), 3: (lambda: lo_from_aux(y_lo[:, 0, :, :], aux4, y_hi[:, 0, :, :], "A_y"),),
                    5: (lambda: diff_logits(0, pr),), 7: (lambda: diff_logits(1, pr2),)},
                9: {0: (lambda: next_block(2),), 2: (diff_weights0,), 4: (diff_weights1,)},
                10: {0: (conv_input,), 2: (lambda: conv_tap(0),), 3: (lambda: conv_tap(1),),
                     4: (lambda: conv_tap(2), conv_end), 6: (diff_norm,)},
                11: {1: (diff_scale,), 3: (conv_lo,), 5: (forget_terms,)},
                12: {4: (forget_logits,)},
            }
            for u in range(5, WIN_UNITS):
                ahead(G_WIN + u * UC, before=mixer_steps[u], after=mod_steps(4 * (u - 1), 4 * (u - 1) % KT))
            next_block(3)
            softmax_end(4)
            dve.wait_ge(evacuated, V_GATE)

            def gate_stage(m):
                g0 = G_GATE + m * DB * (UC + BC)
                with dve.Fori(0, DB // 2) as i:
                    for b in range(2):
                        n = 2 * i + b
                        g, s = g0 + n * (UC + BC), b * (UC + BC)
                        ahead(g, s, after=mod_steps(3 * KT + 4 * (m * DB + n), 8 * i + 4 * b, m > 1))
                        evac_begin(g + UC)
                        dve.wait_ge(brow_in[b], (ADA_UNITS + m * DB) * 8 + 16 * i + 16)
                        dve.tensor_tensor(zt[:, 0], ps[:, 1], wide(brow[:, b, :], NT), ALU.add).then_inc(evacuated, 1)
                        ahead(g + UC, s + UC, BC)
                        evac_begin(g + UC + BC)
                        dve.wait_ge(gate_ready, m * DB + n + 1)
                        col = bass.ts(n, NB)
                        if m == 0:
                            dve.tensor_tensor(merged[:, :, col], ps[:, 0], zt[:, 0], ALU.mult).then_inc(evacuated, 1)
                        else:
                            dve.tensor_tensor(zt[:, 0], ps[:, 0], zt[:, 0], ALU.mult).then_inc(evacuated, 1)
                            dve.wait_ge(evacuated, V_GATE + 2 * (m * DB + n) + 2)
                            if m > 1:
                                dve.wait_ge(merged_ready, (m - 2) * DB + n + 1)
                            dve.tensor_tensor(merged[:, :, col], merged[:, :, col], zt[:, 0], ALU.add)\
                                .then_inc(merged_ready, 1)

            gate_stage(0)
            next_block(4)
            gate_stage(1)
            next_block(5)
            lo_from_aux(y_lo[:, 1, :, :], aux4, y_hi[:, 1, :, :], "B_y")
            gate_stage(2)
            next_block(6)
            lo_from_aux(y_lo[:, 3, :, :], aux4, y_hi[:, 3, :, :], "D_y")
            gate_stage(3)
            next_block(7)
            for n in range(2):
                block_lo("m", n)

            def add_to_x(v, col, pair, b, gate, added=None):
                dve.tensor_tensor(zt[:, b], ps[:, pair], wide(gate[:, col], NT), ALU.mult)\
                    .then_inc(evacuated, 1)
                dve.wait_ge(evacuated, v + 1)
                if added is not None:
                    dve.wait_ge(x_added, added)
                dve.tensor_tensor(x3[:, :, col], x3[:, :, col], zt[:, b], ALU.add).then_inc(x_added, 1)

            def scale_rows():
                dve.wait_ge(scale_in, 32)
                dve.scalar_tensor_tensor(gs2[:, :], gs2[:, :], 1.0, gnb[:, :], ALU.add, ALU.mult).then_inc(gs2_ready, 1)

            def late_lo(rnd):
                return {2: (lambda: block_lo(rnd, 2),), 4: (lambda: block_lo(rnd, 3),)}

            for n in range(DB):
                g = G_WO + n * UC

                def residual(n=n):
                    evac_begin(G_WO + (n + 1) * UC)
                    dve.wait_ge(*((x_added, n) if n else (x_in_again, 32)))
                    add_to_x(V_WO + n, slice(n * NB, (n + 1) * NB), (n + 1) % 2, 0, gt1b)

                ahead(g, before={**{0: late_lo("m"), 2: {4: (scale_rows,)}}.get(n, {}), 7: (residual,)},
                      after=mod_steps(7 * KT + 4 * n, 4 * n, True))

            def row_sums(n):
                dve.wait_ge(squared, DB * n)
                link(dve.tensor_reduce(ss[:, :], ss4[:, :, :], AX_X, ALU.add))

            row_sums(1)
            mean_squares()
            inverse_root(2)
            dve.wait_ge(gs2_ready, 1)
            dve.wait_ge(shift_in, 16)
            for n in range(DB):
                norm_mult(h2, x3, n, gs2)
                norm_shift(h2, n, sh2b)
                if n in (1, 2):
                    block_lo("n", n - 1)

            def hidden_lo(q, j):
                dve.wait_ge(aux_hi, len(HI_ROUNDS) + 4 * q + j + 1)
                dve.tensor_tensor(a_lo[:, 4 * j:4 * j + 4, :], aux4, a_hi[:, 4 * j:4 * j + 4, :].bitcast(F32),
                                  ALU.subtract).then_inc(aux_free, 1)

            def ff_group(q, start=False, last=False):
                v, g = V_FF + 2 * DB * q, G_FF + 2 * DB * UC * q
                for j in range(DB):
                    ahead(g + j * UC, before={3: (lambda: hidden_lo(q, j - 1),)} if j else
                          late_lo("n") if start else {})
                    evac_begin(g + (j + 1) * UC)
                    dve.tensor_scalar(zt[:, j % 2], ps[:, (1 + j) % 2], 0.0, None, ALU.max).then_inc(evacuated, 1)
                v, g = v + DB, g + DB * UC
                for j in range(DB):
                    ahead(g + j * UC, before={} if j else {3: (lambda: hidden_lo(q, DB - 1),)},
                          last=last and j == DB - 1)
                    evac_begin(g + (j + 1) * UC)
                    if start and j == 0:
                        dve.wait_ge(gate_in, 16)
                    add_to_x(v + j, slice(j * NB, (j + 1) * NB), (1 + j) % 2, j % 2, gt2b,
                             DB * (1 + q) + j)

            ff_group(0, start=True)
            with dve.Fori(1, FF_GROUPS - 1) as q:
                ff_group(q)
            ff_group(FF_GROUPS - 1, last=True)
            row_sums(2)
            mean_squares()
            inverse_root(3)
            dve.wait_ge(gfin_in, 16)
            for t, col in OUT_PARTS:
                dve.scalar_tensor_tensor(x3[:, t, col], x3[:, t, col], rstd[:, t:t + 1], gnb[:, col], ALU.mult, ALU.mult)\
                    .then_inc(fin_ready, 1)

        @block.gpsimd
        def _(pool):
            link = Links(pool, pool_step)
            for dst, src in ((mod_lines[0:2 * MOD_BLOCKS, :], mod_bias), (convw[:, :, :], conv_cols), (tabT[:, :], tab),
                             (bf[:, :], bcast_rows(b_f[0:1, :])), (gsub[:, :], bcast_rows(g_subln[0:1, :])),
                             (lamb[:, :, :].rearrange("p a d -> p (a d)"), bcast_rows(lam[0:1, :]))):
                pool.dma_start(dst, src).then_inc(small_in, 16)
            link(pool.memset(ident[:, :], 0.0))
            pool.affine_select(out=ident[:, :], in_=ident[:, :], compare_op=ALU.not_equal, fill=1.0, base=0,
                               pattern=[[-1, P]], channel_multiplier=1).then_inc(consts, 1)
            link(pool.memset(mirror[:, :], 0.0))
            pool.affine_select(out=mirror[:, :], in_=mirror[:, :], compare_op=ALU.not_equal, fill=1.0, base=1 - P,
                               pattern=[[1, P]], channel_multiplier=1).then_inc(consts, 1)
            link(pool.memset(triones[:, :], 1.0))
            pool.affine_select(out=triones[:, :], in_=triones[:, :], compare_op=ALU.is_ge, fill=0.0, base=0,
                               pattern=[[1, SEQ]], channel_multiplier=-1).then_inc(consts, 1)

            def bias_of(r):
                return bcast_rows(bias_rows[bass.ds(r, 1), :])

            for b in range(2):
                pool.dma_start(brow[:, b, :], bcast_rows(bias_rows[b:b + 1, :])).then_inc(brow_in[b], 16)
            pool.wait_ge(dist_ready, 1)
            pool.dma_start(dist_d.ap(), dist[:, :]).then_inc(dist_out, 16)

            def ada_rows(i):
                for b in range(2):
                    pool.wait_ge(evacuated, 2 * i + b - 1)
                    pool.dma_start(brow[:, b, :], bias_of(2 * i + b)).then_inc(brow_in[b], 16)

            ada_rows(1)
            pool.wait_ge(dist_out, 16)
            pool.dma_start(steps[:, :, :], bass.AP(tensor=dist_d, offset=0,
                                                   ap=[[1, P], [LOG_COLS, 2 * NH], [1, SEQ]])).then_inc(steps_in, 16)
            with pool.Fori(2, 4) as i:
                ada_rows(i)
            pool.wait_ge(bias_turned, 1)
            pool.affine_select(out=Bm[:, :, :], in_=Bm[:, :, :], compare_op=ALU.is_ge, fill=NEG, base=P,
                               pattern=[[0, 2 * NH], [-1, SEQ]], channel_multiplier=1).then_inc(bm_ready, 1)

            def begin_block(d):
                if d:
                    pool.wait_ge(aux_full, RND[f"mod{d - 1}"] + 1)
                link(pool.memset(acc, 0.0))
                n = 2 * MOD_BLOCKS
                for k in range(2):
                    ins = pool.tensor_tensor(acc[0:n, k * NB:(k + 1) * NB], mod_lines[0:n, :],
                                             ident[0:n, 2 * d + k:2 * d + k + 1].to_broadcast([n, NB]), ALU.mult)
                    if k == 0:
                        link.step(ins)
                    else:
                        ins.then_inc(acc_ready if d else mod_used, 1)
                link.wait()

            pool.wait_ge(small_in, 16 * SMALL_LOADS)
            pool.wait_ge(consts, 1)
            begin_block(0)

            def causal(t0, t1, pat, sem_out):
                link.step(pool.affine_select(out=t0, in_=t0, compare_op=ALU.is_ge, fill=NEG,
                                             base=0, pattern=pat + [[-1, P]], channel_multiplier=1))
                link.wait()
                pool.affine_select(out=t1, in_=t1, compare_op=ALU.is_ge, fill=NEG, base=P, pattern=pat + [[-1, SEQ]], channel_multiplier=1)\
                    .then_inc(sem_out, 1)

            begin_block(1)
            pool.wait_ge(score_ready, 1)
            causal(score[:, 0:P], score[:, P:LOG_COLS], [], score_masked)

            def gate_row(m, n, b):
                pool.wait_ge(evacuated, V_GATE + 2 * (m * DB + n) - 3)
                pool.dma_start(brow[:, b, :], bias_of(ADA_UNITS + m * DB + n)).then_inc(brow_in[b], 16)

            def gate_rows(m, i):
                for b in range(2):
                    gate_row(m, 2 * i + b, b)

            def mod_of(r):
                return bcast_rows(mods_d.ap()[2 * r:2 * r + 2].rearrange("d h n -> (d h n)").unsqueeze(0))

            begin_block(2)
            pool.wait_ge(row_out, 32)
            pool.dma_start(gt1b[:, :], mod_of(0)).then_inc(x_in_again, 16)
            gate_rows(0, 0)
            pool.wait_ge(aux_free, RND["D_sums"] + 1)
            causal(pr[:, :, 0:P], pr[:, :, P:LOG_COLS], [[0, NH]], dm_ready)
            begin_block(3)
            gate_rows(0, 1)
            for m in (1, 2):
                gate_rows(m, 0)
                begin_block(3 + m)
                gate_rows(m, 1)
            gate_rows(3, 0)
            begin_block(6)
            pool.wait_ge(aux_free, RND["D_y"] + 1)
            pool.dma_start(x3[:, :, :], x_v).then_inc(x_in_again, 16)
            pool.wait_ge(row_out, 16 * 6)
            pool.dma_start(sh2b[:, :], mod_of(1)).then_inc(shift_in, 16)
            gate_rows(3, 1)
            begin_block(7)
            pool.dma_start(gs2[:, :], mod_of(2)).then_inc(scale_in, 16)
            pool.dma_start(gnb[:, :], bcast_rows(g_norm2[0:1, :])).then_inc(scale_in, 16)
            pool.wait_ge(x_added, DB)
            pool.wait_ge(row_out, 16 * MOD_BLOCKS)
            pool.dma_start(gt2b[:, :], mod_of(3)).then_inc(gate_in, 16)
            pool.wait_ge(gs2_ready, 1)
            pool.dma_start(gnb[:, :], bcast_rows(g_final[0:1, :])).then_inc(gfin_in, 16)
            pool.wait_ge(gfin_in, 16)


def tiles(w):
    import numpy as np
    k, n = w.shape
    return np.ascontiguousarray(w.reshape(k // (CK * P), CK, P, n // NB, NB).transpose(3, 0, 2, 1, 4))\
        .reshape(-1, P, CK * NB)


def kernel(**inputs):
    import numpy as np
    import concourse.bacc as bacc
    from concourse.bass_utils import run_bass_kernel_spmd

    i = {k: np.asarray(v) for k, v in inputs.items()}
    w_in = i["w_in"][0]
    cuts = np.cumsum([0, 512, 512, 512, 256, 64, 4, 512, 512, 512, 512, 512, 512, 512, 512, 512, 4])
    qa, ka, va, iq, ik, iw, qb, kb, vb, bg, cg, xin, qd, kd, vd, fd = (
        w_in[:, a:b] for a, b in zip(cuts[:-1], cuts[1:]))
    pad = np.zeros((D, NB - IK0 - IDX_DIM - 2 * NH), w_in.dtype)
    w_ada, b_ada = i["w_ada"][0], i["b_ada"][0]
    stream = [tiles(w_ada[:, :2 * D])]
    stream += [tiles(np.concatenate([iq, ik, iw, fd, pad], axis=1))]
    stream += [tiles(w) for w in (qa, ka, va, qb, kb, vb, bg, cg, xin, qd, kd, vd)]
    for m in MIXERS:
        gate = tiles(i["w_gate"][0][:, m * D:(m + 1) * D]).reshape(DB, UC, P, CK * NB)
        branch = tiles(i["w_branch"][0, m]).reshape(DB, BC, P, CK * NB)
        stream += [np.concatenate([gate, branch], axis=1).reshape(-1, P, CK * NB)]
    stream += [tiles(i["w_o"][0])]
    for q in range(FF_GROUPS):
        stream += [tiles(i["w_ff1"][0][:, q * D:(q + 1) * D]), tiles(i["w_ff2"][0][q * D:(q + 1) * D, :])]
    stream = np.concatenate(stream, axis=0)
    b_gate = i["b_gate"][0].reshape(4, DB, NB)
    arrays = {
        "stream": stream,
        "mod_stream": np.ascontiguousarray(w_ada[:, 2 * D:].reshape(KT, P, MOD_BLOCKS, MOD_W).transpose(2, 0, 1, 3))
        .reshape(MOD_STEPS, P, MOD_W),
        "bias_rows": np.concatenate([b_ada[:2 * D].reshape(-1, NB)] + [b_gate[m] for m in MIXERS], axis=0),
        "x": i["x"][0],
        "c_cols": np.ascontiguousarray(i["c"][0].reshape(KT, P).T),
        "conv_cols": np.ascontiguousarray(i["conv_w"][0].reshape(3, NH, P).transpose(2, 1, 0)),
        "lam": i["lam"].reshape(1, 4 * DD),
        "g_subln": i["g_subln"].reshape(1, HD),
        "tab": np.ascontiguousarray(i["rel_bias"].T),
        "b_f": i["b_f"].reshape(1, NH),
        "mod_bias": b_ada[2 * D:].reshape(2 * MOD_BLOCKS, NB),
        "g_norm1": i["g_norm1"].reshape(1, D),
        "g_norm2": i["g_norm2"].reshape(1, D),
        "g_final": i["g_final"].reshape(1, D),
    }
    nc = bacc.Bacc("TRN2", target_bir_lowering=False, num_devices=1)
    args = [nc.dram_tensor(f"in_{k}", a.shape, mybir.dt.from_np(a.dtype), kind="ExternalInput").ap()
            for k, a in arrays.items()]
    args.append(nc.dram_tensor("out_x", (SEQ, D), F32, kind="ExternalOutput").ap())
    build(nc, *args)
    r = run_bass_kernel_spmd(nc, [{f"in_{k}": a for k, a in arrays.items()}], core_ids=[0])
    return r.results[0]["out_x"].reshape(1, SEQ, D)
```
